# Optimizing a Trainium2 kernel written in Bass

```python
import math
import jax, jax.numpy as jnp
from jax import lax
import numpy as np

D_MODEL = 1024
BATCH = 1
SEQ = 2048
DEPTH = 1

CHUNK = 64
MIX_WIDTH = D_MODEL
CONV_WIDTH = MIX_WIDTH // 2
SSM_WIDTH = MIX_WIDTH - CONV_WIDTH
CONV_HEADS = 8
CONV_KERNEL = 31
SSM_GROUP = 16
SSM_GROUPS = SSM_WIDTH // SSM_GROUP
SSM_STATE = 64
DT_MIN = 1e-3
DT_MAX = 1e-1
IN_WIDTH = 2 * CONV_WIDTH + SSM_WIDTH
MOE_GROUPS = 4
EXPERTS_PER_GROUP = 8
N_EXPERTS = MOE_GROUPS * EXPERTS_PER_GROUP
TOP_K = 2
D_EXPERT = D_MODEL // 2
MOE_BLOCK = 128
EPS = 1e-6

kernel_name = "hybrid_conv_s5_hmoe_encoder"

def rms_norm(x, g):
    xf = x.astype(jnp.float32)
    y = xf * lax.rsqrt(jnp.mean(xf * xf, axis=-1, keepdims=True) + EPS)
    return (y * g.astype(jnp.float32)).astype(x.dtype)

def layer_norm(x, g, b):
    xf = x.astype(jnp.float32)
    mu = jnp.mean(xf, axis=-1, keepdims=True)
    xc = xf - mu
    y = xc * lax.rsqrt(jnp.mean(xc * xc, axis=-1, keepdims=True) + EPS)
    return (y * g.astype(jnp.float32) + b.astype(jnp.float32)).astype(x.dtype)

def conformer_conv(v, gate, w, b, ln_g, ln_b):
    u = v * jax.nn.sigmoid(gate)
    up = jnp.pad(u, ((0, 0), (CONV_KERNEL - 1, 0), (0, 0)))
    y = lax.conv_general_dilated(up, w[:, None, :], window_strides=(1,), padding='VALID',
                                 dimension_numbers=('NWC', 'WIO', 'NWC'),
                                 feature_group_count=CONV_WIDTH) + b
    y = layer_norm(y, ln_g, ln_b)
    return jax.nn.silu(y)

def _complex_scan_combine(left, right):
    a1r, a1i, b1r, b1i = left
    a2r, a2i, b2r, b2i = right
    return (a2r * a1r - a2i * a1i,
            a2r * a1i + a2i * a1r,
            a2r * b1r - a2i * b1i + b2r,
            a2r * b1i + a2i * b1r + b2i)

def s5_ssm(u, lam_re, lam_im, log_dt, b_re, b_im, c_re, c_im, d, glu_w, glu_b):
    f32 = jnp.float32
    bsz, seq, _ = u.shape
    uf = u.astype(f32)
    ug = uf.reshape(bsz, seq, SSM_GROUPS, SSM_GROUP)
    dt = jnp.exp(log_dt.astype(f32))[:, None]
    lr = lam_re.astype(f32)
    li = lam_im.astype(f32)
    mag = jnp.exp(lr * dt)
    ab_re = mag * jnp.cos(li * dt)
    ab_im = mag * jnp.sin(li * dt)
    den = lr * lr + li * li
    nr = ab_re - 1.0
    q_re = (nr * lr + ab_im * li) / den
    q_im = (ab_im * lr - nr * li) / den
    br = b_re.astype(f32)
    bi = b_im.astype(f32)
    bb_re = q_re[..., None] * br - q_im[..., None] * bi
    bb_im = q_re[..., None] * bi + q_im[..., None] * br
    drv_re = jnp.einsum('bsgc,gnc->sbgn', ug, bb_re)
    drv_im = jnp.einsum('bsgc,gnc->sbgn', ug, bb_im)
    a_re = jnp.broadcast_to(ab_re[None, None], (seq, 1, SSM_GROUPS, SSM_STATE))
    a_im = jnp.broadcast_to(ab_im[None, None], (seq, 1, SSM_GROUPS, SSM_STATE))
    _, _, h_re, h_im = lax.associative_scan(_complex_scan_combine,
                                            (a_re, a_im, drv_re, drv_im), axis=0)
    y = (jnp.einsum('sbgn,gcn->bsgc', h_re, c_re.astype(f32))
         - jnp.einsum('sbgn,gcn->bsgc', h_im, c_im.astype(f32)))
    y = y.reshape(bsz, seq, SSM_WIDTH) + d.astype(f32) * uf
    y = jax.nn.gelu(y).astype(u.dtype)
    return y * jax.nn.sigmoid(y @ glu_w + glu_b)

def hierarchical_moe(x, w_rg, b_rg, w_re, b_re, w_gate, w_up, w_down):
    f32 = jnp.float32
    bsz, seq, dm = x.shape
    n_tok = bsz * seq
    xt = x.reshape(n_tok, dm)
    xf = xt.astype(f32)
    tok_idx = jnp.arange(n_tok)
    g_logits = xf @ w_rg.astype(f32) + b_rg.astype(f32)
    g_prob = jax.nn.softmax(g_logits, axis=-1)
    grp = jnp.argmax(g_logits, axis=-1)
    p_grp = g_prob[tok_idx, grp]
    e_logits = (xf @ w_re.astype(f32) + b_re.astype(f32)).reshape(n_tok, MOE_GROUPS, EXPERTS_PER_GROUP)
    e_in = e_logits[tok_idx, grp]
    top_v, top_i = lax.top_k(e_in, TOP_K)
    gates = jax.nn.softmax(top_v, axis=-1) * p_grp[:, None]
    expert = (grp[:, None] * EXPERTS_PER_GROUP + top_i).reshape(-1).astype(jnp.int32)
    gate = gates.reshape(-1)
    token = jnp.repeat(tok_idx, TOP_K).astype(jnp.int32)
    n_asg = n_tok * TOP_K
    n_blocks = -(-n_asg // MOE_BLOCK) + N_EXPERTS
    cap = n_blocks * MOE_BLOCK
    order = jnp.argsort(expert)
    e_sorted = expert[order]
    counts = jnp.bincount(expert, length=N_EXPERTS)
    starts = jnp.cumsum(counts) - counts
    padded = (counts + MOE_BLOCK - 1) // MOE_BLOCK * MOE_BLOCK
    pad_ends = jnp.cumsum(padded)
    pad_starts = pad_ends - padded
    slot = pad_starts[e_sorted] + jnp.arange(n_asg) - starts[e_sorted]
    slot_token = jnp.full((cap,), n_tok, jnp.int32).at[slot].set(token[order])
    slot_gate = jnp.zeros((cap,), f32).at[slot].set(gate[order])
    block_expert = jnp.minimum(
        jnp.searchsorted(pad_ends, jnp.arange(n_blocks) * MOE_BLOCK, side='right'), N_EXPERTS - 1)
    x_pad = jnp.concatenate([xt, jnp.zeros((1, dm), xt.dtype)], axis=0)
    xb = x_pad[slot_token].reshape(n_blocks, MOE_BLOCK, dm)

    def expert_block(args):
        xblk, e = args
        hid = jax.nn.silu(xblk @ w_gate[e]) * (xblk @ w_up[e])
        return hid @ w_down[e]

    yb = lax.map(expert_block, (xb, block_expert)).reshape(cap, dm)
    y = jax.ops.segment_sum(yb.astype(f32) * slot_gate[:, None], slot_token, num_segments=n_tok + 1)[:n_tok]
    return y.astype(x.dtype).reshape(bsz, seq, dm)

def setup_inputs(seed: int = 0) -> dict:
    key = jax.random.key(seed)
    ks = jax.random.split(key, 32)
    f32 = jnp.float32
    L = DEPTH

    def nrm(k, shape, scale):
        return jax.random.normal(k, shape, f32) * scale

    x = jax.random.normal(ks[0], (BATCH, SEQ, D_MODEL), f32)
    g_mix = 1.0 + nrm(ks[1], (L, D_MODEL), 0.02)
    w_in = nrm(ks[2], (L, D_MODEL, IN_WIDTH), D_MODEL ** -0.5)
    conv_w = nrm(ks[3], (L, CONV_KERNEL, CONV_WIDTH), CONV_KERNEL ** -0.5)
    conv_b = nrm(ks[4], (L, CONV_WIDTH), 0.02)
    conv_ln_g = 1.0 + nrm(ks[5], (L, CONV_WIDTH), 0.02)
    conv_ln_b = nrm(ks[6], (L, CONV_WIDTH), 0.02)
    ssm_lam_re = -0.5 * jnp.exp(nrm(ks[7], (L, SSM_GROUPS, SSM_STATE), 0.05))
    ssm_lam_im = (jnp.pi * jnp.arange(SSM_STATE, dtype=f32))[None, None, :] + nrm(ks[8], (L, SSM_GROUPS, SSM_STATE), 0.01)
    ssm_log_dt = jax.random.uniform(ks[9], (L, SSM_GROUPS), f32, math.log(DT_MIN), math.log(DT_MAX))
    ssm_b_re = nrm(ks[10], (L, SSM_GROUPS, SSM_STATE, SSM_GROUP), (2 * SSM_GROUP) ** -0.5)
    ssm_b_im = nrm(ks[11], (L, SSM_GROUPS, SSM_STATE, SSM_GROUP), (2 * SSM_GROUP) ** -0.5)
    ssm_c_re = nrm(ks[12], (L, SSM_GROUPS, SSM_GROUP, SSM_STATE), (2 * SSM_STATE) ** -0.5)
    ssm_c_im = nrm(ks[13], (L, SSM_GROUPS, SSM_GROUP, SSM_STATE), (2 * SSM_STATE) ** -0.5)
    ssm_d = nrm(ks[14], (L, SSM_WIDTH), 1.0)
    ssm_glu_w = nrm(ks[15], (L, SSM_WIDTH, SSM_WIDTH), SSM_WIDTH ** -0.5)
    ssm_glu_b = nrm(ks[16], (L, SSM_WIDTH), 0.02)
    g_branch = 1.0 + nrm(ks[17], (L, MIX_WIDTH), 0.02)
    w_out = nrm(ks[18], (L, MIX_WIDTH, D_MODEL), MIX_WIDTH ** -0.5)
    g_ffn = 1.0 + nrm(ks[19], (L, D_MODEL), 0.02)
    w_router_group = nrm(ks[20], (L, D_MODEL, MOE_GROUPS), D_MODEL ** -0.5)
    b_router_group = nrm(ks[21], (L, MOE_GROUPS), 0.01)
    w_router_expert = nrm(ks[22], (L, D_MODEL, N_EXPERTS), D_MODEL ** -0.5)
    b_router_expert = nrm(ks[23], (L, N_EXPERTS), 0.01)
    w_gate = nrm(ks[24], (L, N_EXPERTS, D_MODEL, D_EXPERT), D_MODEL ** -0.5)
    w_up = nrm(ks[25], (L, N_EXPERTS, D_MODEL, D_EXPERT), D_MODEL ** -0.5)
    w_down = nrm(ks[26], (L, N_EXPERTS, D_EXPERT, D_MODEL), D_EXPERT ** -0.5)
    g_final = 1.0 + nrm(ks[27], (D_MODEL,), 0.02)
    return {"x": x, "g_mix": g_mix, "w_in": w_in, "conv_w": conv_w, "conv_b": conv_b,
            "conv_ln_g": conv_ln_g, "conv_ln_b": conv_ln_b,
            "ssm_lam_re": ssm_lam_re, "ssm_lam_im": ssm_lam_im, "ssm_log_dt": ssm_log_dt,
            "ssm_b_re": ssm_b_re, "ssm_b_im": ssm_b_im, "ssm_c_re": ssm_c_re, "ssm_c_im": ssm_c_im,
            "ssm_d": ssm_d, "ssm_glu_w": ssm_glu_w, "ssm_glu_b": ssm_glu_b,
            "g_branch": g_branch, "w_out": w_out, "g_ffn": g_ffn,
            "w_router_group": w_router_group, "b_router_group": b_router_group,
            "w_router_expert": w_router_expert, "b_router_expert": b_router_expert,
            "w_gate": w_gate, "w_up": w_up, "w_down": w_down, "g_final": g_final}

def reference(x, g_mix, w_in, conv_w, conv_b, conv_ln_g, conv_ln_b,
              ssm_lam_re, ssm_lam_im, ssm_log_dt, ssm_b_re, ssm_b_im, ssm_c_re, ssm_c_im,
              ssm_d, ssm_glu_w, ssm_glu_b, g_branch, w_out, g_ffn,
              w_router_group, b_router_group, w_router_expert, b_router_expert,
              w_gate, w_up, w_down, g_final):
    for l in range(DEPTH):
        h = rms_norm(x, g_mix[l])
        z = h @ w_in[l]
        c_val = z[..., :CONV_WIDTH]
        c_gate = z[..., CONV_WIDTH:2 * CONV_WIDTH]
        s_in = z[..., 2 * CONV_WIDTH:]
        y_conv = conformer_conv(c_val, c_gate, conv_w[l], conv_b[l], conv_ln_g[l], conv_ln_b[l])
        y_ssm = s5_ssm(s_in, ssm_lam_re[l], ssm_lam_im[l], ssm_log_dt[l], ssm_b_re[l], ssm_b_im[l],
                       ssm_c_re[l], ssm_c_im[l], ssm_d[l], ssm_glu_w[l], ssm_glu_b[l])
        gb = g_branch[l]
        y_cat = jnp.concatenate([rms_norm(y_conv, gb[:CONV_WIDTH]),
                                 rms_norm(y_ssm, gb[CONV_WIDTH:])], axis=-1)
        x = x + y_cat @ w_out[l]
        h = rms_norm(x, g_ffn[l])
        x = x + hierarchical_moe(h, w_router_group[l], b_router_group[l],
                                 w_router_expert[l], b_router_expert[l],
                                 w_gate[l], w_up[l], w_down[l])
    return rms_norm(x, g_final)


_drawn_inputs = setup_inputs


def setup_inputs(seed=0):
    import zlib

    import numpy as np

    out = dict(_drawn_inputs(seed))
    spreads = {}
    factors = {'conv_ln_g': 25.03,
     'conv_ln_b': 24.401,
     'ssm_lam_re': 200.0,
     'ssm_glu_b': 5.435,
     'b_router_group': 29.592,
     'b_router_expert': 5.174,
     'g_final': 30.413,
     'ssm_lam_im': 16.891,
     'ssm_log_dt': 18.122,
     'ssm_b_re': 22.451,
     'ssm_b_im': 23.206,
     'ssm_c_re': 23.907,
     'ssm_c_im': 26.4,
     'g_ffn': 2.923}
    for name, (base, spread) in spreads.items():
        noise = np.random.default_rng([zlib.crc32(name.encode()), seed]).standard_normal(out[name].shape)
        drawn = base * np.exp(spread * noise) if base else spread * noise
        out[name] = __import__('jax').numpy.asarray(drawn.astype(out[name].dtype))
    for name, factor in factors.items():
        out[name] = (out[name] * factor).astype(out[name].dtype)
    return out
```

```python
import math
from contextlib import ExitStack

import concourse.bass as bass
from concourse import mybir

FP32 = mybir.dt.float32
FP32R = mybir.dt.float32r
INT32 = mybir.dt.int32
ALU = mybir.AluOpType
ACT = mybir.ActivationFunctionType
AX = mybir.AxisListType

P = 128
EPS = 1e-6
SEQ, D = 2048, 1024
CW = SW = 512
TAPS = 31
GRP, GC, NS = 32, 16, 64
NG, EPG, F = 4, 8, 512
NE = NG * EPG
T8 = 8
NK = SEQ // T8
KD = D // P
CT = CW // P
TT = SEQ // P
NBLK = SEQ * 2 // P + NE
TBLK = NBLK + SEQ // P + 1
ROWS = SEQ + P
UG = 4
NU = GRP // UG
LAGS = 2 * T8 - 1


class Chain:

    def __init__(self, engine, sem, base=0):
        self.engine, self.sem, self.base, self.n = engine, sem, base, 0

    def __call__(self, instruction):
        self.n += 1
        instruction.then_inc(self.sem, 1)
        self.engine.wait_ge(self.sem, self.base + self.n)


def bc(ap, axis, n):
    v = ap.unsqueeze(axis)
    shape = list(v.shape)
    shape[axis] = n
    return v.broadcast_to(shape)


RSQRT_STEPS = 12


def rsqrt(nc, step, y, a, t, u):
    yi, ai = y.bitcast(INT32), a.bitcast(INT32)
    step(nc.vector.tensor_scalar(yi, ai, 1, None, ALU.logical_shift_right))
    step(nc.vector.tensor_scalar(yi, yi, -1.0, float(0x5F3759DF), ALU.mult, ALU.add))
    step(nc.vector.tensor_scalar(a, a, -0.5, None, ALU.mult))
    for _ in range(3):
        step(nc.vector.tensor_tensor(t, y, y, ALU.mult))
        step(nc.vector.tensor_tensor(u, t, a, ALU.mult))
        step(nc.vector.scalar_tensor_tensor(out=y, in0=u, scalar=1.5, in1=y, op0=ALU.add, op1=ALU.mult))


MAGIC = 1.5 * 2.0 ** 23


def exp_precise(nc, step, y, x, t, n, q):
    ln2_hi, ln2_lo = 0.693359375, -2.12194440e-4
    step(nc.vector.tensor_scalar(x, x, 88.0, -88.0, ALU.min, ALU.max))
    step(nc.vector.tensor_scalar(n, x, 1.0 / math.log(2.0), MAGIC, ALU.mult, ALU.add))
    step(nc.vector.tensor_scalar(n, n, -MAGIC, None, ALU.add))
    step(nc.vector.scalar_tensor_tensor(out=t, in0=n, scalar=-ln2_hi, in1=x, op0=ALU.mult, op1=ALU.add))
    step(nc.vector.scalar_tensor_tensor(out=t, in0=n, scalar=-ln2_lo, in1=t, op0=ALU.mult, op1=ALU.add))
    step(nc.vector.tensor_scalar(q, t, 1.0 / math.factorial(8), None, ALU.mult))
    for d in range(7, 0, -1):
        step(nc.vector.scalar_tensor_tensor(out=q, in0=q, scalar=1.0 / math.factorial(d), in1=t,
                                            op0=ALU.add, op1=ALU.mult))
    step(nc.vector.tensor_scalar(n.bitcast(INT32), n, 127.0, 2.0 ** 23, ALU.add, ALU.mult))
    step(nc.vector.scalar_tensor_tensor(out=y, in0=q, scalar=1.0, in1=n, op0=ALU.add, op1=ALU.mult))


def sincos_precise(nc, step, s, c, x, n, t):
    two_pi = 2 * math.pi
    p1 = 6.28125
    p2 = float(int((two_pi - p1) * 2 ** 22)) / 2 ** 22
    p3 = two_pi - p1 - p2
    step(nc.vector.tensor_scalar(n, x, 1.0 / two_pi, MAGIC, ALU.mult, ALU.add))
    step(nc.vector.tensor_scalar(n, n, -MAGIC, None, ALU.add))
    for p in (p1, p2, p3):
        step(nc.vector.scalar_tensor_tensor(out=x, in0=n, scalar=-p, in1=x, op0=ALU.mult, op1=ALU.add))
    step(nc.vector.tensor_scalar(x, x, 3.2, -3.2, ALU.min, ALU.max))
    step(nc.vector.tensor_scalar(x, x, 0.25, None, ALU.mult))
    step(nc.vector.tensor_tensor(t, x, x, ALU.mult))
    for out, first in ((s, 11), (c, 12)):
        terms = list(range(first, 1, -2))
        step(nc.vector.tensor_scalar(out, t, (-1) ** (first // 2) / math.factorial(first), None, ALU.mult))
        for d in terms[1:]:
            step(nc.vector.scalar_tensor_tensor(out=out, in0=out, scalar=(-1) ** (d // 2) / math.factorial(d),
                                                in1=t, op0=ALU.add, op1=ALU.mult))
    step(nc.vector.scalar_tensor_tensor(out=s, in0=s, scalar=1.0, in1=x, op0=ALU.add, op1=ALU.mult))
    step(nc.vector.tensor_scalar(c, c, 1.0, None, ALU.add))
    for _ in range(2):
        step(nc.vector.tensor_tensor(t, s, s, ALU.mult))
        step(nc.vector.scalar_tensor_tensor(out=s, in0=s, scalar=2.0, in1=c, op0=ALU.mult, op1=ALU.mult))
        step(nc.vector.tensor_scalar(c, t, -2.0, 1.0, ALU.mult, ALU.add))


def complex_mul(engine, step, outr, outi, ar, ai, br, bi, t, u):
    step(engine.tensor_tensor(t, ar, br, ALU.mult))
    step(engine.tensor_tensor(u, ai, bi, ALU.mult))
    step(engine.tensor_tensor(outr, t, u, ALU.subtract))
    step(engine.tensor_tensor(t, ar, bi, ALU.mult))
    step(engine.tensor_tensor(u, ai, br, ALU.mult))
    step(engine.tensor_tensor(outi, t, u, ALU.add))


def hybrid_encoder(nc, x, g_mix, w_in, conv_w, conv_b, conv_ln_g, conv_ln_b, lam_re, lam_im, log_dt,
                   b_re, b_im, c_re, c_im, ssm_d, glu_w, glu_b, g_branch, w_out, g_ffn, w_rg, b_rg,
                   w_re, b_re_router, w_gate, w_up, w_down, g_final, out):
    def dram(name, shape, dt=FP32):
        return nc.dram_tensor(name, shape, dt).ap()

    scratch = dict(
        s=dram("ssm_input", [SW, T8, NK]),
        u=dram("conv_input", [CW, T8, NK]),
        conv=dram("conv_output", [CW, T8, NK]),
        y=dram("ssm_output", [SW, T8, NK]),
        w12=dram("state_in_weights", [P, GRP, 2 * P]),
        o1=dram("state_out_weights_1", [P, GRP, T8 * GC]),
        o2=dram("state_out_weights_2", [P, GRP, T8 * GC]),
        kernel=dram("chunk_kernels", [GC, GRP, LAGS * GC]),
        twc=dram("turn_cos", [P, GRP, NK]),
        tws=dram("turn_sin", [P, GRP, NK]),
        h=dram("ffn_input", [ROWS, D]),
        acc=dram("residual", [ROWS, D]),
        table=dram("slot_table", [TBLK * P, 2], INT32),
    )
    ctx = ExitStack()
    with ctx:
        ident = ctx.enter_context(nc.sbuf_tensor("ident", [P, P], FP32))
        eye_turn = ctx.enter_context(nc.sbuf_tensor("eye_turn", [P, 2 * P], FP32))
        decay8 = ctx.enter_context(nc.sbuf_tensor("decay8", [P, GRP], FP32))
        logits = ctx.enter_context(nc.sbuf_tensor("logits", [P, TT, NG + NE], FP32))
        counts = ctx.enter_context(nc.sbuf_tensor("counts", [P, 3, NE], INT32))
        with ExitStack() as early:
            early_sem = semaphores_cleared_after(nc, early)
            constants(nc, early_sem, ident, eye_turn)
            projection(nc, early_sem, scratch, x, g_mix, w_in, ident)
        ssm_tables(nc, scratch, ident, eye_turn, decay8, lam_re, lam_im, log_dt, b_re, b_im, c_re, c_im)
        ssm(nc, scratch, decay8)
        convolution(nc, scratch, conv_w, conv_b)
        mix(nc, scratch, ident, logits, x, conv_ln_g, conv_ln_b, ssm_d, glu_w, glu_b, g_branch, w_out,
            g_ffn, w_rg, b_rg, w_re, b_re_router)
        route(nc, scratch, ident, logits, counts)
        experts(nc, scratch, ident, counts, w_gate, w_up, w_down)
        final_norm(nc, scratch, g_final, out)


def load_column(nc, engine, to, vector):
    with nc.allow_non_contiguous_dma(reason="a short vector, read once"):
        return engine.dma_start(to, vector.rearrange("(c p) -> p c", p=P))


def alloc(nc, ctx, prefix):
    def sb(name, shape, dt=FP32):
        return ctx.enter_context(nc.sbuf_tensor(f"{prefix}_{name}", shape, dt))

    def ps(name, shape=(P, 512)):
        return ctx.enter_context(nc.psum_tensor(f"{prefix}_{name}", list(shape), FP32))

    def sem(name):
        return ctx.enter_context(nc.semaphore(f"{prefix}_{name}"))

    return sb, ps, sem


def semaphores_cleared_after(nc, ctx):
    taken = []

    def give_back():
        nc.all_engine_barrier()
        nc.clear_and_free_semaphores(taken)
        nc.all_engine_barrier()

    ctx.callback(give_back)

    def sem(name):
        taken.append(nc.alloc_semaphore(name=name))
        return taken[-1]

    return sem


def constants(nc, sem, ident, eye_turn):
    with ExitStack() as ctx:
        cleared, built = sem("cleared"), sem("built")
        block = ctx.enter_context(nc.Block())

        @block.gpsimd
        def _(pool):
            nc.gpsimd.memset(ident[:, :], 0.0).then_inc(cleared, 1)
            nc.gpsimd.memset(eye_turn[:, :], 0.0).then_inc(cleared, 1)
            pool.wait_ge(cleared, 2)
            step = Chain(pool, built)

            def diagonal(ap, base, fill):
                step(nc.gpsimd.affine_select(out=ap, in_=ap, compare_op=ALU.not_equal, fill=fill, base=-base,
                                             pattern=[[-1, ap.shape[1]]], channel_multiplier=1))

            diagonal(ident[:, :], 0, 1.0)
            diagonal(eye_turn[:, 0:P], 0, 1.0)
            diagonal(eye_turn[:, P:2 * P], NS, 1.0)
            diagonal(eye_turn[:, P:2 * P], -NS, -1.0)


def projection(nc, sem, scratch, x, g_mix, w_in, ident):
    NZ = 3 * CW
    x_rows = x.rearrange("(h k s) d -> s k h d", s=T8, h=2)
    w_rows = w_in.rearrange("(c p) n -> c p n", p=P)
    with ExitStack() as ctx:
        sb, ps, _ = alloc(nc, ctx, "proj")
        w_raw = sb("w_raw", [P, 2, NZ])
        w_hi, w_lo = sb("w_hi", [P, KD, NZ], FP32R), sb("w_lo", [P, KD, NZ], FP32R)
        h_hi, h_lo = sb("h_hi", [P, 2, KD, NK], FP32R), sb("h_lo", [P, 2, KD, NK], FP32R)
        x_sb = sb("x_sb", [P, 2, 2, D])
        junk = sb("junk", [P, D])
        gain = sb("gain", [P, KD])
        stat = sb("stat", [P, 4, 2])
        sig = sb("sig", [P, 2, NK])
        s_out, u_out = sb("s_out", [P, CT, NK]), sb("u_out", [P, CT, NK])
        p_tr = [ps("p_tr0"), ps("p_tr1")]
        p_z = [ps(f"p_z{i}") for i in range(6)]

        w_read = [sem("w_read0"), sem("w_read1")]
        w_hi_done, w_lo_done = sem("w_hi_done"), sem("w_lo_done")
        gain_in, x_in = sem("gain_in"), [sem("x_in0"), sem("x_in1")]
        squared, own, scaled = sem("squared"), sem("own"), sem("scaled")
        turned, hi_done, lo_done = sem("turned"), sem("hi_done"), sem("lo_done")
        z_done, z_free_s, sig_done, u_done = sem("z_done"), sem("z_free_s"), sem("sig_done"), sem("u_done")
        s_stored, u_stored = sem("s_stored"), sem("u_stored")
        block = ctx.enter_context(nc.Block())
        PAIRS = T8 // 2

        def over_tiles(engine, body):
            with engine.Fori(0, PAIRS - 1) as i:
                body(i * 2, 0, True)
                body(i * 2 + 1, 1, True)
            body(T8 - 2, 0, True)
            body(T8 - 1, 1, False)

        @block.sync
        def _(sp):
            load_column(nc, sp, gain[:, :], g_mix).then_inc(gain_in, 16)
            for n in range(2):
                sp.dma_start(x_sb[:, n], x_rows[n]).then_inc(x_in[n], 16)
            for c in range(KD):
                if c >= 2:
                    sp.wait_ge(w_lo_done, c - 1)
                sp.dma_start(w_raw[:, c % 2], w_rows[c]).then_inc(w_read[c % 2], 16)
            s_v = scratch["s"].rearrange("(c p) s k -> s p c k", p=P)
            u_v = scratch["u"].rearrange("(c p) s k -> s p c k", p=P)

            def body(n, half, more):
                sp.wait_ge(z_free_s, n * 2 + 2)
                sp.dma_start(s_v[n], s_out[:, :, :]).then_inc(s_stored, 16)
                sp.wait_ge(u_done, n * CT + CT)
                sp.dma_start(u_v[n], u_out[:, :, :]).then_inc(u_stored, 16)

            with sp.Fori(0, PAIRS - 1) as i:
                for half in range(2):
                    n = i * 2 + half
                    sp.wait_ge(turned, n * 4 + 4)
                    sp.dma_start(x_sb[:, half], x_rows[n + 2]).then_inc(x_in[half], 16)
                    body(n, half, True)
            for n in (T8 - 2, T8 - 1):
                body(n, n % 2, True)
            sp.wait_ge(s_stored, 16 * T8)
            sp.wait_ge(u_stored, 16 * T8)

        @block.scalar
        def _(act):
            def square(n, half):
                act.wait_ge(x_in[half], (n - half) * 8 + 16)
                for h in range(2):
                    nc.scalar.activation(junk[:, :], x_sb[:, half, h], ACT.Square,
                                         accum_out=stat[:, 0, h:h + 1]).then_inc(squared, 1)
                    act.wait_ge(squared, n * 2 + h + 1)

            def highs(n, half, js):
                for j in js:
                    act.wait_ge(turned, n * 4 + j + 1)
                    for c in (2 * j, 2 * j + 1):
                        last = nc.scalar.activation(h_hi[:, half, c], p_tr[j % 2][:, (c % 2) * NK:(c % 2 + 1) * NK],
                                                    ACT.Copy, scale=gain[:, c:c + 1])
                    last.then_inc(hi_done, 1)

            def copy_ssm(n):
                for j in range(2):
                    act.wait_ge(z_done, n * 6 + j + 1)
                    if j == 0:
                        act.wait_ge(s_stored, n * 16)
                    nc.scalar.copy(s_out[:, 2 * j:2 * j + 2, :].rearrange("p c k -> p (c k)"),
                                   p_z[j][:, :]).then_inc(z_free_s, 1)
            def gates(n, js):
                for j in js:
                    act.wait_ge(z_done, n * 6 + 3 + j)
                    if j >= 2:
                        act.wait_ge(u_done, n * CT + j - 1)
                    nc.scalar.activation(sig[:, j % 2], p_z[2 + j][:, NK:2 * NK], ACT.Sigmoid).then_inc(sig_done, 1)

            act.wait_ge(gain_in, 16)
            square(0, 0)
            for c in range(KD):
                act.wait_ge(w_read[c % 2], 16 * (c // 2 + 1))
                nc.scalar.copy(w_hi[:, c], w_raw[:, c % 2]).then_inc(w_hi_done, 1)
            highs(0, 0, range(4))

            def body(n, half, more):
                if more:
                    square(n + 1, 1 - half)
                copy_ssm(n)
                for js in ((0, 1), (2, 3)):
                    if more:
                        highs(n + 1, 1 - half, js)
                    gates(n, js)
            over_tiles(act, body)

        @block.vector
        def _(dve):
            def scale_x(n, half):
                step = Chain(dve, own, n * (RSQRT_STEPS + 1))
                dve.wait_ge(squared, n * 2 + 2)
                a = stat[:, 1]
                step(nc.vector.tensor_scalar(a, stat[:, 0], 1.0 / D, EPS, ALU.mult, ALU.add))
                rsqrt(nc, step, stat[:, 3], a, stat[:, 2], stat[:, 0])
                for h in range(2):
                    last = nc.vector.tensor_scalar(x_sb[:, half, h], x_sb[:, half, h], stat[:, 3, h:h + 1], None, ALU.mult)
                last.then_inc(scaled, 1)

            def lows(n, half, js):
                for j in js:
                    dve.wait_ge(hi_done, n * 4 + j + 1)
                    for c in (2 * j, 2 * j + 1):
                        last = nc.vector.scalar_tensor_tensor(
                            out=h_lo[:, half, c], in0=p_tr[j % 2][:, (c % 2) * NK:(c % 2 + 1) * NK],
                            scalar=gain[:, c:c + 1], in1=h_hi[:, half, c].bitcast(FP32),
                            op0=ALU.mult, op1=ALU.subtract)
                    last.then_inc(lo_done, 1)

            def glu(n, js):
                for j in js:
                    dve.wait_ge(sig_done, n * CT + j + 1)
                    if j == 0:
                        dve.wait_ge(u_stored, n * 16)
                    nc.vector.tensor_tensor(u_out[:, j], p_z[2 + j][:, 0:NK], sig[:, j % 2], ALU.mult).then_inc(u_done, 1)

            dve.wait_ge(gain_in, 16)
            scale_x(0, 0)
            for c in range(KD):
                dve.wait_ge(w_hi_done, c + 1)
                nc.vector.tensor_tensor(w_lo[:, c], w_raw[:, c % 2], w_hi[:, c].bitcast(FP32),
                                        ALU.subtract).then_inc(w_lo_done, 1)
            lows(0, 0, range(4))

            def body(n, half, more):
                if more:
                    scale_x(n + 1, 1 - half)
                for js in ((0, 1), (2, 3)):
                    if more:
                        lows(n + 1, 1 - half, js)
                    glu(n, js)
            over_tiles(dve, body)

        @block.tensor
        def _(pe):
            def transposes(n, half, js):
                pe.wait_ge(scaled, n + 1)
                for j in js:
                    if j >= 2:
                        pe.wait_ge(lo_done, n * 4 + j - 1)
                    for c in (2 * j, 2 * j + 1):
                        for h in range(2):
                            at = (c % 2) * NK + h * P
                            last = nc.tensor.transpose(p_tr[j % 2][:, at:at + P], x_sb[:, half, h, c * P:(c + 1) * P], ident[:, :])
                    last.then_inc(turned, 1)

            def products(n, half, more):
                pe.wait_ge(lo_done, n * 4 + 4)
                units = [(8, 9), (10, 11), (0, 4), (1, 5), (2, 6), (3, 7)]
                for j, blocks in enumerate(units):
                    if j == 0:
                        pe.wait_ge(z_free_s, n * 2)
                        pe.wait_ge(u_done, n * CT)
                    for b, m in enumerate(blocks):
                        o = p_z[j][:, b * NK:(b + 1) * NK]
                        for c in range(KD):
                            whi, wlo = w_hi[:, c, m * P:(m + 1) * P], w_lo[:, c, m * P:(m + 1) * P]
                            nc.tensor.matmul(o, whi, h_hi[:, half, c], start=c == 0, stop=False)
                            nc.tensor.matmul(o, whi, h_lo[:, half, c], start=False, stop=False)
                            last = nc.tensor.matmul(o, wlo, h_hi[:, half, c], start=False, stop=c == KD - 1)
                    last.then_inc(z_done, 1)
                    if more and j in (1, 3):
                        transposes(n + 1, 1 - half, (j - 1, j))

            transposes(0, 0, range(4))
            pe.wait_ge(w_lo_done, KD)

            over_tiles(pe, products)


def ssm_tables(nc, scratch, ident, eye_turn, decay8, lam_re, lam_im, log_dt, b_re, b_im, c_re, c_im):
    NP = T8 + 1
    with ExitStack() as ctx:
        sb, ps, sem = alloc(nc, ctx, "tab")
        lam_rows = sb("lam_rows", [GRP, 2, P])
        lam = sb("lam", [P, 2, GRP])
        dt = sb("dt", [P, GRP])
        b_raw, bb = sb("b_raw", [P, 2, GRP, GC]), sb("bb", [P, 2, GRP, GC])
        c_rows, c_cols = sb("c_rows", [P, 2, CT, P]), sb("c_cols", [P, 2, GRP * GC])
        tmp = sb("tmp", [P, 2, GRP, GC])
        small, wide = sb("small", [P, 8, GRP]), sb("wide", [P, 2, T8 // 2, GRP])
        pw_re, pw_im = sb("pw_re", [P, NP, GRP]), sb("pw_im", [P, NP, GRP])
        turn8 = sb("turn8", [P, 2, GRP])
        in_re, in_im = sb("in_re", [P, GRP, NP]), sb("in_im", [P, GRP, NP])
        out_re, out_im = sb("out_re", [P, GRP, NP]), sb("out_im", [P, GRP, NP])
        v = sb("v", [P, UG, T8, GC])
        o1 = sb("o1", [P, UG, NP, GC])
        vt = sb("vt", [P, UG, NP, GC])
        w12, o2 = sb("w12", [P, UG, 2 * P]), sb("o2", [P, UG, P])
        kern = sb("kern", [GC, UG, LAGS * GC])
        turn = sb("turn", [P, 2, UG, NK])
        tt = sb("tt", [P, 2, UG, NK // 2])
        p_w = [ps("p_w0"), ps("p_w1")]
        p_k, p_o = ps("p_k"), ps("p_o")
        p_c = [ps("p_c0"), ps("p_c1")]

        loaded, own, own_pool = sem("loaded"), sem("own"), sem("own_pool")
        lam_turned, c_turned, c_ready = sem("lam_turned"), sem("c_turned"), sem("c_ready")
        base_ready, turn8_ready = sem("base_ready"), sem("turn8_ready")
        v_ready, products_done, copied, turns_done = sem("v_ready"), sem("products_done"), sem("copied"), sem("turns_done")
        kern_clear = sem("kern_clear")
        st_w, st_o1, st_o2, st_k, st_t = (sem(n) for n in ("st_w", "st_o1", "st_o2", "st_k", "st_t"))
        block = ctx.enter_context(nc.Block())
        LOADS = 4 + 1 + 4 + 4

        @block.sync
        def _(sp):
            for i, a in enumerate((lam_re, lam_im)):
                for h in range(2):
                    sp.dma_start(lam_rows[:, i, h * NS:(h + 1) * NS], a).then_inc(loaded, 16)
            sp.dma_start(dt[:, :], log_dt.partition_broadcast(P)).then_inc(loaded, 16)
            for i, a in enumerate((c_re, c_im)):
                rows = a.rearrange("(t g) c n -> (g c) t n", t=CT)
                for h in range(2):
                    sp.dma_start(c_rows[:, i, :, h * NS:(h + 1) * NS], rows).then_inc(loaded, 16)
            for i, a in enumerate((b_re, b_im)):
                for h in range(2):
                    sp.dma_start(b_raw[h * NS:(h + 1) * NS, i], a.rearrange("g n c -> n g c")).then_inc(loaded, 16)
            with sp.Fori(0, NU) as n:
                sp.wait_ge(copied, 3 * n + 3)
                sp.dma_start(scratch["w12"].rearrange("p (u g) m -> u p g m", g=UG)[n], w12[:, :, :]).then_inc(st_w, 16)
                sp.dma_start(scratch["kernel"].rearrange("p (u g) m -> u p g m", g=UG)[n], kern[:, :, :]).then_inc(st_k, 16)
                sp.dma_start(scratch["o2"].rearrange("p (u g) m -> u p g m", g=UG)[n], o2[:, :, :]).then_inc(st_o2, 16)
                sp.wait_ge(v_ready, 2 * n + 2)
                sp.dma_start(scratch["o1"].rearrange("p (u g) m -> u p g m", g=UG)[n],
                             o1[:, :, 1:NP].rearrange("p g j c -> p g (j c)")).then_inc(st_o1, 16)
                sp.wait_ge(turns_done, n + 1)
                sp.dma_start(scratch["twc"].rearrange("p (u g) m -> u p g m", g=UG)[n], turn[:, 0]).then_inc(st_t, 16)
                sp.dma_start(scratch["tws"].rearrange("p (u g) m -> u p g m", g=UG)[n], turn[:, 1]).then_inc(st_t, 16)
            for s, k in ((st_w, 1), (st_k, 1), (st_o1, 1), (st_o2, 1), (st_t, 2)):
                sp.wait_ge(s, 16 * NU * k)

        @block.gpsimd
        def _(pool):
            pool.wait_ge(turn8_ready, 1)
            nc.gpsimd.memset(kern[:, :, :], 0.0).then_inc(kern_clear, 1)
            for i, one in enumerate((1.0, 0.0)):
                nc.gpsimd.memset(turn[:, i, :, 0:1], one)
            turn_steps = 2 + 6 * int(math.log2(NK))
            with pool.Fori(0, NU) as n:
                step = Chain(pool, own_pool, n * turn_steps)
                pool.wait_ge(st_t, n * 32)
                for i in range(2):
                    t8 = turn8[:, i, :].rearrange("p (u g) -> p u g", g=UG)[:, bass.ds(n, 1)]
                    step(nc.gpsimd.tensor_copy(turn[:, i, :, 1:2], t8.rearrange("p u g -> p g u")))
                m = 1
                while m < NK:
                    w = min(m, NK - 1 - m)
                    at_m = [turn[:, i, :, m:m + 1].broadcast_to([P, UG, w]) for i in range(2)]
                    known = [turn[:, i, :, 1:1 + w] for i in range(2)]
                    new = [turn[:, i, :, m + 1:m + 1 + w] for i in range(2)]
                    complex_mul(nc.gpsimd, step, *new, *at_m, *known, tt[:, 0, :, 0:w], tt[:, 1, :, 0:w])
                    m *= 2
                assert step.n == turn_steps
                pool.sem_inc(turns_done, 1)

        @block.scalar
        def _(act):
            act.wait_ge(kern_clear, 1)
            with act.Fori(0, NU) as n:
                act.wait_ge(products_done, n + 1)
                act.wait_ge(st_w, n * 16)
                for i in range(2):
                    last = nc.scalar.copy(w12[:, 2 * i:2 * i + 2, :].rearrange("p g m -> p (g m)"), p_w[i][:, :])
                last.then_inc(copied, 1)
                act.wait_ge(st_k, n * 16)
                nc.scalar.copy(kern[:, :, (T8 - 1) * GC:], p_k[0:GC, :].rearrange("p (g m) -> p g m", g=UG)).then_inc(copied, 1)
                act.wait_ge(st_o2, n * 16)
                nc.scalar.copy(o2[:, :, :].rearrange("p g m -> p (g m)"), p_o[:, :]).then_inc(copied, 1)

        @block.tensor
        def _(pe):
            pe.wait_ge(loaded, 16 * LOADS)
            for i in range(2):
                last = nc.tensor.transpose(p_k[:, i * GRP:(i + 1) * GRP], lam_rows[:, i, :], ident[0:GRP, 0:GRP])
            last.then_inc(lam_turned, 1)
            for i in range(2):
                for t in range(CT):
                    last = nc.tensor.transpose(p_c[i][:, t * P:(t + 1) * P], c_rows[:, i, t, :], ident[:, :])
            last.then_inc(c_turned, 1)
            pe.wait_ge(c_ready, 1)
            with pe.Fori(0, NU) as n:
                pe.wait_ge(v_ready, n * 2 + 2)
                pe.wait_ge(copied, n * 3)
                for g in range(UG):
                    nc.tensor.matmul(p_w[g // 2][:, (g % 2) * 2 * P:(g % 2 + 1) * 2 * P],
                                     v[:, g].rearrange("p j c -> p (j c)"), eye_turn[:, :], start=True, stop=True)
                    nc.tensor.matmul(p_k[0:GC, g * P:(g + 1) * P], v[:, g, 0, :],
                                     o1[:, g, 0:T8, :].rearrange("p j c -> p (j c)"), start=True, stop=True)
                for g in range(UG):
                    last = nc.tensor.matmul(p_o[:, g * P:(g + 1) * P], eye_turn[:, P:2 * P],
                                            o1[:, g, 1:NP, :].rearrange("p j c -> p (j c)"), start=True, stop=True)
                last.then_inc(products_done, 1)

        @block.vector
        def _(dve):
            step = Chain(dve, own)
            V = nc.vector

            def tt2(o, a, b, op):
                step(V.tensor_tensor(o, a, b, op))

            dve.wait_ge(loaded, 16 * LOADS)
            dve.wait_ge(lam_turned, 1)
            step(V.tensor_copy(lam[:, :, :].rearrange("p i g -> p (i g)"), p_k[:, 0:2 * GRP]))
            dve.wait_ge(c_turned, 1)
            for i in range(2):
                step(V.tensor_copy(c_cols[:, i, :], p_c[i][:, :]))
            lr, li = lam[:, 0, :], lam[:, 1, :]
            scr = [small[:, i, :] for i in range(8)]
            exp_precise(nc, step, dt[:, :], dt[:, :], scr[0], scr[1], scr[2])
            mag, sn, cs = scr[3], scr[4], scr[5]
            tt2(scr[6], lr, dt[:, :], ALU.mult)
            exp_precise(nc, step, mag, scr[6], scr[0], scr[1], scr[2])
            tt2(scr[6], li, dt[:, :], ALU.mult)
            sincos_precise(nc, step, sn, cs, scr[6], scr[0], scr[1])
            step(V.memset(pw_re[:, 0, :], 1.0))
            step(V.memset(pw_im[:, 0, :], 0.0))
            tt2(pw_re[:, 1, :], mag, cs, ALU.mult)
            tt2(pw_im[:, 1, :], mag, sn, ALU.mult)
            tt2(scr[6], mag, mag, ALU.mult)
            tt2(scr[7], scr[6], scr[6], ALU.mult)
            tt2(decay8[:, :], scr[7], scr[7], ALU.mult)
            for _ in range(3):
                tt2(scr[0], sn, sn, ALU.mult)
                step(V.scalar_tensor_tensor(out=sn, in0=sn, scalar=2.0, in1=cs, op0=ALU.mult, op1=ALU.mult))
                step(V.tensor_scalar(cs, scr[0], -2.0, 1.0, ALU.mult, ALU.add))
            tt2(scr[0], sn, sn, ALU.mult)
            tt2(scr[1], cs, cs, ALU.mult)
            tt2(scr[0], scr[0], scr[1], ALU.add)
            step(V.tensor_scalar(scr[0], scr[0], -0.5, 1.5, ALU.mult, ALU.add))
            tt2(turn8[:, 0, :], cs, scr[0], ALU.mult)
            step(V.tensor_tensor(turn8[:, 1, :], sn, scr[0], ALU.mult))
            V.engine_nop().then_inc(turn8_ready, 1)
            m = 1
            while m < T8:
                at_m = [pw[:, m:m + 1, :].broadcast_to([P, m, GRP]) for pw in (pw_re, pw_im)]
                complex_mul(V, step, pw_re[:, m + 1:2 * m + 1, :], pw_im[:, m + 1:2 * m + 1, :], *at_m,
                            pw_re[:, 1:m + 1, :], pw_im[:, 1:m + 1, :],
                            wide[:, 0, 0:m, :], wide[:, 1, 0:m, :])
                m *= 2
            step(V.tensor_scalar(scr[0], pw_re[:, 1, :], -1.0, None, ALU.add))
            ai = pw_im[:, 1, :]
            tt2(scr[1], lr, lr, ALU.mult)
            tt2(scr[2], li, li, ALU.mult)
            tt2(scr[1], scr[1], scr[2], ALU.add)
            step(V.reciprocal(scr[1], scr[1]))
            tt2(scr[2], scr[0], lr, ALU.mult)
            tt2(scr[3], ai, li, ALU.mult)
            tt2(scr[2], scr[2], scr[3], ALU.add)
            tt2(scr[2], scr[2], scr[1], ALU.mult)
            tt2(scr[3], ai, lr, ALU.mult)
            tt2(scr[4], scr[0], li, ALU.mult)
            tt2(scr[3], scr[3], scr[4], ALU.subtract)
            tt2(scr[3], scr[3], scr[1], ALU.mult)
            q_re, q_im = (scr[i].unsqueeze(2).broadcast_to([P, GRP, GC]) for i in (2, 3))
            complex_mul(V, step, bb[:, 0], bb[:, 1], q_re, q_im, b_raw[:, 0], b_raw[:, 1], tmp[:, 0], tmp[:, 1])
            top, low = slice(0, NS), slice(NS, P)
            for to, half, of, sign in ((in_re, top, pw_re, 1), (in_re, low, pw_im, 1),
                                       (in_im, top, pw_im, -1), (in_im, low, pw_re, 1),
                                       (out_re, top, pw_re, 1), (out_re, low, pw_im, -1),
                                       (out_im, top, pw_im, -1), (out_im, low, pw_re, -1)):
                step(V.tensor_scalar(to[half].rearrange("p g j -> p j g"), of[half], float(sign), None, ALU.mult))
            V.engine_nop().then_inc(c_ready, 1)
            base = step.n
            unit_steps = 4
            with dve.Fori(0, NU) as n:
                step = Chain(dve, own, n * unit_steps + base)
                dve.wait_ge(products_done, n)
                dve.wait_ge(st_o1, n * 16)

                def of_unit(ap, pattern, **kw):
                    return ap.rearrange(pattern, g=UG, **kw)[:, bass.ds(n, 1)].squeeze(1)

                def expand(to, fac_re, fac_im, ar, ai, lags):
                    for fac, a, o in ((fac_re, ar, to), (fac_im, ai, vt[:, :, 0:lags, :])):
                        f = of_unit(fac[:, :, :], "p (u g) j -> p u g j")[:, :, 0:lags]
                        step(V.tensor_tensor(o, f.unsqueeze(3).broadcast_to([P, UG, lags, GC]),
                                             of_unit(a, "p (u g) c -> p u g c").unsqueeze(2).broadcast_to([P, UG, lags, GC]),
                                             ALU.mult))
                    V.tensor_tensor(to, to, vt[:, :, 0:lags, :], ALU.add).then_inc(v_ready, 1)

                expand(v[:, :, :, :], in_re, in_im, bb[:, 0], bb[:, 1], T8)
                dve.wait_ge(v_ready, n * 2 + 1)
                cc = [c_cols[:, i, :].rearrange("p (g c) -> p g c", c=GC) for i in range(2)]
                expand(o1[:, :, :, :], out_re, out_im, *cc, NP)


def ssm(nc, scratch, decay8):
    SG = GRP // CT
    with ExitStack() as ctx:
        sb, ps, sem = alloc(nc, ctx, "ssm")
        inp = sb("inp", [P, 2, SG, NK])
        w12 = sb("w12", [P, 2, SG, 2 * P])
        o1, o2 = sb("o1", [P, 2, SG, P]), sb("o2", [P, 2, SG, P])
        kern = sb("kern", [P, 2, SG, P])
        twc, tws = sb("twc", [P, 2, SG, NK]), sb("tws", [P, 2, SG, NK])
        a, b = sb("a", [P, 2, NK]), sb("b", [P, 2, NK])
        drive = sb("drive", [P, 2, 2, NK])
        state = sb("state", [P, 2, 2, NK])
        e1, e2 = sb("e1", [P, 2, 2, NK + 1]), sb("e2", [P, 2, 2, NK + 1])
        y = sb("y", [P, 2, SG, NK])
        p_in = [ps(f"p_in{i}") for i in range(4)]
        p_y = [ps("p_y0"), ps("p_y1")]
        loaded = [sem("loaded0"), sem("loaded1")]
        cleared = sem("cleared")
        driven, a_done, b_done, d_done, scanned = (sem(n) for n in ("driven", "a_done", "b_done", "d_done", "scanned"))
        e_done, y_done, y_copied = sem("e_done"), sem("y_done"), sem("y_copied")
        y_stored = [sem("y_stored0"), sem("y_stored1")]
        block = ctx.enter_context(nc.Block())
        PR = SG // 2
        LOADS = T8 + T8 + 5

        def over_blocks(engine, body):
            with engine.Fori(0, CT // 2) as i:
                for half in range(2):
                    body(i * 2 + half, i, half)

        @block.sync
        def _(sp):
            s_v = scratch["s"].rearrange("(t g c) s k -> t s c g k", g=SG, c=GC)
            k_v = scratch["kernel"].rearrange("c (t g) m -> t c g m", g=SG)

            def load(n, half):
                for s in range(T8):
                    rows = slice((T8 - 1 - s) * GC, (T8 - s) * GC)
                    sp.dma_start(inp[rows, half], s_v[n][s]).then_inc(loaded[half], 16)
                    first = (T8 - 1 - s) * GC
                    sp.dma_start(kern[rows, half], k_v[n][:, :, first:first + P]).then_inc(loaded[half], 16)
                for to, name in ((w12, "w12"), (o1, "o1"), (o2, "o2"), (twc, "twc"), (tws, "tws")):
                    sp.dma_start(to[:, half], scratch[name].rearrange("p (t g) m -> t p g m", g=SG)[n]).then_inc(loaded[half], 16)
            load(0, 0)
            load(1, 1)
            with sp.Fori(0, CT // 2 - 1) as i:
                for half in range(2):
                    sp.wait_ge(y_done, (i * 2 + half + 1) * PR)
                    load(i * 2 + half + 2, half)

        @block.tensor
        def _(pe):
            def body(n, i, half):
                pe.wait_ge(loaded[half], (i + 1) * 16 * LOADS)
                for q in range(PR):
                    m = n * PR + q
                    bank = q % 2
                    if q >= 2:
                        pe.wait_ge(b_done, m - 1)
                    else:
                        pe.wait_ge(b_done, n * PR)
                    for g in range(2):
                        for part in range(2):
                            last = nc.tensor.matmul(p_in[2 * bank + part][:, g * NK:(g + 1) * NK],
                                                    w12[:, half, 2 * q + g, part * P:(part + 1) * P],
                                                    inp[:, half, 2 * q + g, :], start=True, stop=True)
                    last.then_inc(driven, 1)
                    if q >= 1:
                        out_of(n, half, q - 1)
                out_of(n, half, PR - 1)

            def out_of(n, half, q):
                m = n * PR + q
                bank = q % 2
                pe.wait_ge(e_done, 2 * m + 2)
                if q >= 2:
                    pe.wait_ge(y_copied, m - 1)
                else:
                    pe.wait_ge(y_copied, n * PR)
                for g in range(2):
                    o = p_y[bank][:, g * NK:(g + 1) * NK]
                    nc.tensor.matmul(o, kern[:, half, 2 * q + g, :], inp[:, half, 2 * q + g, :], start=True, stop=False)
                    nc.tensor.matmul(o, o1[:, half, 2 * q + g, :], e1[:, bank, g, 0:NK], start=False, stop=False)
                    last = nc.tensor.matmul(o, o2[:, half, 2 * q + g, :], e2[:, bank, g, 0:NK], start=False, stop=True)
                last.then_inc(y_done, 1)
            over_blocks(pe, body)

        @block.vector
        def _(dve):
            V = nc.vector
            V.memset(e1[:, :, :, 0:1], 0.0).then_inc(cleared, 1)
            V.memset(e2[:, :, :, 0:1], 0.0).then_inc(cleared, 1)

            def body(n, i, half):
                dve.wait_ge(loaded[half], (i + 1) * 16 * LOADS)
                for q in range(PR):
                    m = n * PR + q
                    bank = q % 2
                    gs = slice(2 * q, 2 * q + 2)
                    dve.wait_ge(driven, m + 1)
                    pair = lambda t: t[:, :].rearrange("p (g k) -> p g k", g=2)
                    V.tensor_tensor(a[:, :, :], pair(p_in[2 * bank]), twc[:, half, gs], ALU.mult).then_inc(a_done, 1)
                    V.tensor_tensor(b[:, :, :], pair(p_in[2 * bank + 1]), tws[:, half, gs], ALU.mult).then_inc(b_done, 1)
                    dve.wait_ge(a_done, m + 1)
                    dve.wait_ge(b_done, m + 1)
                    V.tensor_tensor(drive[:, bank], a[:, :, :], b[:, :, :], ALU.add).then_inc(d_done, 1)
                    dve.wait_ge(d_done, m + 1)
                    if q >= 2:
                        dve.wait_ge(e_done, 2 * m - 2)
                    else:
                        dve.wait_ge(e_done, n * PR * 2)
                    for g in range(2):
                        col = decay8[:, bass.ds(n * SG + (2 * q + g), 1)]
                        V.tensor_tensor_scan(state[:, bank, g], col.broadcast_to([P, NK]), drive[:, bank, g], 0.0,
                                             ALU.mult, ALU.add).then_inc(scanned, 1)
            over_blocks(dve, body)

        @block.gpsimd
        def _(pool):
            pool.wait_ge(cleared, 2)

            def body(n, i, half):
                for q in range(PR):
                    m = n * PR + q
                    bank = q % 2
                    gs = slice(2 * q, 2 * q + 2)
                    pool.wait_ge(scanned, 2 * m + 2)
                    if q >= 2:
                        pool.wait_ge(y_done, m - 1)
                    else:
                        pool.wait_ge(y_done, n * PR)
                    nc.gpsimd.tensor_tensor(e1[:, bank, :, 1:NK + 1], state[:, bank], twc[:, half, gs], ALU.mult).then_inc(e_done, 1)
                    nc.gpsimd.tensor_tensor(e2[:, bank, :, 1:NK + 1], state[:, bank], tws[:, half, gs], ALU.mult).then_inc(e_done, 1)
            over_blocks(pool, body)

        @block.scalar
        def _(act):
            y_v = scratch["y"].rearrange("(t g c) s k -> t s c g k", g=SG, c=GC)

            def body(n, i, half):
                act.wait_ge(y_stored[half], i * T8 * 16)
                for q in range(PR):
                    m = n * PR + q
                    act.wait_ge(y_done, m + 1)
                    nc.scalar.copy(y[:, half, 2 * q:2 * q + 2, :].rearrange("p g k -> p (g k)"), p_y[q % 2][:, :]).then_inc(y_copied, 1)
                act.wait_ge(y_copied, n * PR + PR)
                for s in range(T8):
                    act.dma_start(y_v[n][s], y[s * GC:(s + 1) * GC, half]).then_inc(y_stored[half], 16)
            over_blocks(act, body)
            for half in range(2):
                act.wait_ge(y_stored[half], CT // 2 * T8 * 16)


def convolution(nc, scratch, conv_w, conv_b):
    BACK = -(-(TAPS - 1) // T8)
    with ExitStack() as ctx:
        sb, ps, sem = alloc(nc, ctx, "conv")
        w_rows = sb("w_rows", [TAPS, CW])
        w = sb("w", [P, CT, TAPS])
        bias = sb("bias", [P, CT])
        u = sb("u", [P, 2, T8, BACK + NK])
        y = sb("y", [P, 2, T8, NK])
        ident = sb("ident", [TAPS, TAPS])
        w_in, b_in, cleared, w_ready = sem("w_in"), sem("b_in"), sem("cleared"), sem("w_ready")
        loaded = [sem("loaded0"), sem("loaded1")]
        own, done, stored = sem("own"), sem("done"), [sem("stored0"), sem("stored1")]
        block = ctx.enter_context(nc.Block())
        pieces = []
        for lag in range(TAPS):
            s = 0
            while s < T8:
                m, src = divmod(s - lag, T8)
                width = min(T8 - s, T8 - src)
                pieces.append((lag, s, src, m, width))
                s += width

        @block.sync
        def _(sp):
            with nc.allow_non_contiguous_dma(reason="the taps, read once"):
                for t in range(CT):
                    sp.dma_start(w[:, t], conv_w.rearrange("l (t p) -> t p l", p=P)[t]).then_inc(w_in, 16)
            load_column(nc, sp, bias[:, :], conv_b).then_inc(w_in, 16)
            u_v = scratch["u"].rearrange("(t p) s k -> t p s k", p=P)
            o_v = scratch["conv"].rearrange("(t p) s k -> t p s k", p=P)
            for t in range(2):
                sp.dma_start(u[:, t, :, BACK:], u_v[t]).then_inc(loaded[t], 16)
            for t in range(CT):
                sp.wait_ge(done, t + 1)
                sp.dma_start(o_v[t], y[:, t % 2]).then_inc(stored[t % 2], 16)
                if t + 2 < CT:
                    sp.dma_start(u[:, t % 2, :, BACK:], u_v[t + 2]).then_inc(loaded[t % 2], 16)
            for half in range(2):
                sp.wait_ge(stored[half], 16 * CT // 2)

        @block.vector
        def _(dve):
            V = nc.vector
            V.memset(u[:, :, :, 0:BACK], 0.0).then_inc(cleared, 1)
            dve.wait_ge(cleared, 1)
            dve.wait_ge(w_in, 16 * (CT + 1))
            step = Chain(dve, own)
            for t in range(CT):
                dve.wait_ge(loaded[t % 2], 16 * (t // 2 + 1))
                if t >= 2:
                    dve.wait_ge(stored[t % 2], 16 * (t // 2))
                for lag, s, src, m, width in pieces:
                    o = y[:, t % 2, s:s + width]
                    i = u[:, t % 2, src:src + width, BACK + m:BACK + m + NK]
                    tap = w[:, t, TAPS - 1 - lag:TAPS - lag]
                    if lag == 0:
                        step(V.tensor_scalar(o, i, tap, bias[:, t:t + 1], ALU.mult, ALU.add))
                    else:
                        step(V.scalar_tensor_tensor(out=o, in0=i, scalar=tap, in1=o, op0=ALU.mult, op1=ALU.add))
                V.engine_nop().then_inc(done, 1)


def wait(engine, sem, value):
    if not isinstance(value, int) or value > 0:
        engine.wait_ge(sem, value)


def mix(nc, scratch, ident, logits, x, ln_g, ln_b, ssm_d, glu_w, glu_b, g_branch, w_out, g_ffn,
        w_rg, b_rg, w_re, b_re):
    TN = NK
    GELU = 2 * math.sqrt(2 / math.pi)
    NL = NG + NE
    with ExitStack() as ctx:
        sb, ps, sem = alloc(nc, ctx, "mix")
        wo_hi, wo_lo = sb("wo_hi", [P, KD, D], FP32R), sb("wo_lo", [P, KD, D], FP32R)
        glu_hi, glu_lo = sb("glu_hi", [P, CT, SW], FP32R), sb("glu_lo", [P, CT, SW], FP32R)
        cols = sb("cols", [P, 7, CT])
        LNG, LNB, DD, GLB, GBC, GBS = range(6)
        gain = sb("gain", [P, D])
        wr, br = sb("wr", [P, KD, NL]), sb("br", [P, NL])
        ones = sb("ones", [P, 1])
        conv_in, y_in, s_in = sb("conv_in", [P, CT, TN]), sb("y_in", [P, CT, TN]), sb("s_in", [P, CT, TN])
        yn = sb("yn", [P, 2, CW])
        bn, mv = sb("bn", [P, 2, 6]), sb("mv", [P, 2, 3])
        st = sb("st", [P, 4, 4])
        rs = sb("rs", [P, 4])
        cube, sg = sb("cube", [P, CT, TN]), sb("sg", [P, CT, TN])
        yg, ys, yc = sb("yg", [P, CT, TN]), sb("ys", [P, CT, TN]), sb("yc", [P, CT, TN])
        yg_hi, yg_lo = sb("yg_hi", [P, CT, TN], FP32R), sb("yg_lo", [P, CT, TN], FP32R)
        sq = sb("sq", [P, 2, CT, TN])
        cat_hi, cat_lo = sb("cat_hi", [P, 2, KD, TN], FP32R), sb("cat_lo", [P, 2, KD, TN], FP32R)
        x_sb, x2, h = sb("x_sb", [P, 2, D]), sb("x2", [P, 2, D]), sb("h", [P, 2, D])
        raw = h
        junk, hT = sb("junk", [P, D]), sb("hT", [P, KD, P])
        zero = junk
        pa, pb, pc, pd = ps("pa"), ps("pb"), ps("pc"), ps("pd")
        p_out = [ps(f"p_out{i}") for i in range(4)]

        params, w_read = sem("params"), [sem("w_read0"), sem("w_read1")]
        w_hi_done, w_lo_done, ones_done = sem("w_hi_done"), sem("w_lo_done"), sem("ones_done")
        conv_ld, y_ld, s_ld = sem("conv_ld"), sem("y_ld"), sem("s_ld")
        x_ld = [sem("x_ld0"), sem("x_ld1")]
        own = sem("own")
        ln_tr, bn_own, yn_done, ln_back = sem("ln_tr"), sem("bn_own"), sem("yn_done"), sem("ln_back")
        v_done, cube_own, cube_done, gelu_sig, yg_done = (sem(n) for n in ("v_done", "cube_own", "cube_done", "gelu_sig", "yg_done"))
        yg_hi_done, yg_lo_done, glu_done, glu_sig, ys_done = (sem(n) for n in ("yg_hi_done", "yg_lo_done", "glu_done", "glu_sig", "ys_done"))
        yc_done, c_hi_done, c_lo_done, s_hi_done, s_lo_done = (sem(n) for n in ("yc_done", "c_hi_done", "c_lo_done", "s_hi_done", "s_lo_done"))
        sums_done, sums_read = sem("sums_done"), sem("sums_read")
        out_done, x2_own, x2_sq, h_done = (sem(n) for n in ("out_done", "x2_own", "x2_sq", "h_done"))
        h_turned, h_copied, logit_done, logit_read = (sem(n) for n in ("h_turned", "h_copied", "logit_done", "logit_read"))
        x2_st, h_st, pads = [sem("x2_st0"), sem("x2_st1")], [sem("h_st0"), sem("h_st1")], sem("pads")
        zeroed, gelu_arg, sums_own, half_a, half_b = (sem(n) for n in ("zeroed", "gelu_arg", "sums_own", "half_a", "half_b"))
        block = ctx.enter_context(nc.Block())
        CHUNKS = CT + KD
        PARAMS = 6 + 5

        def over_steps(engine, body):
            body(0, 0)
            body(1, 1)
            with engine.Fori(0, (T8 - 4) // 2) as i:
                body(i * 2 + 2, 0)
                body(i * 2 + 3, 1)
            body(T8 - 2, 0)
            body(T8 - 1, 1)
            body(T8, 0)

        def first(n):
            return isinstance(n, int) and n == 0

        def last_step(n):
            return isinstance(n, int) and n == T8

        x_rows = x.rearrange("(h k s) d -> s h k d", s=T8, h=2)
        rows = lambda name: scratch[name][0:SEQ, :].rearrange("(n t p) d -> n t p d", t=2, p=P)
        tiles = lambda name: scratch[name].rearrange("(c p) s k -> s p c k", p=P)

        @block.sync
        def _(sp):
            vectors = ((LNG, ln_g), (LNB, ln_b), (DD, ssm_d), (GLB, glu_b), (GBC, g_branch[0:CW]), (GBS, g_branch[CW:D]))
            chunks = [glu_w.rearrange("(c p) n -> c p n", p=P)[c] for c in range(CT)]
            chunks += [w_out.rearrange("(c p) n -> c p n", p=P)[c] for c in range(KD)]

            def load_front(n):
                sp.dma_start(conv_in[:, :, :], tiles("conv")[n]).then_inc(conv_ld, 16)

            def load_ssm(n):
                sp.dma_start(y_in[:, :, :], tiles("y")[n]).then_inc(y_ld, 16)
                sp.dma_start(s_in[:, :, :], tiles("s")[n]).then_inc(s_ld, 16)

            load_front(0)
            load_ssm(0)
            for to, v in vectors:
                load_column(nc, sp, cols[:, to], v).then_inc(params, 16)
            for c, chunk in enumerate(chunks):
                if c >= 2:
                    sp.wait_ge(w_lo_done, c - 1)
                sp.dma_start(raw[:, c % 2, 0:chunk.shape[1]], chunk).then_inc(w_read[c % 2], 16)
            sp.dma_start(gain[:, :], g_ffn.partition_broadcast(P)).then_inc(params, 16)
            sp.dma_start(wr[:, :, 0:NG], w_rg.rearrange("(c p) n -> p c n", p=P)).then_inc(params, 16)
            sp.dma_start(wr[:, :, NG:NL], w_re.rearrange("(c p) n -> p c n", p=P)).then_inc(params, 16)
            sp.dma_start(br[:, 0:NG], b_rg.partition_broadcast(P)).then_inc(params, 16)
            sp.dma_start(br[:, NG:NL], b_re.partition_broadcast(P)).then_inc(params, 16)
            for t in range(2):
                sp.dma_start(x_sb[:, t], x_rows[0][t]).then_inc(x_ld[t], 16)
            sp.wait_ge(zeroed, 1)
            sp.dma_start(scratch["h"][SEQ:ROWS, :], zero[:, :]).then_inc(pads, 16)
            sp.dma_start(scratch["acc"][SEQ:ROWS, :], zero[:, :]).then_inc(pads, 16)

            def body(n, par):
                if not last_step(n) and not (isinstance(n, int) and n == T8 - 1):
                    sp.wait_ge(ln_tr, n * 2 + 2)
                    load_front(n + 1)
                    sp.wait_ge(yg_done, n + 1)
                    load_ssm(n + 1)
                if not first(n):
                    for t in range(2):
                        q = n * 2 - 2 + t
                        sp.wait_ge(h_done, q + 1)
                        sp.dma_start(rows("acc")[n - 1][t], x2[:, t]).then_inc(x2_st[t], 16)
                        sp.dma_start(rows("h")[n - 1][t], h[:, t]).then_inc(h_st[t], 16)
                        if not last_step(n):
                            sp.dma_start(x_sb[:, t], x_rows[n][t]).then_inc(x_ld[t], 16)
            over_steps(sp, body)
            for t in range(2):
                sp.wait_ge(x2_st[t], 16 * T8)
                sp.wait_ge(h_st[t], 16 * T8)
            sp.wait_ge(pads, 32)

        @block.gpsimd
        def _(pool):
            nc.gpsimd.memset(ones[:, :], 1.0).then_inc(ones_done, 1)
            nc.gpsimd.memset(zero[:, :], 0.0).then_inc(zeroed, 1)
            with pool.Fori(0, T8) as n:
                pool.wait_ge(v_done, n + 1)
                nc.gpsimd.tensor_tensor(cube[:, :, :], y_in[:, :, :], y_in[:, :, :], ALU.mult).then_inc(cube_own, 1)
                pool.wait_ge(cube_own, n + 1)
                nc.gpsimd.tensor_tensor(cube[:, :, :], cube[:, :, :], y_in[:, :, :], ALU.mult).then_inc(cube_done, 1)

        @block.scalar
        def _(act):
            for c in range(CHUNKS):
                act.wait_ge(w_read[c % 2], 16 * (c // 2 + 1))
                if c < CT:
                    nc.scalar.copy(glu_hi[:, c], raw[:, c % 2, 0:SW]).then_inc(w_hi_done, 1)
                else:
                    nc.scalar.copy(wo_hi[:, c - CT], raw[:, c % 2]).then_inc(w_hi_done, 1)
            act.wait_ge(pads, 32)
            act.wait_ge(params, 16 * PARAMS)

            def front1(n):
                act.wait_ge(gelu_arg, n + 1)
                nc.scalar.activation(sg[:, :, :], cube[:, :, :], ACT.Sigmoid, scale=GELU).then_inc(gelu_sig, 1)
                act.wait_ge(yg_done, n + 1)
                nc.scalar.copy(yg_hi[:, :, :], yg[:, :, :]).then_inc(yg_hi_done, 1)

            def front2(n, par):
                wait(act, c_lo_done, n)
                for b, bank in enumerate((pb, pc)):
                    act.wait_ge(ln_back, n * 2 + b + 1)
                    for c in (2 * b, 2 * b + 1):
                        nc.scalar.activation(yc[:, c], bank[:, (c % 2) * TN:(c % 2 + 1) * TN], ACT.Silu,
                                             scale=cols[:, LNG, c:c + 1], bias=cols[:, LNB, c:c + 1]).then_inc(yc_done, 1)
                act.wait_ge(yc_done, n * CT + CT)
                nc.scalar.activation(sq[:, 0], yc[:, :, :], ACT.Square)
                for c in range(CT):
                    last = nc.scalar.activation(cat_hi[:, par, c], yc[:, c], ACT.Copy, scale=cols[:, GBC, c:c + 1])
                last.then_inc(c_hi_done, 1)
                for b, bank in enumerate((pa, pb)):
                    act.wait_ge(glu_done, n * 2 + b + 1)
                    for m in (2 * b, 2 * b + 1):
                        last = nc.scalar.activation(sg[:, m], bank[:, (m % 2) * TN:(m % 2 + 1) * TN], ACT.Sigmoid,
                                                    bias=cols[:, GLB, m:m + 1])
                    last.then_inc(glu_sig, 1)
                act.wait_ge(ys_done, n + 1)
                nc.scalar.activation(sq[:, 1], ys[:, :, :], ACT.Square)
                for c in range(CT):
                    last = nc.scalar.activation(cat_hi[:, par, CT + c], ys[:, c], ACT.Copy, scale=cols[:, GBS, c:c + 1])
                last.then_inc(s_hi_done, 1)

            def tile_square(q, t):
                act.wait_ge(half_b, q * 2 + 2)
                nc.scalar.activation(junk[:, :], x2[:, t], ACT.Square, accum_out=st[:, 3, 3:4]).then_inc(x2_sq, 1)

            def logit(q, t):
                for b, bank in enumerate((pc, pa)):
                    act.wait_ge(h_turned, q * 2 + b + 1)
                    wait(act, logit_done, q)
                    nc.scalar.copy(hT[:, 4 * b:4 * b + 4, :].rearrange("p c k -> p (c k)"), bank[:, :]).then_inc(h_copied, 1)

            def body(n, par):
                if not last_step(n):
                    front1(n)
                if not first(n):
                    tile_square(n * 2 - 2, 0)
                    if not (isinstance(n, int) and n == 1):
                        logit(n * 2 - 3, 1)
                if not last_step(n):
                    front2(n, par)
                if not first(n):
                    tile_square(n * 2 - 1, 1)
                    logit(n * 2 - 2, 0)
            over_steps(act, body)
            logit(2 * T8 - 1, 1)

        @block.vector
        def _(dve):
            V = nc.vector
            for c in range(CHUNKS):
                dve.wait_ge(w_hi_done, c + 1)
                w, hi, lo = ((raw[:, c % 2, 0:SW], glu_hi[:, c], glu_lo[:, c]) if c < CT
                             else (raw[:, c % 2], wo_hi[:, c - CT], wo_lo[:, c - CT]))
                V.tensor_tensor(lo, w, hi.bitcast(FP32), ALU.subtract).then_inc(w_lo_done, 1)
            dve.wait_ge(params, 16 * PARAMS)

            F1 = 7 + RSQRT_STEPS
            FS = RSQRT_STEPS
            FO = 1 + RSQRT_STEPS

            def front1(n):
                step = Chain(dve, bn_own, n * F1)
                dve.wait_ge(y_ld, 16 * (n + 1))
                dve.wait_ge(s_ld, 16 * (n + 1))
                for c in range(CT):
                    last = V.scalar_tensor_tensor(out=y_in[:, c], in0=s_in[:, c], scalar=cols[:, DD, c:c + 1],
                                                  in1=y_in[:, c], op0=ALU.mult, op1=ALU.add)
                last.then_inc(v_done, 1)
                dve.wait_ge(ln_tr, n * 2 + 2)
                for t, bank in enumerate((pa, pb)):
                    V.bn_stats(bn[:, t], bank[:, :]).then_inc(own, 1)
                dve.wait_ge(own, n * 2 + 2)
                me, mo, ve, vo = (bn[:, :, i] for i in (1, 4, 2, 5))
                mean, dif, var = mv[:, :, 0], mv[:, :, 1], mv[:, :, 2]
                step(V.tensor_tensor(mean, me, mo, ALU.add))
                step(V.tensor_tensor(dif, me, mo, ALU.subtract))
                step(V.tensor_tensor(var, ve, vo, ALU.add))
                step(V.tensor_scalar(mean, mean, 0.5, None, ALU.mult))
                step(V.tensor_tensor(dif, dif, dif, ALU.mult))
                step(V.scalar_tensor_tensor(out=var, in0=dif, scalar=CW / 4.0, in1=var, op0=ALU.mult, op1=ALU.add))
                a = st[:, 0, 0:2]
                step(V.tensor_scalar(a, var, 1.0 / CW, EPS, ALU.mult, ALU.add))
                rsqrt(nc, step, st[:, 1, 0:2], a, st[:, 2, 0:2], st[:, 3, 0:2])
                for t, bank in enumerate((pa, pb)):
                    last = V.tensor_scalar(yn[:, t], bank[:, :], mv[:, t, 0:1], st[:, 1, t:t + 1], ALU.subtract, ALU.mult)
                last.then_inc(yn_done, 1)
                dve.wait_ge(cube_done, n + 1)
                V.scalar_tensor_tensor(out=cube[:, :, :], in0=cube[:, :, :], scalar=0.044715, in1=y_in[:, :, :],
                                       op0=ALU.mult, op1=ALU.add).then_inc(gelu_arg, 1)
                dve.wait_ge(gelu_sig, n + 1)
                V.tensor_tensor(yg[:, :, :], y_in[:, :, :], sg[:, :, :], ALU.mult).then_inc(yg_done, 1)
                dve.wait_ge(yg_hi_done, n + 1)
                V.tensor_tensor(yg_lo[:, :, :], yg[:, :, :], yg_hi[:, :, :].bitcast(FP32), ALU.subtract).then_inc(yg_lo_done, 1)

            def front2(n, par):
                dve.wait_ge(c_hi_done, n + 1)
                for c in range(CT):
                    last = V.scalar_tensor_tensor(out=cat_lo[:, par, c], in0=yc[:, c], scalar=cols[:, GBC, c:c + 1],
                                                  in1=cat_hi[:, par, c].bitcast(FP32), op0=ALU.mult, op1=ALU.subtract)
                last.then_inc(c_lo_done, 1)
                dve.wait_ge(glu_sig, n * 2 + 2)
                V.tensor_tensor(ys[:, :, :], yg[:, :, :], sg[:, :, :], ALU.mult).then_inc(ys_done, 1)
                dve.wait_ge(s_hi_done, n + 1)
                for c in range(CT):
                    last = V.scalar_tensor_tensor(out=cat_lo[:, par, CT + c], in0=ys[:, c], scalar=cols[:, GBS, c:c + 1],
                                                  in1=cat_hi[:, par, CT + c].bitcast(FP32), op0=ALU.mult, op1=ALU.subtract)
                last.then_inc(s_lo_done, 1)

            def sums(n):
                step = Chain(dve, sums_own, n * FS)
                dve.wait_ge(sums_done, n + 1)
                V.tensor_scalar(st[:, 0, :], pd[:, 0:4], 1.0 / CW, EPS, ALU.mult, ALU.add).then_inc(sums_read, 1)
                dve.wait_ge(sums_read, n + 1)
                rsqrt(nc, step, rs[:, :], st[:, 0, :], st[:, 1, :], st[:, 2, :])

            def out_tile(q, n, t):
                step = Chain(dve, x2_own, q * FO)
                dve.wait_ge(x_ld[t], 16 * (n + 1))
                wait(dve, x2_st[t], n * 16)
                wait(dve, h_st[t], n * 16)
                for half in range(2):
                    dve.wait_ge(out_done, q * 2 + half + 1)
                    sl = slice(half * 512, (half + 1) * 512)
                    V.scalar_tensor_tensor(out=x2[:, t, sl], in0=p_out[2 * half][:, :], scalar=rs[:, 2 * t:2 * t + 1],
                                           in1=x_sb[:, t, sl], op0=ALU.mult, op1=ALU.add).then_inc(half_a, 1)
                    dve.wait_ge(half_a, q * 2 + half + 1)
                    V.scalar_tensor_tensor(out=x2[:, t, sl], in0=p_out[2 * half + 1][:, :], scalar=rs[:, 2 * t + 1:2 * t + 2],
                                           in1=x2[:, t, sl], op0=ALU.mult, op1=ALU.add).then_inc(half_b, 1)
                dve.wait_ge(x2_sq, q + 1)
                step(V.tensor_scalar(st[:, 0, 0:1], st[:, 3, 3:4], 1.0 / D, EPS, ALU.mult, ALU.add))
                rsqrt(nc, step, st[:, 1, 0:1], st[:, 0, 0:1], st[:, 2, 0:1], st[:, 2, 1:2])
                V.scalar_tensor_tensor(out=h[:, t], in0=x2[:, t], scalar=st[:, 1, 0:1], in1=gain[:, :],
                                       op0=ALU.mult, op1=ALU.mult).then_inc(h_done, 1)

            def logit(q, t):
                dve.wait_ge(logit_done, q + 1)
                V.tensor_tensor(logits[:, bass.ds(q, 1), :].squeeze(1), pd[:, 64:64 + NL], br[:, :], ALU.add).then_inc(logit_read, 1)

            def body(n, par):
                if not last_step(n):
                    front1(n)
                if not first(n):
                    sums(n - 1)
                    out_tile(n * 2 - 2, n - 1, 0)
                    if not (isinstance(n, int) and n == 1):
                        logit(n * 2 - 3, 1)
                if not last_step(n):
                    front2(n, par)
                if not first(n):
                    out_tile(n * 2 - 1, n - 1, 1)
                    logit(n * 2 - 2, 0)
            over_steps(dve, body)
            logit(2 * T8 - 1, 1)

        @block.tensor
        def _(pe):
            def ln_in(n):
                pe.wait_ge(conv_ld, 16 * (n + 1))
                wait(pe, glu_sig, n * 2)
                if not (isinstance(n, int) and n < 2):
                    pe.wait_ge(h_copied, n * 4 - 6)
                for t, bank in enumerate((pa, pb)):
                    for c in range(CT):
                        last = nc.tensor.transpose(bank[:, c * P:(c + 1) * P], conv_in[:, c, t * P:(t + 1) * P], ident[:, :])
                    last.then_inc(ln_tr, 1)

            def ln_out(n):
                pe.wait_ge(yn_done, n + 1)
                wait(pe, yc_done, n * CT)
                for b, bank in enumerate((pb, pc)):
                    for c in (2 * b, 2 * b + 1):
                        for t in range(2):
                            at = (c % 2) * TN + t * P
                            last = nc.tensor.transpose(bank[:, at:at + P], yn[:, t, c * P:(c + 1) * P], ident[:, :])
                    last.then_inc(ln_back, 1)

            def glu(n):
                pe.wait_ge(yg_lo_done, n + 1)
                for b, bank in enumerate((pa, pb)):
                    if b == 1:
                        pe.wait_ge(yc_done, n * CT + 2)
                    for m in (2 * b, 2 * b + 1):
                        o = bank[:, (m % 2) * TN:(m % 2 + 1) * TN]
                        for c in range(CT):
                            ms = slice(m * P, (m + 1) * P)
                            nc.tensor.matmul(o, glu_hi[:, c, ms], yg_hi[:, c], start=c == 0, stop=False)
                            nc.tensor.matmul(o, glu_hi[:, c, ms], yg_lo[:, c], start=False, stop=False)
                            last = nc.tensor.matmul(o, glu_lo[:, c, ms], yg_hi[:, c], start=False, stop=c == CT - 1)
                    last.then_inc(glu_done, 1)

            def sums(n):
                pe.wait_ge(s_hi_done, n + 1)
                if not first(n):
                    pe.wait_ge(logit_read, n * 2 - 1)
                for t in range(2):
                    for branch in range(2):
                        for c in range(CT):
                            last = nc.tensor.matmul(pd[:, 2 * t + branch:2 * t + branch + 1], sq[:, branch, c, t * P:(t + 1) * P],
                                                    ones[:, :], start=c == 0, stop=c == CT - 1)
                last.then_inc(sums_done, 1)

            def out_tile(q, n, t, par):
                pe.wait_ge(c_lo_done, n + 1)
                pe.wait_ge(s_lo_done, n + 1)
                for half in range(2):
                    wait(pe, half_b, q * 2 - 1 + half if not (isinstance(q, int) and q == 0) else 0)
                    sl = slice(half * 512, (half + 1) * 512)
                    for branch in range(2):
                        o = p_out[2 * half + branch]
                        for c in range(CT):
                            k = branch * CT + c
                            ts = slice(t * P, (t + 1) * P)
                            nc.tensor.matmul(o[:, :], cat_hi[:, par, k, ts], wo_hi[:, k, sl], start=c == 0, stop=False)
                            nc.tensor.matmul(o[:, :], cat_lo[:, par, k, ts], wo_hi[:, k, sl], start=False, stop=False)
                            last = nc.tensor.matmul(o[:, :], cat_hi[:, par, k, ts], wo_lo[:, k, sl], start=False, stop=c == CT - 1)
                    last.then_inc(out_done, 1)

            def logit(q, t, sums_n):
                pe.wait_ge(h_done, q + 1)
                for b, bank in enumerate((pc, pa)):
                    for c in range(4 * b, 4 * b + 4):
                        last = nc.tensor.transpose(bank[:, (c % 4) * P:(c % 4 + 1) * P], h[:, t, c * P:(c + 1) * P], ident[:, :])
                    last.then_inc(h_turned, 1)
                pe.wait_ge(h_copied, q * 2 + 2)
                pe.wait_ge(sums_read, sums_n)
                wait(pe, logit_read, q)
                for c in range(KD):
                    last = nc.tensor.matmul(pd[:, 64:64 + NL], hT[:, c], wr[:, c], start=c == 0, stop=c == KD - 1)
                last.then_inc(logit_done, 1)

            pe.wait_ge(ones_done, 1)
            pe.wait_ge(w_lo_done, CHUNKS)
            pe.wait_ge(params, 16 * PARAMS)

            def body(n, par):
                if not last_step(n):
                    ln_in(n)
                if not first(n):
                    sums(n - 1)
                    out_tile(n * 2 - 2, n - 1, 0, 1 - par)
                    if not (isinstance(n, int) and n == 1):
                        if not last_step(n):
                            pe.wait_ge(yn_done, n + 1)
                        logit(n * 2 - 3, 1, n)
                if not last_step(n):
                    ln_out(n)
                    glu(n)
                if not first(n):
                    out_tile(n * 2 - 1, n - 1, 1, 1 - par)
                    if not last_step(n):
                        pe.wait_ge(yc_done, n * CT + CT)
                        pe.wait_ge(glu_sig, n * 2 + 1)
                    logit(n * 2 - 2, 0, n)
            over_steps(pe, body)
            logit(2 * T8 - 1, 1, T8)


def route(nc, scratch, ident, logits, counts):
    MAXB = SEQ // P
    with ExitStack() as ctx:
        sb, ps, sem = alloc(nc, ctx, "route")
        before, ones = sb("before", [P, P]), sb("ones", [P, P])
        desc, thresh = sb("desc", [P, EPG]), sb("thresh", [P, MAXB])
        desc_i, thresh_i = sb("desc_i", [P, EPG], INT32), sb("thresh_i", [P, MAXB], INT32)
        blank = sb("blank", [P, TBLK, 2], INT32)
        pay, slot_i = sb("pay", [P, TT, 2, 2], INT32), sb("slot_i", [P, TT, 2], INT32)
        s1 = [sb(f"s1_{i}", [P, TT]) for i in range(12)]
        g4 = [sb(f"g4_{i}", [P, TT, NG]) for i in range(5)]
        e8 = [sb(f"e8_{i}", [P, TT, EPG]) for i in range(6)]
        pick = [sb(f"pick{k}", [P, TT, NE]) for k in range(2)]
        both, w1, w2, w3 = (sb(n, [P, TT, NE]) for n in ("both", "w1", "w2", "w3"))
        tot = sb("tot", [P, TT, NE])
        n32 = [sb(f"n32_{i}", [P, NE]) for i in range(4)]
        cmp = sb("cmp", [P, NE, MAXB])
        p_rank, p_tot = ps("p_rank"), ps("p_tot")
        cleared, built, blank_st, own = sem("cleared"), sem("built"), sem("blank_st"), sem("own")
        both_done, ranked, slots_done, scattered, iotas = (sem(n) for n in ("both_done", "ranked", "slots_done", "scattered", "iotas"))
        block = ctx.enter_context(nc.Block())

        @block.gpsimd
        def _(pool):
            G = nc.gpsimd
            G.memset(before[:, :], 1.0).then_inc(cleared, 1)
            G.memset(blank[:, :, :], 0).then_inc(cleared, 1)
            G.memset(ones[:, :], 1.0).then_inc(built, 1)
            pool.wait_ge(cleared, 2)
            G.affine_select(out=before[:, :], in_=before[:, :], compare_op=ALU.is_gt, fill=0.0, base=0,
                            pattern=[[1, P]], channel_multiplier=-1).then_inc(built, 1)
            G.iota(blank[:, :, 0:1], pattern=[[0, TBLK]], base=SEQ, channel_multiplier=1).then_inc(iotas, 1)
            G.iota(desc_i[:, :], pattern=[[-1, EPG]], base=EPG, channel_multiplier=0).then_inc(iotas, 1)
            G.iota(thresh_i[:, :], pattern=[[P, MAXB]], base=0, channel_multiplier=0).then_inc(iotas, 1)
            for k in range(2):
                G.iota(pay[:, :, k, 0:1], pattern=[[P, TT]], base=0, channel_multiplier=1).then_inc(iotas, 1)
            pool.wait_ge(iotas, 5)
            pool.dma_start(scratch["table"].rearrange("(b p) w -> p b w", p=P), blank[:, :, :]).then_inc(blank_st, 16)
            pool.wait_ge(blank_st, 16)
            pool.wait_ge(slots_done, 1)
            for i in range(TT):
                for k in range(2):
                    G.indirect_dma_start(
                        out=scratch["table"][:, :],
                        out_offset=bass.IndirectOffsetOnAxis(ap=slot_i[:, i, k:k + 1], axis=0),
                        in_=pay[:, i, k, :], in_offset=None).then_inc(scattered, 16)
            pool.wait_ge(scattered, 16 * 2 * TT)

        @block.tensor
        def _(pe):
            pe.wait_ge(built, 2)
            pe.wait_ge(both_done, 1)
            m = both[:, :, :].rearrange("p i e -> p (i e)")
            nc.tensor.matmul(p_rank[:, :], before[:, :], m, start=True, stop=True)
            nc.tensor.matmul(p_tot[:, :], ones[:, :], m, start=True, stop=True).then_inc(ranked, 1)

        @block.vector
        def _(dve):
            V = nc.vector
            step = Chain(dve, own)

            def t2(o, a, b, op):
                step(V.tensor_tensor(o, a, b, op))

            def largest(values, w, key, one, m, km):
                step(V.reduce_max(m, values, AX.X))
                t2(key, values, m.unsqueeze(2).broadcast_to([P, TT, w]), ALU.is_equal)
                t2(key, key, desc[:, 0:w].unsqueeze(1).broadcast_to([P, TT, w]), ALU.mult)
                step(V.reduce_max(km, key, AX.X))
                t2(one, key, km.unsqueeze(2).broadcast_to([P, TT, w]), ALU.is_equal)

            dve.wait_ge(iotas, 5)
            step(V.tensor_copy(desc[:, :], desc_i[:, :]))
            step(V.tensor_copy(thresh[:, :], thresh_i[:, :]))
            gl, el = logits[:, :, 0:NG], logits[:, :, NG:NG + NE]
            gmax, km, psum_, pgrp, m1, m2, ex, den, gate1, gate2 = (t[:, :] for t in s1[:10])
            key_g, one_g, dg, tg, ng = (t[:, :, :] for t in g4)
            key_e, one1, one2, e_in, e2, te = (t[:, :, :] for t in e8)
            largest(gl, NG, key_g, one_g, gmax, km)
            t2(dg, gl, gmax.unsqueeze(2).broadcast_to([P, TT, NG]), ALU.subtract)
            flat = lambda ap: ap.rearrange("p i g -> p (i g)")
            exp_precise(nc, step, flat(dg), flat(dg), flat(tg), flat(ng), flat(key_g))
            step(V.reduce_sum(psum_, dg, AX.X))
            step(V.reciprocal(pgrp, psum_))
            w4 = w1[:, :, :].rearrange("p i (g e) -> p i g e", g=NG)
            t2(w4, el.rearrange("p i (g e) -> p i g e", g=NG), one_g.unsqueeze(3).broadcast_to([P, TT, NG, EPG]), ALU.mult)
            step(V.reduce_sum(e_in, w1[:, :, :].rearrange("p i (g e) -> p i e g", g=NG), AX.X))
            largest(e_in, EPG, key_e, one1, m1, km)
            step(V.tensor_scalar(te, one1, -6e38 / 2, 3e38 / 2, ALU.mult, ALU.add))
            step(V.tensor_scalar(te, te, 2.0, None, ALU.mult))
            t2(e2, e_in, te, ALU.min)
            largest(e2, EPG, key_e, one2, m2, km)
            t2(ex, m2, m1, ALU.subtract)
            exp_precise(nc, step, ex, ex, s1[10][:, :], s1[11][:, :], km)
            step(V.tensor_scalar(den, ex, 1.0, None, ALU.add))
            step(V.reciprocal(den, den))
            t2(gate1, den, pgrp, ALU.mult)
            t2(gate2, gate1, ex, ALU.mult)
            for k, gate in enumerate((gate1, gate2)):
                step(V.tensor_copy(pay[:, :, k, 1:2].bitcast(FP32).squeeze(2), gate))
            for k, one in enumerate((one1, one2)):
                t2(pick[k][:, :, :].rearrange("p i (g e) -> p i g e", g=NG),
                   one_g.unsqueeze(3).broadcast_to([P, TT, NG, EPG]),
                   one.unsqueeze(2).broadcast_to([P, TT, NG, EPG]), ALU.mult)
            step(V.tensor_tensor(both[:, :, :], pick[0][:, :, :], pick[1][:, :, :], ALU.add))
            dve.sem_inc(both_done, 1)
            dve.wait_ge(ranked, 1)
            step(V.tensor_copy(tot[:, :, :].rearrange("p i e -> p (i e)"), p_tot[:, :]))
            a, b = tot[:, :, :], w1[:, :, :]
            spare = w2[:, :, :]
            d = 1
            while d < TT:
                step(V.tensor_copy(b[:, 0:d], a[:, 0:d]))
                t2(b[:, d:], a[:, d:], a[:, 0:TT - d], ALU.add)
                a, b, spare = b, (spare if d == 1 else a), spare
                d *= 2
            upto = a
            t2(w3[:, :, :], upto, tot[:, :, :], ALU.subtract)
            n, c1, c2, n2 = (t[:, :] for t in n32)
            t2(cmp[:, :, :], upto[:, TT - 1, :].unsqueeze(2).broadcast_to([P, NE, MAXB]),
               thresh[:, :].unsqueeze(1).broadcast_to([P, NE, MAXB]), ALU.is_gt)
            step(V.reduce_sum(n, cmp[:, :, :], AX.X))
            step(V.tensor_scalar(n, n, 1.0, None, ALU.max))
            step(V.tensor_copy(c1, n))
            d = 1
            while d < NE:
                step(V.tensor_copy(c2[:, 0:d], c1[:, 0:d]))
                t2(c2[:, d:], c1[:, d:], c1[:, 0:NE - d], ALU.add)
                c1, c2 = c2, c1
                d *= 2
            t2(c2, c1, n, ALU.subtract)
            step(V.tensor_copy(counts[:, 0, :], n))
            step(V.tensor_copy(counts[:, 1, :], c2))
            step(V.tensor_copy(n2, n))
            step(V.tensor_scalar(n2[:, NE - 1:NE], n[:, NE - 1:NE], float(2 * NBLK), None, ALU.add))
            step(V.tensor_copy(counts[:, 2, :], n2))
            t2(w3[:, :, :], w3[:, :, :], p_rank[:, :].rearrange("p (i e) -> p i e", i=TT), ALU.add)
            step(V.tensor_scalar(c2, c2, float(P), None, ALU.mult))
            t2(w3[:, :, :], w3[:, :, :], c2.unsqueeze(1).broadcast_to([P, TT, NE]), ALU.add)
            for k in range(2):
                t2(pick[k][:, :, :], pick[k][:, :, :], w3[:, :, :], ALU.mult)
                step(V.reduce_sum(m1, pick[k][:, :, :], AX.X))
                step(V.tensor_copy(slot_i[:, :, k:k + 1].squeeze(2), m1))
            dve.sem_inc(slots_done, 1)


def experts(nc, scratch, ident, counts, w_gate, w_up, w_down):
    HALVES = 2
    with ExitStack() as ctx:
        sb, ps, sem = alloc(nc, ctx, "moe")
        raw = [sb(f"raw{u}", [P, 8, 512]) for u in range(3)]
        hi = [sb(f"hi{u}", [P, 8, 512], FP32R) for u in range(3)]
        lo = [sb(f"lo{u}", [P, 8, 512], FP32R) for u in range(3)]
        ids_g, ids_s = sb("ids_g", [P, 2], INT32), sb("ids_s", [P, 2], INT32)
        xg = sb("xg", [P, D])
        xh, xl = sb("xh", [P, KD, P], FP32R), sb("xl", [P, KD, P], FP32R)
        sil, hid = sb("sil", [P, F]), sb("hid", [P, F])
        hh, hl = sb("hh", [P, F // P, P], FP32R), sb("hl", [P, F // P, P], FP32R)
        y = sb("y", [P, D])
        p_gate, p_up, p_hid = ps("p_gate"), ps("p_up"), ps("p_hid")
        p_x = [ps("p_x0"), ps("p_x1")]
        p_y = [ps("p_y0"), ps("p_y1")]

        raw_in = [sem(f"raw_in{u}") for u in range(3)]
        w_hi = [sem(f"w_hi{u}") for u in range(3)]
        w_lo = [sem(f"w_lo{u}") for u in range(3)]
        ids_g_in, ids_s_in, x_in, scattered = sem("ids_g_in"), sem("ids_s_in"), sem("x_in"), sem("scattered")
        gathers, scatters = sem("gathers"), sem("scatters")
        x_turned, x_hi, x_lo = sem("x_turned"), sem("x_hi"), sem("x_lo")
        gate_done, up_done, sil_done, hid_done = (sem(n) for n in ("gate_done", "up_done", "sil_done", "hid_done"))
        hid_turned, hid_hi, hid_lo, down_done, y_done = (sem(n) for n in ("hid_turned", "hid_hi", "hid_lo", "down_done", "y_done"))
        block = ctx.enter_context(nc.Block())
        views = [w_gate.rearrange("e (c p) f -> e p c f", p=P), w_up.rearrange("e (c p) f -> e p c f", p=P),
                 w_down.rearrange("e (c p) (h f) -> e p h c f", p=P, h=2)]

        def over_blocks(engine, body, before=None, flags=False):
            with engine.Fori(0, NE) as e:
                n = engine.value_load(counts[0:1, 0, bass.ds(e, 1)], min_val=1, max_val=SEQ // P)
                start = engine.value_load(counts[0:1, 1, bass.ds(e, 1)], min_val=0, max_val=NBLK)
                last = engine.value_load(counts[0:1, 2, bass.ds(e, 1)], min_val=1, max_val=3 * NBLK) if flags else None
                with engine.Fori(0, n) as j:
                    body(start + j, e, j, last)

        @block.sync
        def _(sp):
            def load(e, u):
                for h in range(HALVES):
                    if u < 2:
                        sp.dma_start(raw[u][:, 4 * h:4 * h + 4], views[u][e][:, 4 * h:4 * h + 4]).then_inc(raw_in[u], 16)
                    else:
                        sp.dma_start(raw[u][:, 4 * h:4 * h + 4], views[u][e][:, h]).then_inc(raw_in[u], 16)
            for u in range(3):
                load(0, u)
            with sp.Fori(0, NE - 1) as e:
                for u in range(3):
                    sp.wait_ge(w_lo[u], (e + 1) * HALVES)
                    load(e + 1, u)

        @block.gpsimd
        def _(pool):
            table = scratch["table"].rearrange("(b p) w -> b p w", p=P)

            def gather(b):
                pool.dma_start(ids_g[:, :], table[b]).then_inc(ids_g_in, 16)
                pool.wait_ge(ids_g_in, b * 16 + 16)
                pool.sem_inc(gathers, 1)
                nc.gpsimd.indirect_dma_start(out=xg[:, :], out_offset=None, in_=scratch["h"][:, :],
                                             in_offset=bass.IndirectOffsetOnAxis(ap=ids_g[:, 0:1], axis=0)).then_inc(x_in, 16)

            gather(0)
            pool.wait_ge(x_in, 16)

            def body(b, e, j, last):
                pool.dma_start(ids_s[:, :], table[b]).then_inc(ids_s_in, 16)
                pool.wait_ge(x_turned, b * 2 + 2)
                gather(b + 1)
                pool.wait_ge(ids_s_in, b * 16 + 16)
                pool.wait_ge(y_done, b * 2 + 2)
                pool.sem_inc(scatters, 1)
                nc.gpsimd.indirect_dma_start(out=scratch["acc"][:, :],
                                             out_offset=bass.IndirectOffsetOnAxis(ap=ids_s[:, 0:1], axis=0),
                                             in_=y[:, :], in_offset=None, compute_op=ALU.add).then_inc(scattered, 16)
                pool.wait_ge(scattered, b * 16 + 16)
            over_blocks(pool, body)

        @block.scalar
        def _(act):
            def split_hi(e, u):
                for h in range(HALVES):
                    act.wait_ge(raw_in[u], e * 32 + 32)
                    nc.scalar.copy(hi[u][:, 4 * h:4 * h + 4], raw[u][:, 4 * h:4 * h + 4]).then_inc(w_hi[u], 1)

            def turn_x(b):
                for i in range(2):
                    act.wait_ge(x_turned, b * 2 + i + 1)
                    nc.scalar.copy(xh[:, 4 * i:4 * i + 4, :].rearrange("p c t -> p (c t)"), p_x[i][:, :]).then_inc(x_hi, 1)

            split_hi(0, 0)
            turn_x(0)
            for u in (1, 2):
                split_hi(0, u)

            def body(b, e, j, last):
                act.wait_ge(gate_done, b + 1)
                nc.scalar.activation(sil[:, :], p_gate[:, :], ACT.Silu).then_inc(sil_done, 1)
                with act.If(j == last - 1):
                    split_hi(e + 1, 0)
                with act.Else():
                    pass
                act.wait_ge(hid_turned, b + 1)
                nc.scalar.copy(hh[:, :, :].rearrange("p c t -> p (c t)"), p_hid[:, :]).then_inc(hid_hi, 1)
                turn_x(b + 1)
                with act.If(j == last - 1):
                    split_hi(e + 1, 1)
                with act.Else():
                    pass
                act.wait_ge(ids_s_in, b * 16 + 16)
                wait(act, scattered, b * 16)
                for i in range(2):
                    act.wait_ge(down_done, b * 2 + i + 1)
                    nc.scalar.activation(y[:, i * 512:(i + 1) * 512], p_y[i][:, :], ACT.Copy,
                                         scale=ids_s[:, 1:2].bitcast(FP32)).then_inc(y_done, 1)
                with act.If(j == last - 1):
                    split_hi(e + 1, 2)
                with act.Else():
                    pass
            over_blocks(act, body, flags=True)

        @block.vector
        def _(dve):
            V = nc.vector

            def split_lo(e, u):
                for h in range(HALVES):
                    dve.wait_ge(w_hi[u], e * HALVES + h + 1)
                    V.tensor_tensor(lo[u][:, 4 * h:4 * h + 4], raw[u][:, 4 * h:4 * h + 4],
                                    hi[u][:, 4 * h:4 * h + 4].bitcast(FP32), ALU.subtract).then_inc(w_lo[u], 1)

            def turn_x(b):
                for i in range(2):
                    dve.wait_ge(x_hi, b * 2 + i + 1)
                    V.tensor_tensor(xl[:, 4 * i:4 * i + 4, :].rearrange("p c t -> p (c t)"), p_x[i][:, :],
                                    xh[:, 4 * i:4 * i + 4, :].rearrange("p c t -> p (c t)").bitcast(FP32), ALU.subtract).then_inc(x_lo, 1)

            split_lo(0, 0)
            turn_x(0)
            for u in (1, 2):
                split_lo(0, u)

            def body(b, e, j, last):
                with dve.If(j == last - 1):
                    split_lo(e + 1, 0)
                with dve.Else():
                    pass
                dve.wait_ge(sil_done, b + 1)
                dve.wait_ge(up_done, b + 1)
                V.tensor_tensor(hid[:, :], p_up[:, :], sil[:, :], ALU.mult).then_inc(hid_done, 1)
                dve.wait_ge(hid_hi, b + 1)
                V.tensor_tensor(hl[:, :, :].rearrange("p c t -> p (c t)"), p_hid[:, :],
                                hh[:, :, :].rearrange("p c t -> p (c t)").bitcast(FP32), ALU.subtract).then_inc(hid_lo, 1)
                turn_x(b + 1)
                with dve.If(j == last - 1):
                    split_lo(e + 1, 1)
                    split_lo(e + 1, 2)
                with dve.Else():
                    pass
            over_blocks(dve, body, flags=True)

        @block.tensor
        def _(pe):
            def turn_x(b):
                pe.wait_ge(x_in, b * 16 + 16)
                for i in range(2):
                    for c in range(4):
                        last = nc.tensor.transpose(p_x[i][:, c * P:(c + 1) * P], xg[:, (4 * i + c) * P:(4 * i + c + 1) * P], ident[:, :])
                    last.then_inc(x_turned, 1)

            def product(out, e, u, a_hi, a_lo, chunk, kc, last):
                nc.tensor.matmul(out[:, :], a_hi, hi[u][:, chunk], start=kc == 0, stop=False)
                nc.tensor.matmul(out[:, :], a_lo, hi[u][:, chunk], start=False, stop=False)
                return nc.tensor.matmul(out[:, :], a_hi, lo[u][:, chunk], start=False, stop=last)

            turn_x(0)

            def body(b, e, j, last):
                pe.wait_ge(x_lo, b * 2 + 2)
                for u, bank, done in ((0, p_gate, gate_done), (1, p_up, up_done)):
                    if u == 0:
                        wait(pe, hid_done, b)
                    for c in range(KD):
                        if c % 4 == 0:
                            pe.wait_ge(w_lo[u], e * HALVES + c // 4 + 1)
                        last_mm = product(bank, e, u, xh[:, c], xl[:, c], c, c, c == KD - 1)
                    last_mm.then_inc(done, 1)
                turn_x(b + 1)
                pe.wait_ge(hid_done, b + 1)
                for c in range(F // P):
                    last_mm = nc.tensor.transpose(p_hid[:, c * P:(c + 1) * P], hid[:, c * P:(c + 1) * P], ident[:, :])
                last_mm.then_inc(hid_turned, 1)
                pe.wait_ge(hid_lo, b + 1)
                wait(pe, y_done, b * 2)
                for i in range(2):
                    pe.wait_ge(w_lo[2], e * HALVES + i + 1)
                    for c in range(F // P):
                        last_mm = product(p_y[i], e, 2, hh[:, c], hl[:, c], 4 * i + c, c, c == F // P - 1)
                    last_mm.then_inc(down_done, 1)
            over_blocks(pe, body)


def final_norm(nc, scratch, g_final, out):
    with ExitStack() as ctx:
        sb, _, sem = alloc(nc, ctx, "final")
        NB = 4
        x, o = sb("x", [P, NB, D]), sb("o", [P, NB, D])
        gain, junk, st = sb("gain", [P, D]), sb("junk", [P, D]), sb("st", [P, NB, 4])
        gain_in, squared, own, made = sem("gain_in"), sem("squared"), sem("own"), sem("made")
        x_in, stored = [sem(f"x_in{i}") for i in range(NB)], [sem(f"stored{i}") for i in range(NB)]
        block = ctx.enter_context(nc.Block())
        rows = scratch["acc"][0:SEQ, :].rearrange("(n i p) d -> i n p d", i=NB, p=P)
        outs = out.rearrange("(h k s) d -> s h k d", s=T8, h=2)
        NI = TT // NB

        @block.sync
        def _(sp):
            for i in range(NB):
                sp.dma_start(x[:, i], rows[i][0]).then_inc(x_in[i], 16)
            sp.dma_start(gain[:, :], g_final.partition_broadcast(P)).then_inc(gain_in, 16)
            with sp.Fori(0, NI - 1) as n:
                for i in range(NB):
                    sp.wait_ge(made, n * NB + i + 1)
                    sp.dma_start(outs[n * 2 + i // 2][i % 2], o[:, i]).then_inc(stored[i], 16)
                    sp.dma_start(x[:, i], rows[i][n + 1]).then_inc(x_in[i], 16)
            for i in range(NB):
                sp.wait_ge(made, (NI - 1) * NB + i + 1)
                sp.dma_start(outs[(NI - 1) * 2 + i // 2][i % 2], o[:, i]).then_inc(stored[i], 16)
            for i in range(NB):
                sp.wait_ge(stored[i], 16 * NI)

        @block.scalar
        def _(act):
            with act.Fori(0, NI) as n:
                for i in range(NB):
                    act.wait_ge(x_in[i], n * 16 + 16)
                    nc.scalar.activation(junk[:, :], x[:, i], ACT.Square, accum_out=st[:, i, 0:1]).then_inc(squared, 1)
                    act.wait_ge(squared, n * NB + (i + 1))

        @block.vector
        def _(dve):
            dve.wait_ge(gain_in, 16)
            with dve.Fori(0, NI) as n:
                for i in range(NB):
                    t = n * NB + i
                    step = Chain(dve, own, t * (1 + RSQRT_STEPS))
                    dve.wait_ge(squared, t + 1)
                    step(nc.vector.tensor_scalar(st[:, i, 1:2], st[:, i, 0:1], 1.0 / D, EPS, ALU.mult, ALU.add))
                    rsqrt(nc, step, st[:, i, 0:1], st[:, i, 1:2], st[:, i, 2:3], st[:, i, 3:4])
                    wait(dve, stored[i], n * 16)
                    nc.vector.scalar_tensor_tensor(out=o[:, i], in0=x[:, i], scalar=st[:, i, 0:1], in1=gain[:, :],
                                                   op0=ALU.mult, op1=ALU.mult).then_inc(made, 1)


_INS = ["x", "g_mix", "w_in", "conv_w", "conv_b", "conv_ln_g", "conv_ln_b", "ssm_lam_re", "ssm_lam_im",
        "ssm_log_dt", "ssm_b_re", "ssm_b_im", "ssm_c_re", "ssm_c_im", "ssm_d", "ssm_glu_w", "ssm_glu_b",
        "g_branch", "w_out", "g_ffn", "w_router_group", "b_router_group", "w_router_expert",
        "b_router_expert", "w_gate", "w_up", "w_down", "g_final"]


def kernel(**inputs):
    import numpy as _np
    import concourse.bacc as _bacc
    from concourse import mybir as _mybir
    from concourse.bass_utils import run_bass_kernel_spmd as _run

    nc = _bacc.Bacc("TRN2", target_bir_lowering=False, num_devices=1)
    arrays, args = {}, []
    for name in _INS:
        a = _np.ascontiguousarray(inputs[name])
        arrays[f"in_{name}"] = a
        ap = nc.dram_tensor(f"in_{name}", a.shape, _mybir.dt.from_np(a.dtype), kind="ExternalInput").ap()
        args.append(ap if name == "g_final" else ap[0])
    out = nc.dram_tensor("out", (1, SEQ, D), FP32, kind="ExternalOutput").ap()
    hybrid_encoder(nc, *args, out[0])
    r = _run(nc, [arrays], core_ids=[0])
    return r.results[0]["out"]
```

```python
import math
from contextlib import ExitStack

import concourse.bass as bass
from concourse import mybir

FP32 = mybir.dt.float32
FP32R = mybir.dt.float32r
INT32 = mybir.dt.int32
ALU = mybir.AluOpType
ACT = mybir.ActivationFunctionType
AX = mybir.AxisListType

P = 128
EPS = 1e-6
SEQ, D = 2048, 1024
CW = SW = 512
TAPS = 31
GRP, GC, NS = 32, 16, 64
NG, EPG, F = 4, 8, 512
NE = NG * EPG
T8 = 8
NK = SEQ // T8
KD = D // P
CT = CW // P
TT = SEQ // P
NBLK = SEQ * 2 // P + NE
TBLK = NBLK + SEQ // P + 2
ROWS = SEQ + P
TB = 32
UG = 4
NU = GRP // UG
LAGS = 2 * T8 - 1


class Chain:

    def __init__(self, engine, sem, base=0):
        self.engine, self.sem, self.base, self.n = engine, sem, base, 0

    def __call__(self, instruction):
        self.n += 1
        instruction.then_inc(self.sem, 1)
        self.engine.wait_ge(self.sem, self.base + self.n)


def bc(ap, axis, n):
    v = ap.unsqueeze(axis)
    shape = list(v.shape)
    shape[axis] = n
    return v.broadcast_to(shape)


RSQRT_STEPS = 12


def rsqrt(nc, step, y, a, t, u):
    yi, ai = y.bitcast(INT32), a.bitcast(INT32)
    step(nc.vector.tensor_scalar(yi, ai, 1, None, ALU.logical_shift_right))
    step(nc.vector.tensor_scalar(yi, yi, -1.0, float(0x5F3759DF), ALU.mult, ALU.add))
    step(nc.vector.tensor_scalar(a, a, -0.5, None, ALU.mult))
    for _ in range(3):
        step(nc.vector.tensor_tensor(t, y, y, ALU.mult))
        step(nc.vector.tensor_tensor(u, t, a, ALU.mult))
        step(nc.vector.scalar_tensor_tensor(out=y, in0=u, scalar=1.5, in1=y, op0=ALU.add, op1=ALU.mult))


MAGIC = 1.5 * 2.0 ** 23


def exp_precise(nc, step, y, x, t, n, q):
    ln2_hi, ln2_lo = 0.693359375, -2.12194440e-4
    step(nc.vector.tensor_scalar(x, x, 88.0, -88.0, ALU.min, ALU.max))
    step(nc.vector.tensor_scalar(n, x, 1.0 / math.log(2.0), MAGIC, ALU.mult, ALU.add))
    step(nc.vector.tensor_scalar(n, n, -MAGIC, None, ALU.add))
    step(nc.vector.scalar_tensor_tensor(out=t, in0=n, scalar=-ln2_hi, in1=x, op0=ALU.mult, op1=ALU.add))
    step(nc.vector.scalar_tensor_tensor(out=t, in0=n, scalar=-ln2_lo, in1=t, op0=ALU.mult, op1=ALU.add))
    step(nc.vector.tensor_scalar(q, t, 1.0 / math.factorial(8), None, ALU.mult))
    for d in range(7, 0, -1):
        step(nc.vector.scalar_tensor_tensor(out=q, in0=q, scalar=1.0 / math.factorial(d), in1=t,
                                            op0=ALU.add, op1=ALU.mult))
    step(nc.vector.tensor_scalar(n.bitcast(INT32), n, 127.0, 2.0 ** 23, ALU.add, ALU.mult))
    step(nc.vector.scalar_tensor_tensor(out=y, in0=q, scalar=1.0, in1=n, op0=ALU.add, op1=ALU.mult))


def sincos_precise(nc, step, s, c, x, n, t):
    two_pi = 2 * math.pi
    p1 = 6.28125
    p2 = float(int((two_pi - p1) * 2 ** 22)) / 2 ** 22
    p3 = two_pi - p1 - p2
    step(nc.vector.tensor_scalar(n, x, 1.0 / two_pi, MAGIC, ALU.mult, ALU.add))
    step(nc.vector.tensor_scalar(n, n, -MAGIC, None, ALU.add))
    for p in (p1, p2, p3):
        step(nc.vector.scalar_tensor_tensor(out=x, in0=n, scalar=-p, in1=x, op0=ALU.mult, op1=ALU.add))
    step(nc.vector.tensor_scalar(x, x, 3.2, -3.2, ALU.min, ALU.max))
    step(nc.vector.tensor_scalar(x, x, 0.25, None, ALU.mult))
    step(nc.vector.tensor_tensor(t, x, x, ALU.mult))
    for out, first in ((s, 11), (c, 12)):
        terms = list(range(first, 1, -2))
        step(nc.vector.tensor_scalar(out, t, (-1) ** (first // 2) / math.factorial(first), None, ALU.mult))
        for d in terms[1:]:
            step(nc.vector.scalar_tensor_tensor(out=out, in0=out, scalar=(-1) ** (d // 2) / math.factorial(d),
                                                in1=t, op0=ALU.add, op1=ALU.mult))
    step(nc.vector.scalar_tensor_tensor(out=s, in0=s, scalar=1.0, in1=x, op0=ALU.add, op1=ALU.mult))
    step(nc.vector.tensor_scalar(c, c, 1.0, None, ALU.add))
    for _ in range(2):
        step(nc.vector.tensor_tensor(t, s, s, ALU.mult))
        step(nc.vector.scalar_tensor_tensor(out=s, in0=s, scalar=2.0, in1=c, op0=ALU.mult, op1=ALU.mult))
        step(nc.vector.tensor_scalar(c, t, -2.0, 1.0, ALU.mult, ALU.add))


def complex_mul(engine, step, outr, outi, ar, ai, br, bi, t, u):
    step(engine.tensor_tensor(t, ar, br, ALU.mult))
    step(engine.tensor_tensor(u, ai, bi, ALU.mult))
    step(engine.tensor_tensor(outr, t, u, ALU.subtract))
    step(engine.tensor_tensor(t, ar, bi, ALU.mult))
    step(engine.tensor_tensor(u, ai, br, ALU.mult))
    step(engine.tensor_tensor(outi, t, u, ALU.add))


def hybrid_encoder(nc, x, g_mix, w_in, conv_w, conv_b, conv_ln_g, conv_ln_b, lam_re, lam_im, log_dt,
                   b_re, b_im, c_re, c_im, ssm_d, glu_w, glu_b, g_branch, w_out, g_ffn, w_rg, b_rg,
                   w_re, b_re_router, w_gate, w_up, w_down, g_final, out):
    def dram(name, shape, dt=FP32):
        return nc.dram_tensor(name, shape, dt).ap()

    scratch = dict(
        s=dram("ssm_input", [SW, T8, NK]),
        u=dram("conv_input", [CW, T8, NK]),
        conv=dram("conv_output", [CW, T8, NK]),
        toeplitz=dram("toeplitz", [CT, TB, 4, 32, 2 * TB]),
        y=dram("ssm_output", [SW, T8, NK]),
        w12=dram("state_in_weights", [P, GRP, 2 * P]),
        o1=dram("state_out_weights_1", [P, GRP, T8 * GC]),
        o2=dram("state_out_weights_2", [P, GRP, T8 * GC]),
        kernel=dram("chunk_kernels", [GC, GRP, LAGS * GC]),
        twc=dram("turn_cos", [P, GRP, NK]),
        tws=dram("turn_sin", [P, GRP, NK]),
        h=dram("ffn_input", [ROWS, D]),
        acc=dram("residual", [ROWS, D]),
        table=dram("slot_table", [TBLK * P, 2], INT32),
    )
    with ExitStack() as ctx:
        ident = ctx.enter_context(nc.sbuf_tensor("ident", [P, P], FP32))
        logits = ctx.enter_context(nc.sbuf_tensor("logits", [P, TT, NG + NE], FP32))
        counts = ctx.enter_context(nc.sbuf_tensor("counts", [P, 3, NE], INT32))
        decay8 = ctx.enter_context(nc.sbuf_tensor("decay8", [P, GRP], FP32))
        tables_st = ctx.enter_context(nc.semaphore("tables_st"))
        with ExitStack() as tables:
            keep = lambda name, shape: tables.enter_context(nc.sbuf_tensor(name, shape, FP32))
            eye_turn = keep("eye_turn", [P, 2 * P])
            lagged = keep("lagged", [P, CT, 3 * TB])
            lam = keep("lam", [P, 2, GRP])
            pw_re, pw_im = keep("pw_re", [P, T8 + 1, GRP]), keep("pw_im", [P, T8 + 1, GRP])
            with ExitStack() as early:
                early_sem = semaphores_cleared_after(nc, early)
                constants(nc, early_sem, ident, eye_turn)
                projection(nc, early_sem, scratch, x, g_mix, w_in, ident, conv_w, lagged, tables_st,
                           lam_re, lam_im, log_dt, lam, pw_re, pw_im, decay8)
            convolution_and_tables(nc, scratch, conv_b, tables_st, ident, eye_turn, lam, pw_re, pw_im,
                                   b_re, b_im, c_re, c_im)
        with ExitStack() as mixing:
            sb, _, _ = alloc(nc, mixing, "weights")
            weights = dict(wo_hi=sb("wo_hi", [P, KD, D], FP32R), wo_lo=sb("wo_lo", [P, KD, D], FP32R),
                           glu_hi=sb("glu_hi", [P, CT, SW], FP32R), glu_lo=sb("glu_lo", [P, CT, SW], FP32R))
            ssm(nc, scratch, decay8, weights, w_out, glu_w)
            mix(nc, scratch, ident, logits, weights, x, conv_ln_g, conv_ln_b, ssm_d, glu_b, g_branch,
                g_ffn, w_rg, b_rg, w_re, b_re_router)
        with ExitStack() as moe:
            weights = ExpertWeights(nc, moe, w_gate, w_up, w_down)
            route(nc, scratch, ident, logits, counts, weights)
            experts(nc, scratch, ident, counts, weights)
        final_norm(nc, scratch, g_final, out)


def load_column(nc, engine, to, vector):
    with nc.allow_non_contiguous_dma(reason="a short vector, read once"):
        return engine.dma_start(to, vector.rearrange("(c p) -> p c", p=P))


def alloc(nc, ctx, prefix):
    def sb(name, shape, dt=FP32):
        return ctx.enter_context(nc.sbuf_tensor(f"{prefix}_{name}", shape, dt))

    def ps(name, shape=(P, 512)):
        return ctx.enter_context(nc.psum_tensor(f"{prefix}_{name}", list(shape), FP32))

    def sem(name):
        return ctx.enter_context(nc.semaphore(f"{prefix}_{name}"))

    return sb, ps, sem


def semaphores_cleared_after(nc, ctx):
    taken = []

    def give_back():
        nc.all_engine_barrier()
        nc.clear_and_free_semaphores(taken)
        nc.all_engine_barrier()

    ctx.callback(give_back)

    def sem(name):
        taken.append(nc.alloc_semaphore(name=name))
        return taken[-1]

    return sem


def constants(nc, sem, ident, eye_turn):
    with ExitStack() as ctx:
        cleared, built = sem("const_cleared"), sem("const_built")
        block = ctx.enter_context(nc.Block())

        @block.gpsimd
        def _(pool):
            nc.gpsimd.memset(ident[:, :], 0.0).then_inc(cleared, 1)
            nc.gpsimd.memset(eye_turn[:, :], 0.0).then_inc(cleared, 1)
            pool.wait_ge(cleared, 2)
            step = Chain(pool, built)

            def diagonal(ap, base, fill):
                step(nc.gpsimd.affine_select(out=ap, in_=ap, compare_op=ALU.not_equal, fill=fill, base=-base,
                                             pattern=[[-1, ap.shape[1]]], channel_multiplier=1))

            diagonal(ident[:, :], 0, 1.0)
            diagonal(eye_turn[:, 0:P], 0, 1.0)
            diagonal(eye_turn[:, P:2 * P], NS, 1.0)
            diagonal(eye_turn[:, P:2 * P], -NS, -1.0)


def projection(nc, sem, scratch, x, g_mix, w_in, ident, conv_w, lagged, tables_st,
               lam_re, lam_im, log_dt, lam, pw_re, pw_im, decay8):
    RAW = 4
    NZ = 3 * CW
    x_rows = x.rearrange("(h k s) d -> s k h d", s=T8, h=2)
    w_rows = w_in.rearrange("(c p) n -> c p n", p=P)
    with ExitStack() as ctx:
        sb, ps, _ = alloc(nc, ctx, "proj")
        w_raw = sb("w_raw", [P, RAW, NZ])
        w_hi, w_lo = sb("w_hi", [P, KD, NZ], FP32R), sb("w_lo", [P, KD, NZ], FP32R)
        h_hi, h_lo = sb("h_hi", [P, 2, KD, NK], FP32R), sb("h_lo", [P, 2, KD, NK], FP32R)
        x_sb = sb("x_sb", [P, 2, 2, D])
        junk = sb("junk", [P, D])
        gain = sb("gain", [P, KD])
        stat = sb("stat", [P, 4, 2])
        sig = sb("sig", [P, 2, NK])
        s_out, u_out = sb("s_out", [P, CT, NK]), sb("u_out", [P, CT, NK])
        p_tr = [ps("p_tr0"), ps("p_tr1")]
        p_z = [ps(f"p_z{i}") for i in range(6)]

        taps, rev = sb("taps", [TAPS, CW]), sb("rev", [TAPS, TAPS])
        lam_rows, dt = sb("lam_rows", [GRP, 2, P]), sb("dt", [P, GRP])
        small, turn8 = sb("small", [P, 8, GRP]), sb("turn8", [P, 2, GRP])
        turn, tt = sb("turn", [P, 2, UG, NK]), sb("tt", [P, 2, UG, NK // 2])
        cleared, rev_done, params_in, taps_turned, taps_laid = (
            sem(n) for n in ("cleared", "rev_done", "params_in", "taps_turned", "taps_laid"))
        lam_turned, lam_read, base_own, turn8_ready, turns_own, turns_st = (
            sem(n) for n in ("lam_turned", "lam_read", "base_own", "turn8_ready", "turns_own", "turns_st"))
        turns_begun = sem("turns_begun")

        w_read = [sem(f"w_read{i}") for i in range(RAW)]
        w_hi_done, w_lo_done = sem("w_hi_done"), sem("w_lo_done")
        gain_in, x_in = sem("gain_in"), [sem("x_in0"), sem("x_in1")]
        squared, own, scaled = sem("squared"), sem("own"), sem("scaled")
        turned, hi_done, lo_done = sem("turned"), sem("hi_done"), sem("lo_done")
        z_done, z_free_s, sig_done, u_done = sem("z_done"), sem("z_free_s"), sem("sig_done"), sem("u_done")
        s_stored, u_stored = sem("s_stored"), sem("u_stored")
        block = ctx.enter_context(nc.Block())
        PAIRS = T8 // 2

        def over_tiles(engine, body):
            with engine.Fori(0, PAIRS - 1) as i:
                body(i * 2, 0, True)
                body(i * 2 + 1, 1, True)
            body(T8 - 2, 0, True)
            body(T8 - 1, 1, False)

        @block.sync
        def _(sp):
            load_column(nc, sp, gain[:, :], g_mix).then_inc(gain_in, 16)
            for n in range(2):
                sp.dma_start(x_sb[:, n], x_rows[n]).then_inc(x_in[n], 16)
            sp.dma_start(taps[:, :], conv_w).then_inc(params_in, 16)
            for i, part in enumerate((lam_re, lam_im)):
                for h in range(2):
                    sp.dma_start(lam_rows[:, i, h * NS:(h + 1) * NS], part).then_inc(params_in, 16)
            sp.dma_start(dt[:, :], log_dt.partition_broadcast(P)).then_inc(params_in, 16)
            for c in range(KD):
                if c >= RAW:
                    sp.wait_ge(w_lo_done, c - RAW + 1)
                sp.dma_start(w_raw[:, c % RAW], w_rows[c]).then_inc(w_read[c % RAW], 16)
            sp.wait_ge(taps_laid, 1)
            for i in range(TB):
                sp.dma_start(scratch["toeplitz"].rearrange("t i g q j -> i (g q) t j")[i],
                             lagged[:, :, TB - 1 - i:3 * TB - 1 - i]).then_inc(tables_st, 16)
            s_v = scratch["s"].rearrange("(c p) s k -> s p c k", p=P)
            u_v = scratch["u"].rearrange("(c p) s k -> s p c k", p=P)

            def body(n, half, more):
                sp.wait_ge(z_free_s, n * 2 + 2)
                sp.dma_start(s_v[n], s_out[:, :, :]).then_inc(s_stored, 16)
                sp.wait_ge(u_done, n * CT + CT)
                sp.dma_start(u_v[n], u_out[:, :, :]).then_inc(u_stored, 16)

            with sp.Fori(0, PAIRS - 1) as i:
                for half in range(2):
                    n = i * 2 + half
                    sp.wait_ge(turned, n * 4 + 4)
                    sp.dma_start(x_sb[:, half], x_rows[n + 2]).then_inc(x_in[half], 16)
                    body(n, half, True)
            for n in (T8 - 2, T8 - 1):
                body(n, n % 2, True)
            sp.wait_ge(s_stored, 16 * T8)
            sp.wait_ge(u_stored, 16 * T8)

        @block.scalar
        def _(act):
            def square(n, half):
                act.wait_ge(x_in[half], (n - half) * 8 + 16)
                for h in range(2):
                    nc.scalar.activation(junk[:, :], x_sb[:, half, h], ACT.Square,
                                         accum_out=stat[:, 0, h:h + 1]).then_inc(squared, 1)
                    act.wait_ge(squared, n * 2 + h + 1)

            def highs(n, half, js):
                for j in js:
                    act.wait_ge(turned, n * 4 + j + 1)
                    for c in (2 * j, 2 * j + 1):
                        last = nc.scalar.activation(h_hi[:, half, c], p_tr[j % 2][:, (c % 2) * NK:(c % 2 + 1) * NK],
                                                    ACT.Copy, scale=gain[:, c:c + 1])
                    last.then_inc(hi_done, 1)

            def copy_ssm(n):
                for j in range(2):
                    act.wait_ge(z_done, n * 6 + j + 1)
                    if j == 0:
                        act.wait_ge(s_stored, n * 16)
                    nc.scalar.copy(s_out[:, 2 * j:2 * j + 2, :].rearrange("p c k -> p (c k)"),
                                   p_z[j][:, :]).then_inc(z_free_s, 1)
            def gates(n, js):
                for j in js:
                    act.wait_ge(z_done, n * 6 + 3 + j)
                    if j >= 2:
                        act.wait_ge(u_done, n * CT + j - 1)
                    nc.scalar.activation(sig[:, j % 2], p_z[2 + j][:, NK:2 * NK], ACT.Sigmoid).then_inc(sig_done, 1)

            act.wait_ge(gain_in, 16)
            square(0, 0)
            for c in range(KD):
                act.wait_ge(w_read[c % RAW], 16 * (c // RAW + 1))
                nc.scalar.copy(w_hi[:, c], w_raw[:, c % RAW]).then_inc(w_hi_done, 1)
            highs(0, 0, range(4))

            def body(n, half, more):
                if more:
                    square(n + 1, 1 - half)
                copy_ssm(n)
                for js in ((0, 1), (2, 3)):
                    if more:
                        highs(n + 1, 1 - half, js)
                    gates(n, js)
            over_tiles(act, body)

        @block.gpsimd
        def _(pool):
            G = nc.gpsimd
            G.memset(rev[:, :], 0.0).then_inc(cleared, 1)
            G.memset(lagged[:, :, :], 0.0).then_inc(cleared, 1)
            pool.wait_ge(cleared, 2)
            G.affine_select(out=rev[:, :], in_=rev[:, :], compare_op=ALU.not_equal, fill=1.0,
                            base=-(TAPS - 1), pattern=[[1, TAPS]], channel_multiplier=1).then_inc(rev_done, 1)
            pool.wait_ge(turn8_ready, 1)
            for i, one in enumerate((1.0, 0.0)):
                G.memset(turn[:, i, :, 0:1], one)
            turn_steps = 2 + 6 * int(math.log2(NK))
            with pool.Fori(0, NU) as n:
                step = Chain(pool, turns_own, n * turn_steps)
                pool.wait_ge(turns_st, n * 32)
                pool.sem_inc(turns_begun, 1)
                for i in range(2):
                    t8 = turn8[:, i, :].rearrange("p (u g) -> p u g", g=UG)[:, bass.ds(n, 1)]
                    step(G.tensor_copy(turn[:, i, :, 1:2], t8.rearrange("p u g -> p g u")))
                m = 1
                while m < NK:
                    w = min(m, NK - 1 - m)
                    at_m = [turn[:, i, :, m:m + 1].broadcast_to([P, UG, w]) for i in range(2)]
                    known = [turn[:, i, :, 1:1 + w] for i in range(2)]
                    new = [turn[:, i, :, m + 1:m + 1 + w] for i in range(2)]
                    complex_mul(G, step, *new, *at_m, *known, tt[:, 0, :, 0:w], tt[:, 1, :, 0:w])
                    m *= 2
                assert step.n == turn_steps
                pool.sem_inc(turns_begun, 1)
                for i, name in enumerate(("twc", "tws")):
                    pool.dma_start(scratch[name].rearrange("p (u g) m -> u p g m", g=UG)[n], turn[:, i]).then_inc(turns_st, 16)
            pool.wait_ge(turns_st, 32 * NU)

        @block.vector
        def _(dve):
            V = nc.vector

            def chunk_turn():
                step = Chain(dve, base_own)
                scr = [small[:, i, :] for i in range(8)]
                exp_precise(nc, step, dt[:, :], dt[:, :], scr[0], scr[1], scr[2])
                mag, sn, cs = scr[3], scr[4], scr[5]
                step(V.tensor_tensor(scr[6], lam[:, 0, :], dt[:, :], ALU.mult))
                exp_precise(nc, step, mag, scr[6], scr[0], scr[1], scr[2])
                step(V.tensor_tensor(scr[6], lam[:, 1, :], dt[:, :], ALU.mult))
                sincos_precise(nc, step, sn, cs, scr[6], scr[0], scr[1])
                step(V.tensor_tensor(pw_re[:, 1, :], mag, cs, ALU.mult))
                step(V.tensor_tensor(pw_im[:, 1, :], mag, sn, ALU.mult))
                step(V.tensor_tensor(scr[6], mag, mag, ALU.mult))
                step(V.tensor_tensor(scr[7], scr[6], scr[6], ALU.mult))
                step(V.tensor_tensor(decay8[:, :], scr[7], scr[7], ALU.mult))
                for _ in range(3):
                    step(V.tensor_tensor(scr[0], sn, sn, ALU.mult))
                    step(V.scalar_tensor_tensor(out=sn, in0=sn, scalar=2.0, in1=cs, op0=ALU.mult, op1=ALU.mult))
                    step(V.tensor_scalar(cs, scr[0], -2.0, 1.0, ALU.mult, ALU.add))
                step(V.tensor_tensor(scr[0], sn, sn, ALU.mult))
                step(V.tensor_tensor(scr[1], cs, cs, ALU.mult))
                step(V.tensor_tensor(scr[0], scr[0], scr[1], ALU.add))
                step(V.tensor_scalar(scr[0], scr[0], -0.5, 1.5, ALU.mult, ALU.add))
                step(V.tensor_tensor(turn8[:, 0, :], cs, scr[0], ALU.mult))
                step(V.tensor_tensor(turn8[:, 1, :], sn, scr[0], ALU.mult))
                V.engine_nop().then_inc(turn8_ready, 1)

            def scale_x(n, half):
                step = Chain(dve, own, n * (RSQRT_STEPS + 1))
                dve.wait_ge(squared, n * 2 + 2)
                a = stat[:, 1]
                step(nc.vector.tensor_scalar(a, stat[:, 0], 1.0 / D, EPS, ALU.mult, ALU.add))
                rsqrt(nc, step, stat[:, 3], a, stat[:, 2], stat[:, 0])
                for h in range(2):
                    last = nc.vector.tensor_scalar(x_sb[:, half, h], x_sb[:, half, h], stat[:, 3, h:h + 1], None, ALU.mult)
                last.then_inc(scaled, 1)

            def lows(n, half, js):
                for j in js:
                    dve.wait_ge(hi_done, n * 4 + j + 1)
                    for c in (2 * j, 2 * j + 1):
                        last = nc.vector.scalar_tensor_tensor(
                            out=h_lo[:, half, c], in0=p_tr[j % 2][:, (c % 2) * NK:(c % 2 + 1) * NK],
                            scalar=gain[:, c:c + 1], in1=h_hi[:, half, c].bitcast(FP32),
                            op0=ALU.mult, op1=ALU.subtract)
                    last.then_inc(lo_done, 1)

            def glu(n, js):
                for j in js:
                    dve.wait_ge(sig_done, n * CT + j + 1)
                    if j == 0:
                        dve.wait_ge(u_stored, n * 16)
                    nc.vector.tensor_tensor(u_out[:, j], p_z[2 + j][:, 0:NK], sig[:, j % 2], ALU.mult).then_inc(u_done, 1)

            dve.wait_ge(gain_in, 16)
            scale_x(0, 0)
            dve.wait_ge(lam_turned, 1)
            nc.vector.tensor_copy(lam[:, :, :].rearrange("p i g -> p (i g)"), p_tr[1][:, 0:2 * GRP]).then_inc(lam_read, 1)
            dve.wait_ge(cleared, 2)
            dve.wait_ge(taps_turned, 1)
            nc.vector.tensor_copy(lagged[:, :, TB - 1:TB - 1 + TAPS],
                                  p_z[5][:, 0:P].rearrange("p (t l) -> p t l", t=CT)[:, :, 0:TAPS]).then_inc(taps_laid, 1)
            for c in range(KD):
                dve.wait_ge(w_hi_done, c + 1)
                nc.vector.tensor_tensor(w_lo[:, c], w_raw[:, c % RAW], w_hi[:, c].bitcast(FP32),
                                        ALU.subtract).then_inc(w_lo_done, 1)
            lows(0, 0, range(4))
            chunk_turn()

            def body(n, half, more):
                if more:
                    scale_x(n + 1, 1 - half)
                for js in ((0, 1), (2, 3)):
                    if more:
                        lows(n + 1, 1 - half, js)
                    glu(n, js)
            over_tiles(dve, body)

        @block.tensor
        def _(pe):
            def transposes(n, half, js):
                pe.wait_ge(scaled, n + 1)
                for j in js:
                    if j >= 2:
                        pe.wait_ge(lo_done, n * 4 + j - 1)
                    for c in (2 * j, 2 * j + 1):
                        for h in range(2):
                            at = (c % 2) * NK + h * P
                            last = nc.tensor.transpose(p_tr[j % 2][:, at:at + P], x_sb[:, half, h, c * P:(c + 1) * P], ident[:, :])
                    last.then_inc(turned, 1)

            def products(n, half, more):
                pe.wait_ge(lo_done, n * 4 + 4)
                units = [(8, 9), (10, 11), (0, 4), (1, 5), (2, 6), (3, 7)]
                for j, blocks in enumerate(units):
                    if j == 0:
                        pe.wait_ge(z_free_s, n * 2)
                        pe.wait_ge(u_done, n * CT)
                    for b, m in enumerate(blocks):
                        o = p_z[j][:, b * NK:(b + 1) * NK]
                        for c in range(KD):
                            whi, wlo = w_hi[:, c, m * P:(m + 1) * P], w_lo[:, c, m * P:(m + 1) * P]
                            nc.tensor.matmul(o, whi, h_hi[:, half, c], start=c == 0, stop=False)
                            nc.tensor.matmul(o, whi, h_lo[:, half, c], start=False, stop=False)
                            last = nc.tensor.matmul(o, wlo, h_hi[:, half, c], start=False, stop=c == KD - 1)
                    last.then_inc(z_done, 1)
                    if more and j in (1, 3):
                        transposes(n + 1, 1 - half, (j - 1, j))

            pe.wait_ge(params_in, 16 * 6)
            for i in range(2):
                last = nc.tensor.transpose(p_tr[1][:, i * GRP:(i + 1) * GRP], lam_rows[:, i, :], ident[0:GRP, 0:GRP])
            last.then_inc(lam_turned, 1)
            pe.wait_ge(rev_done, 1)
            for t in range(CT):
                last = nc.tensor.matmul(p_z[5][:, t * 32:t * 32 + TAPS], taps[:, t * P:(t + 1) * P], rev[:, :],
                                        start=True, stop=True)
            last.then_inc(taps_turned, 1)
            pe.wait_ge(lam_read, 1)
            transposes(0, 0, range(4))
            pe.wait_ge(taps_laid, 1)
            pe.wait_ge(w_lo_done, KD)

            over_tiles(pe, products)


def convolution_and_tables(nc, scratch, conv_b, tables_st, ident, eye_turn, lam, pw_re, pw_im,
                           b_re, b_im, c_re, c_im):
    NB = SEQ // TB
    QB = 512 // NB
    BANKS = 32 // QB
    NP = T8 + 1
    FREE_TILES = CT - NU // BANKS
    with ExitStack() as ctx:
        sb, ps, sem = alloc(nc, ctx, "conv")
        toep = sb("toep", [P, 2, 32, 2, P])
        bias = sb("bias", [P, CT])
        u = sb("u", [P, T8, NK])
        ut = sb("ut", [P, 2, 1 + NB, 32])
        o = sb("o", [P, NB, 32])
        yt, y = sb("yt", [P, NK, T8]), sb("y", [P, 2, T8, NK])
        p_o = ps("p_o", (P, BANKS, 512))
        b_in, cleared, cleared_dve, ut_cleared = (sem(n) for n in ("b_in", "cleared", "cleared_dve", "ut_cleared"))
        u_in, toep_in = sem("u_in"), [sem("toep_in0"), sem("toep_in1")]
        turned, product, copied, back, made = (sem(n) for n in ("turned", "product", "copied", "back", "made"))
        stored = [sem("stored0"), sem("stored1")]

        b_raw, bb = sb("b_raw", [P, 2, GRP, GC]), sb("bb", [P, 2, GRP, GC])
        c_rows, c_cols = sb("c_rows", [P, 2, CT, P]), sb("c_cols", [P, 2, GRP * GC])
        tmp = sb("tmp", [P, 2, GRP, GC])
        small, wide = sb("small", [P, 8, GRP]), sb("wide", [P, 2, T8 // 2, GRP])
        in_re, in_im = sb("in_re", [P, GRP, NP]), sb("in_im", [P, GRP, NP])
        out_re, out_im = sb("out_re", [P, GRP, NP]), sb("out_im", [P, GRP, NP])
        v = sb("v", [P, UG, T8, GC])
        o1 = sb("o1", [P, UG, NP, GC])
        vt = sb("vt", [P, UG, NP, GC])
        w12, o2 = sb("w12", [P, UG, 2 * P]), sb("o2", [P, UG, P])
        kern = sb("kern", [GC, UG, LAGS * GC])
        p_w = [ps("p_w0"), ps("p_w1")]
        p_k, p_oo = ps("p_k"), ps("p_oo")
        loaded, own, v_own = sem("loaded"), sem("own"), sem("v_own")
        c_turned, c_ready, factors_ready = sem("c_turned"), sem("c_ready"), sem("factors_ready")
        v_ready, products_done, tab_copied = sem("v_ready"), sem("products_done"), sem("tab_copied")
        kern_clear = sem("kern_clear")
        st_w, st_o1, st_o2, st_k = (sem(n) for n in ("st_w", "st_o1", "st_o2", "st_k"))
        block = ctx.enter_context(nc.Block())
        LOADS = 4 + 4

        @block.gpsimd
        def _(pool):
            for half in range(2):
                nc.gpsimd.memset(toep[:, half, 16:].rearrange("p q h o -> p (q h o)"), 0.0).then_inc(cleared, 1)
            nc.gpsimd.memset(kern[:, :, :], 0.0).then_inc(kern_clear, 1)

        @block.sync
        def _(sp):
            u_v = scratch["u"].rearrange("(t p) s k -> t p s k", p=P)
            sp.dma_start(u[:, :, :], u_v[0]).then_inc(u_in, 16)
            load_column(nc, sp, bias[:, :], conv_b).then_inc(b_in, 16)
            sp.wait_ge(tables_st, 16 * TB)
            for t in range(CT):
                half = t % 2
                if t < 2:
                    sp.wait_ge(cleared, t + 1)
                    sp.wait_ge(cleared_dve, t + 1)
                else:
                    sp.wait_ge(product, (t - 1) * BANKS)
                for g in range(4):
                    sp.dma_start(toep[g * 32:(g + 1) * 32, half, :, :, g * 32:(g + 1) * 32],
                                 scratch["toeplitz"][t, :, g].rearrange("i q (h o) -> i q h o", h=2)).then_inc(toep_in[half], 16)
                if t == 0:
                    for i, a in enumerate((c_re, c_im)):
                        rows = a.rearrange("(t g) c n -> (g c) t n", t=CT)
                        for h in range(2):
                            sp.dma_start(c_rows[:, i, :, h * NS:(h + 1) * NS], rows).then_inc(loaded, 16)
                    for i, a in enumerate((b_re, b_im)):
                        for h in range(2):
                            sp.dma_start(b_raw[h * NS:(h + 1) * NS, i], a.rearrange("g n c -> n g c")).then_inc(loaded, 16)
                if t + 1 < CT:
                    sp.wait_ge(turned, t + 1)
                    sp.dma_start(u[:, :, :], u_v[t + 1]).then_inc(u_in, 16)
            with sp.Fori(0, NU) as n:
                sp.wait_ge(v_ready, 2 * n + 2)
                sp.dma_start(scratch["o1"].rearrange("p (u g) m -> u p g m", g=UG)[n],
                             o1[:, :, 1:NP].rearrange("p g j c -> p g (j c)")).then_inc(st_o1, 16)
                sp.wait_ge(tab_copied, 3 * n + 3)
                sp.dma_start(scratch["w12"].rearrange("p (u g) m -> u p g m", g=UG)[n], w12[:, :, :]).then_inc(st_w, 16)
                sp.dma_start(scratch["kernel"].rearrange("p (u g) m -> u p g m", g=UG)[n], kern[:, :, :]).then_inc(st_k, 16)
                sp.dma_start(scratch["o2"].rearrange("p (u g) m -> u p g m", g=UG)[n], o2[:, :, :]).then_inc(st_o2, 16)
            for s in (st_w, st_k, st_o1, st_o2):
                sp.wait_ge(s, 16 * NU)

        @block.vector
        def _(dve):
            V = nc.vector
            step = Chain(dve, own)

            def tt2(o, a, b, op):
                step(V.tensor_tensor(o, a, b, op))

            def turn(t):
                half = t % 2
                dve.wait_ge(u_in, 16 * (t + 1))
                if t >= 2:
                    dve.wait_ge(product, (t - 1) * BANKS)
                V.transpose(ut[:, half, 1:], u[:, :, :].rearrange("p s k -> p k s")).then_inc(turned, 1)

            def turn_back(t):
                dve.wait_ge(copied, (t + 1) * BANKS)
                if t >= 1:
                    dve.wait_ge(made, t)
                V.transpose(yt[:, :, :].rearrange("p k s -> p (k s)"), o[:, :, :].rearrange("p b q -> p (b q)")).then_inc(back, 1)

            def factors():
                dve.wait_ge(loaded, 16 * LOADS)
                dve.wait_ge(c_turned, 1)
                for i in range(2):
                    step(V.tensor_copy(c_cols[:, i, :], p_w[i][:, :]))
                lr, li = lam[:, 0, :], lam[:, 1, :]
                scr = [small[:, i, :] for i in range(8)]
                step(V.memset(pw_re[:, 0, :], 1.0))
                step(V.memset(pw_im[:, 0, :], 0.0))
                m = 1
                while m < T8:
                    at_m = [pw[:, m:m + 1, :].broadcast_to([P, m, GRP]) for pw in (pw_re, pw_im)]
                    complex_mul(V, step, pw_re[:, m + 1:2 * m + 1, :], pw_im[:, m + 1:2 * m + 1, :], *at_m,
                                pw_re[:, 1:m + 1, :], pw_im[:, 1:m + 1, :],
                                wide[:, 0, 0:m, :], wide[:, 1, 0:m, :])
                    m *= 2
                step(V.tensor_scalar(scr[0], pw_re[:, 1, :], -1.0, None, ALU.add))
                ai = pw_im[:, 1, :]
                tt2(scr[1], lr, lr, ALU.mult)
                tt2(scr[2], li, li, ALU.mult)
                tt2(scr[1], scr[1], scr[2], ALU.add)
                step(V.reciprocal(scr[1], scr[1]))
                tt2(scr[2], scr[0], lr, ALU.mult)
                tt2(scr[3], ai, li, ALU.mult)
                tt2(scr[2], scr[2], scr[3], ALU.add)
                tt2(scr[2], scr[2], scr[1], ALU.mult)
                tt2(scr[3], ai, lr, ALU.mult)
                tt2(scr[4], scr[0], li, ALU.mult)
                tt2(scr[3], scr[3], scr[4], ALU.subtract)
                tt2(scr[3], scr[3], scr[1], ALU.mult)
                q_re, q_im = (scr[i].unsqueeze(2).broadcast_to([P, GRP, GC]) for i in (2, 3))
                complex_mul(V, step, bb[:, 0], bb[:, 1], q_re, q_im, b_raw[:, 0], b_raw[:, 1], tmp[:, 0], tmp[:, 1])
                top, low = slice(0, NS), slice(NS, P)
                for to, half, of, sign in ((in_re, top, pw_re, 1), (in_re, low, pw_im, 1),
                                           (in_im, top, pw_im, -1), (in_im, low, pw_re, 1),
                                           (out_re, top, pw_re, 1), (out_re, low, pw_im, -1),
                                           (out_im, top, pw_im, -1), (out_im, low, pw_re, -1)):
                    step(V.tensor_scalar(to[half].rearrange("p g j -> p j g"), of[half], float(sign), None, ALU.mult))

            def units(first, end):
                def of_unit(ap, pattern, n):
                    return ap.rearrange(pattern, g=UG)[:, bass.ds(n, 1)].squeeze(1)

                def expand(n, k, to, fac_re, fac_im, ar, ai, lags):
                    vstep = Chain(dve, v_own, n * 4 + 2 * k)
                    for fac, a, out in ((fac_re, ar, to), (fac_im, ai, vt[:, :, 0:lags, :])):
                        f = of_unit(fac[:, :, :], "p (u g) j -> p u g j", n)[:, :, 0:lags]
                        vstep(V.tensor_tensor(out, f.unsqueeze(3).broadcast_to([P, UG, lags, GC]),
                                              of_unit(a, "p (u g) c -> p u g c", n).unsqueeze(2).broadcast_to([P, UG, lags, GC]),
                                              ALU.mult))
                    V.tensor_tensor(to, to, vt[:, :, 0:lags, :], ALU.add).then_inc(v_ready, 1)

                with dve.Fori(first, end) as n:
                    dve.wait_ge(products_done, n)
                    dve.wait_ge(st_o1, n * 16)
                    expand(n, 0, v[:, :, :, :], in_re, in_im, bb[:, 0], bb[:, 1], T8)
                    dve.wait_ge(v_ready, n * 2 + 1)
                    cc = [c_cols[:, i, :].rearrange("p (g c) -> p g c", c=GC) for i in range(2)]
                    expand(n, 1, o1[:, :, :, :], out_re, out_im, *cc, NP)

            V.memset(ut[:, :, 0], 0.0).then_inc(ut_cleared, 1)
            for half in range(2):
                V.memset(toep[:, half, 0:16].rearrange("p q h o -> p (q h o)"), 0.0).then_inc(cleared_dve, 1)
            turn(0)
            turn(1)
            factors()
            turn_back(0)
            turn(2)
            turn_back(1)
            turn(3)
            for t in range(FREE_TILES, CT):
                units((t - FREE_TILES) * BANKS, (t - FREE_TILES + 1) * BANKS)
                turn_back(t)

        @block.tensor
        def _(pe):
            def quads(t, i):
                half = t % 2
                if t > 0:
                    pe.wait_ge(copied, i + ((t - 1) * BANKS + 1))
                for j in range(QB):
                    out = p_o[:, i, j * NB:(j + 1) * NB]
                    q = i * QB + j
                    nc.tensor.matmul(out, toep[:, half, q, 0], ut[:, half, 1:, q],
                                     start=True, stop=False)
                    last = nc.tensor.matmul(out, toep[:, half, q, 1], ut[:, half, 0:NB, q],
                                            start=False, stop=True)
                last.then_inc(product, 1)

            def unit(n):
                pe.wait_ge(v_ready, n * 2 + 2)
                wait(pe, tab_copied, n * 3)
                for g in range(UG):
                    nc.tensor.matmul(p_w[g // 2][:, (g % 2) * 2 * P:(g % 2 + 1) * 2 * P],
                                     v[:, g].rearrange("p j c -> p (j c)"), eye_turn[:, :], start=True, stop=True)
                    nc.tensor.matmul(p_k[0:GC, g * P:(g + 1) * P], v[:, g, 0, :],
                                     o1[:, g, 0:T8, :].rearrange("p j c -> p (j c)"), start=True, stop=True)
                for g in range(UG):
                    last = nc.tensor.matmul(p_oo[:, g * P:(g + 1) * P], eye_turn[:, P:2 * P],
                                            o1[:, g, 1:NP, :].rearrange("p j c -> p (j c)"), start=True, stop=True)
                last.then_inc(products_done, 1)

            pe.wait_ge(ut_cleared, 1)
            for t in range(CT):
                pe.wait_ge(toep_in[t % 2], 64 * (t // 2 + 1))
                pe.wait_ge(turned, t + 1)
                if t == 1:
                    pe.wait_ge(loaded, 16 * LOADS)
                    for i in range(2):
                        for c in range(CT):
                            last = nc.tensor.transpose(p_w[i][:, c * P:(c + 1) * P], c_rows[:, i, c, :], ident[:, :])
                    last.then_inc(c_turned, 1)
                for i in range(BANKS):
                    quads(t, i)
                    if t >= FREE_TILES:
                        unit(i + (t - FREE_TILES) * BANKS)

        @block.scalar
        def _(act):
            act.wait_ge(b_in, 16)
            o_v = scratch["conv"].rearrange("(t p) s k -> t p s k", p=P)

            def copy_bank(t, i):
                act.wait_ge(product, i + (t * BANKS + 1))
                if t >= 1:
                    act.wait_ge(back, t)
                nc.scalar.copy(o[:, :, bass.ds(i * QB, QB)].rearrange("p b q -> p q b"),
                               p_o[:, bass.ds(i, 1), :].squeeze(1).rearrange("p (q b) -> p q b", q=QB)).then_inc(copied, 1)

            def copy_unit(n):
                act.wait_ge(products_done, n + 1)
                act.wait_ge(st_w, n * 16)
                for i in range(2):
                    last = nc.scalar.copy(w12[:, 2 * i:2 * i + 2, :].rearrange("p g m -> p (g m)"), p_w[i][:, :])
                last.then_inc(tab_copied, 1)
                act.wait_ge(st_k, n * 16)
                nc.scalar.copy(kern[:, :, (T8 - 1) * GC:], p_k[0:GC, :].rearrange("p (g m) -> p g m", g=UG)).then_inc(tab_copied, 1)
                act.wait_ge(st_o2, n * 16)
                nc.scalar.copy(o2[:, :, :].rearrange("p g m -> p (g m)"), p_oo[:, :]).then_inc(tab_copied, 1)

            def finish(t):
                half = t % 2
                act.wait_ge(back, t + 1)
                if t >= 2:
                    act.wait_ge(stored[half], 16 * (t // 2))
                nc.scalar.activation(y[:, half], yt[:, :, :].rearrange("p k s -> p s k"), ACT.Identity,
                                     bias=bias[:, t:t + 1]).then_inc(made, 1)
                act.wait_ge(made, t + 1)
                act.dma_start(o_v[t], y[:, half]).then_inc(stored[half], 16)

            act.wait_ge(kern_clear, 1)
            for t in range(CT):
                with act.Fori(0, BANKS) as i:
                    copy_bank(t, i)
                    if t >= FREE_TILES:
                        copy_unit(i + (t - FREE_TILES) * BANKS)
                finish(t)
            for half in range(2):
                act.wait_ge(stored[half], 16 * CT // 2)


def ssm(nc, scratch, decay8, weights, w_out, glu_w):
    SG = GRP // CT
    SLOTS = SG // 2
    with ExitStack() as ctx:
        sb, ps, sem = alloc(nc, ctx, "ssm")
        inp = sb("inp", [P, 2, SG, NK])
        w12 = sb("w12", [P, 2, SG, 2 * P])
        o1, o2 = sb("o1", [P, 2, SG, P]), sb("o2", [P, 2, SG, P])
        kern = sb("kern", [P, 2, SG, P])
        twc, tws = sb("twc", [P, 2, SG, NK]), sb("tws", [P, 2, SG, NK])
        b = sb("b", [P, 2, NK])
        drive = sb("drive", [P, 2, 2, NK])
        state = sb("state", [P, 2, 2, NK])
        e1, e2 = sb("e1", [P, 2, 2, NK + 1]), sb("e2", [P, 2, 2, NK + 1])
        y = sb("y", [P, SG, NK])
        p_in = [ps(f"p_in{i}") for i in range(4)]
        p_y = [ps("p_y0"), ps("p_y1")]
        wo_raw, glu_raw = sb("wo_raw", [P, SLOTS, 512]), sb("glu_raw", [P, SW])
        wo_in, glu_in = [sem(f"wo_in{i}") for i in range(SLOTS)], sem("glu_in")
        wo_hi_done, wo_lo_done, glu_hi_done, glu_lo_done = (
            sem(n) for n in ("wo_hi_done", "wo_lo_done", "glu_hi_done", "glu_lo_done"))
        in_loaded, turn_loaded, out_loaded = ([sem(f"{n}{half}") for half in range(2)]
                                              for n in ("in_loaded", "turn_loaded", "out_loaded"))
        cleared = sem("cleared")
        driven, a_done, b_done, d_done, scanned = (sem(n) for n in ("driven", "a_done", "b_done", "d_done", "scanned"))
        e_done, y_done, y_copied = sem("e_done"), sem("y_done"), sem("y_copied")
        y_stored = [sem("y_stored0"), sem("y_stored1")]
        block = ctx.enter_context(nc.Block())
        PR = SG // 2
        IN_LOADS, TURN_LOADS, OUT_LOADS = T8 + 1, 2, T8 + 2

        def over_blocks(engine, body):
            with engine.Fori(0, CT // 2) as i:
                for half in range(2):
                    body(i * 2 + half, i, half)

        def piece(t, i, half, k):
            return t[:, bass.ds(i * 4 + (2 * half + k // 2), 1), (k % 2) * 512:(k % 2 + 1) * 512].squeeze(1)

        @block.sync
        def _(sp):
            s_v = scratch["s"].rearrange("(t g c) s k -> t s c g k", g=SG, c=GC)
            k_v = scratch["kernel"].rearrange("c (t g) m -> t c g m", g=SG)

            def load(n, half):
                whole = lambda name: scratch[name].rearrange("p (t g) m -> t p g m", g=SG)[n]
                for s in range(T8):
                    rows = slice((T8 - 1 - s) * GC, (T8 - s) * GC)
                    sp.dma_start(inp[rows, half], s_v[n][s]).then_inc(in_loaded[half], 16)
                sp.dma_start(w12[:, half], whole("w12")).then_inc(in_loaded[half], 16)
                sp.dma_start(twc[:, half], whole("twc")).then_inc(turn_loaded[half], 16)
                sp.dma_start(tws[:, half], whole("tws")).then_inc(turn_loaded[half], 16)
                for s in range(T8):
                    rows, first = slice((T8 - 1 - s) * GC, (T8 - s) * GC), (T8 - 1 - s) * GC
                    sp.dma_start(kern[rows, half], k_v[n][:, :, first:first + P]).then_inc(out_loaded[half], 16)
                sp.dma_start(o1[:, half], whole("o1")).then_inc(out_loaded[half], 16)
                sp.dma_start(o2[:, half], whole("o2")).then_inc(out_loaded[half], 16)

            pieces = w_out.rearrange("(c p) (h f) -> c h p f", p=P, h=2)
            glu_rows = glu_w.rearrange("(c p) f -> c p f", p=P)

            def load_piece(i, half, q):
                sp.dma_start(wo_raw[:, q], pieces[i * 4 + (2 * half + q // 2)][q % 2]).then_inc(wo_in[q], 16)

            def body(i, half, blocks, next_pieces):
                if next_pieces or half == 0:
                    for q in range(PR):
                        sp.wait_ge(wo_lo_done, i * 8 + (4 * half + q + 1))
                        load_piece(i + half, 1 - half, q)
                if next_pieces or half == 0:
                    sp.wait_ge(glu_lo_done, i * 2 + (half + 1))
                    sp.dma_start(glu_raw[:, :], glu_rows[i * 2 + (half + 1)]).then_inc(glu_in, 16)
                if blocks:
                    sp.wait_ge(y_done, (i * 2 + half + 1) * PR)
                    load(i * 2 + half + 2, half)

            load(0, 0)
            for q in range(PR):
                load_piece(0, 0, q)
            sp.dma_start(glu_raw[:, :], glu_rows[0]).then_inc(glu_in, 16)
            load(1, 1)
            with sp.Fori(0, CT // 2 - 1) as i:
                for half in range(2):
                    body(i, half, True, True)
            for half in range(2):
                body(CT // 2 - 1, half, False, False)

        @block.tensor
        def _(pe):
            def drive_of(n, i, half, q):
                m = n * PR + q
                bank = q % 2
                if q == 0:
                    pe.wait_ge(in_loaded[half], (i + 1) * 16 * IN_LOADS)
                wait(pe, b_done, m - 1 if q else n * PR - 1 if not isinstance(n, int) or n else 0)
                for g in range(2):
                    for part in range(2):
                        last = nc.tensor.matmul(p_in[2 * bank + part][:, g * NK:(g + 1) * NK],
                                                w12[:, half, 2 * q + g, part * P:(part + 1) * P],
                                                inp[:, half, 2 * q + g, :], start=True, stop=True)
                last.then_inc(driven, 1)

            def body(n, i, half, more=True):
                for q in range(PR):
                    if q + 1 < PR:
                        drive_of(n, i, half, q + 1)
                    elif more:
                        drive_of(n + 1, i + half, 1 - half, 0)
                    if q == 0:
                        pe.wait_ge(out_loaded[half], (i + 1) * 16 * OUT_LOADS)
                    out_of(n, half, q)

            def out_of(n, half, q):
                m = n * PR + q
                bank = q % 2
                pe.wait_ge(e_done, 2 * m + 2)
                if q >= 2:
                    pe.wait_ge(y_copied, m - 1)
                else:
                    pe.wait_ge(y_copied, n * PR)
                for g in range(2):
                    o = p_y[bank][:, g * NK:(g + 1) * NK]
                    nc.tensor.matmul(o, kern[:, half, 2 * q + g, :], inp[:, half, 2 * q + g, :], start=True, stop=False)
                    nc.tensor.matmul(o, o1[:, half, 2 * q + g, :], e1[:, bank, g, 0:NK], start=False, stop=False)
                    last = nc.tensor.matmul(o, o2[:, half, 2 * q + g, :], e2[:, bank, g, 0:NK], start=False, stop=True)
                last.then_inc(y_done, 1)

            drive_of(0, 0, 0, 0)
            with pe.Fori(0, CT // 2 - 1) as i:
                for half in range(2):
                    body(i * 2 + half, i, half)
            body(CT - 2, CT // 2 - 1, 0)
            body(CT - 1, CT // 2 - 1, 1, more=False)

        @block.vector
        def _(dve):
            V = nc.vector
            V.memset(e1[:, :, :, 0:1], 0.0).then_inc(cleared, 1)
            V.memset(e2[:, :, :, 0:1], 0.0).then_inc(cleared, 1)

            def body(n, i, half):
                dve.wait_ge(turn_loaded[half], (i + 1) * 16 * TURN_LOADS)
                for q in range(PR):
                    m = n * PR + q
                    bank = q % 2
                    gs = slice(2 * q, 2 * q + 2)
                    dve.wait_ge(driven, m + 1)
                    pair = lambda t: t[:, :].rearrange("p (g k) -> p g k", g=2)
                    V.tensor_tensor(drive[:, bank], pair(p_in[2 * bank]), twc[:, half, gs], ALU.mult).then_inc(a_done, 1)
                    V.tensor_tensor(b[:, :, :], pair(p_in[2 * bank + 1]), tws[:, half, gs], ALU.mult).then_inc(b_done, 1)
                    dve.wait_ge(a_done, m + 1)
                    dve.wait_ge(b_done, m + 1)
                    V.tensor_tensor(drive[:, bank], drive[:, bank], b[:, :, :], ALU.add).then_inc(d_done, 1)
                    dve.wait_ge(d_done, m + 1)
                    if q >= 2:
                        dve.wait_ge(e_done, 2 * m - 2)
                    else:
                        dve.wait_ge(e_done, n * PR * 2)
                    for g in range(2):
                        col = decay8[:, bass.ds(n * SG + (2 * q + g), 1)]
                        V.tensor_tensor_scan(state[:, bank, g], col.broadcast_to([P, NK]), drive[:, bank, g], 0.0,
                                             ALU.mult, ALU.add).then_inc(scanned, 1)
                    for k in ((), (0, 1), (2,), (3,))[q]:
                        dve.wait_ge(wo_hi_done, n * PR + k + 1)
                        V.tensor_tensor(piece(weights["wo_lo"], i, half, k), wo_raw[:, k],
                                        piece(weights["wo_hi"], i, half, k).bitcast(FP32), ALU.subtract).then_inc(wo_lo_done, 1)
                    if q == 2:
                        dve.wait_ge(glu_hi_done, n + 1)
                        V.tensor_tensor(weights["glu_lo"][:, bass.ds(n, 1)].squeeze(1), glu_raw[:, :],
                                        weights["glu_hi"][:, bass.ds(n, 1)].squeeze(1).bitcast(FP32),
                                        ALU.subtract).then_inc(glu_lo_done, 1)
            over_blocks(dve, body)

        @block.gpsimd
        def _(pool):
            pool.wait_ge(cleared, 2)

            def body(n, i, half):
                for q in range(PR):
                    m = n * PR + q
                    bank = q % 2
                    gs = slice(2 * q, 2 * q + 2)
                    pool.wait_ge(scanned, 2 * m + 2)
                    if q >= 2:
                        pool.wait_ge(y_done, m - 1)
                    else:
                        pool.wait_ge(y_done, n * PR)
                    nc.gpsimd.tensor_tensor(e1[:, bank, :, 1:NK + 1], state[:, bank], twc[:, half, gs], ALU.mult).then_inc(e_done, 1)
                    nc.gpsimd.tensor_tensor(e2[:, bank, :, 1:NK + 1], state[:, bank], tws[:, half, gs], ALU.mult).then_inc(e_done, 1)
            over_blocks(pool, body)

        @block.scalar
        def _(act):
            y_v = scratch["y"].rearrange("(t g c) s k -> t s c g k", g=SG, c=GC)

            def body(n, i, half):
                for q in range(PR):
                    m = n * PR + q
                    if q % 2 == 0:
                        act.wait_ge(y_stored[q // 2], n * T8 * 16)
                    act.wait_ge(y_done, m + 1)
                    nc.scalar.copy(y[:, 2 * q:2 * q + 2, :].rearrange("p g k -> p (g k)"), p_y[q % 2][:, :]).then_inc(y_copied, 1)
                    if q == 0:
                        for k in range(PR):
                            act.wait_ge(wo_in[k], n * 16 + 16)
                            nc.scalar.copy(piece(weights["wo_hi"], i, half, k), wo_raw[:, k]).then_inc(wo_hi_done, 1)
                        act.wait_ge(glu_in, n * 16 + 16)
                        nc.scalar.copy(weights["glu_hi"][:, bass.ds(n, 1)].squeeze(1), glu_raw[:, :]).then_inc(glu_hi_done, 1)
                    if q % 2 == 1:
                        act.wait_ge(y_copied, m + 1)
                        gs = slice(2 * q - 2, 2 * q + 2)
                        for s in range(T8):
                            act.dma_start(y_v[n][s][:, gs], y[s * GC:(s + 1) * GC, gs]).then_inc(y_stored[q // 2], 16)
            over_blocks(act, body)
            for h in range(2):
                act.wait_ge(y_stored[h], CT * T8 * 16)


def wait(engine, sem, value):
    if not isinstance(value, int) or value > 0:
        engine.wait_ge(sem, value)


def mix(nc, scratch, ident, logits, weights, x, ln_g, ln_b, ssm_d, glu_b, g_branch, g_ffn,
        w_rg, b_rg, w_re, b_re):
    TN = NK
    GELU = 2 * math.sqrt(2 / math.pi)
    NL = NG + NE
    with ExitStack() as ctx:
        sb, ps, sem = alloc(nc, ctx, "mix")
        wo_hi, wo_lo, glu_hi, glu_lo = (weights[n] for n in ("wo_hi", "wo_lo", "glu_hi", "glu_lo"))
        cols = sb("cols", [P, 7, CT])
        LNG, LNB, DD, GLB, GBC, GBS = range(6)
        gain = sb("gain", [P, D])
        wr, br = sb("wr", [P, KD, NL]), sb("br", [P, NL])
        ones = sb("ones", [P, 1])
        conv_in, y_in, s_in = sb("conv_in", [P, CT, TN]), sb("y_in", [P, CT, TN]), sb("s_in", [P, CT, TN])
        yn = sb("yn", [P, 2, CW])
        bn, mv = sb("bn", [P, 2, 6]), sb("mv", [P, 2, 3])
        st = sb("st", [P, 4, 4])
        rs = sb("rs", [P, 4])
        cube, sg = sb("cube", [P, CT, TN]), sb("sg", [P, CT, TN])
        yg, ys, yc = sb("yg", [P, CT, TN]), sb("ys", [P, CT, TN]), sb("yc", [P, CT, TN])
        yg_hi, yg_lo = sb("yg_hi", [P, CT, TN], FP32R), sb("yg_lo", [P, CT, TN], FP32R)
        sq = sb("sq", [P, 2, CT, TN])
        cat_hi, cat_lo = sb("cat_hi", [P, 2, KD, TN], FP32R), sb("cat_lo", [P, 2, KD, TN], FP32R)
        x_sb, x2, h = sb("x_sb", [P, 2, D]), sb("x2", [P, 2, D]), sb("h", [P, 2, D])
        junk, hT = sb("junk", [P, D]), sb("hT", [P, KD, P])
        zero = junk
        pa, pb, pc, pd = ps("pa"), ps("pb"), ps("pc"), ps("pd")
        p_out = [ps(f"p_out{i}") for i in range(4)]

        params, ones_done, summed = sem("params"), sem("ones_done"), sem("summed")
        adds = sem("adds")
        conv_ld, y_ld, s_ld = sem("conv_ld"), sem("y_ld"), sem("s_ld")
        x_ld = [sem("x_ld0"), sem("x_ld1")]
        own = sem("own")
        ln_tr, bn_own, yn_done, ln_back = sem("ln_tr"), sem("bn_own"), sem("yn_done"), sem("ln_back")
        v_done, cube_own, cube_done, gelu_sig, yg_done = (sem(n) for n in ("v_done", "cube_own", "cube_done", "gelu_sig", "yg_done"))
        yg_hi_done, yg_lo_done, glu_done, glu_sig, ys_done = (sem(n) for n in ("yg_hi_done", "yg_lo_done", "glu_done", "glu_sig", "ys_done"))
        yc_done, c_hi_done, c_lo_done, s_hi_done, s_lo_done = (sem(n) for n in ("yc_done", "c_hi_done", "c_lo_done", "s_hi_done", "s_lo_done"))
        sums_done, sums_read = sem("sums_done"), sem("sums_read")
        out_done, x2_own, x2_sq, h_done = (sem(n) for n in ("out_done", "x2_own", "x2_sq", "h_done"))
        h_turned, h_copied, logit_done, logit_read = (sem(n) for n in ("h_turned", "h_copied", "logit_done", "logit_read"))
        x2_st, h_st, pads = [sem("x2_st0"), sem("x2_st1")], [sem("h_st0"), sem("h_st1")], sem("pads")
        zeroed, gelu_arg, sums_own, half_a, half_b = (sem(n) for n in ("zeroed", "gelu_arg", "sums_own", "half_a", "half_b"))
        block = ctx.enter_context(nc.Block())
        PARAMS = 6 + 5

        def over_steps(engine, body):
            body(0, 0)
            body(1, 1)
            with engine.Fori(0, (T8 - 4) // 2) as i:
                body(i * 2 + 2, 0)
                body(i * 2 + 3, 1)
            body(T8 - 2, 0)
            body(T8 - 1, 1)
            body(T8, 0)

        def first(n):
            return isinstance(n, int) and n == 0

        def last_step(n):
            return isinstance(n, int) and n == T8

        x_rows = x.rearrange("(h k s) d -> s h k d", s=T8, h=2)
        rows = lambda name: scratch[name][0:SEQ, :].rearrange("(n t p) d -> n t p d", t=2, p=P)
        tiles = lambda name: scratch[name].rearrange("(c p) s k -> s p c k", p=P)

        @block.sync
        def _(sp):
            vectors = ((LNG, ln_g), (LNB, ln_b), (DD, ssm_d), (GLB, glu_b), (GBC, g_branch[0:CW]), (GBS, g_branch[CW:D]))

            def load_front(n):
                sp.dma_start(conv_in[:, :, :], tiles("conv")[n]).then_inc(conv_ld, 16)

            def load_ssm(n):
                sp.dma_start(y_in[:, :, :], tiles("y")[n]).then_inc(y_ld, 16)
                sp.dma_start(s_in[:, :, :], tiles("s")[n]).then_inc(s_ld, 16)

            load_front(0)
            load_ssm(0)
            for to, v in vectors:
                load_column(nc, sp, cols[:, to], v).then_inc(params, 16)
            sp.dma_start(gain[:, :], g_ffn.partition_broadcast(P)).then_inc(params, 16)
            sp.dma_start(wr[:, :, 0:NG], w_rg.rearrange("(c p) n -> p c n", p=P)).then_inc(params, 16)
            sp.dma_start(wr[:, :, NG:NL], w_re.rearrange("(c p) n -> p c n", p=P)).then_inc(params, 16)
            sp.dma_start(br[:, 0:NG], b_rg.partition_broadcast(P)).then_inc(params, 16)
            sp.dma_start(br[:, NG:NL], b_re.partition_broadcast(P)).then_inc(params, 16)
            for t in range(2):
                sp.dma_start(x_sb[:, t], x_rows[0][t]).then_inc(x_ld[t], 16)
            sp.wait_ge(zeroed, 1)
            sp.dma_start(scratch["h"][SEQ:ROWS, :], zero[:, :]).then_inc(pads, 16)
            sp.dma_start(scratch["acc"][SEQ:ROWS, :], zero[:, :]).then_inc(pads, 16)

            def body(n, par):
                if not last_step(n) and not (isinstance(n, int) and n == T8 - 1):
                    sp.wait_ge(ln_tr, n * 2 + 2)
                    load_front(n + 1)
                    sp.wait_ge(yg_done, n + 1)
                    load_ssm(n + 1)
                if not first(n):
                    for t in range(2):
                        q = n * 2 - 2 + t
                        sp.wait_ge(h_done, q + 1)
                        sp.dma_start(rows("acc")[n - 1][t], x2[:, t]).then_inc(x2_st[t], 16)
                        sp.dma_start(rows("h")[n - 1][t], h[:, t]).then_inc(h_st[t], 16)
                        if not last_step(n):
                            sp.dma_start(x_sb[:, t], x_rows[n][t]).then_inc(x_ld[t], 16)
            over_steps(sp, body)
            for t in range(2):
                sp.wait_ge(x2_st[t], 16 * T8)
                sp.wait_ge(h_st[t], 16 * T8)
            sp.wait_ge(pads, 32)

        @block.gpsimd
        def _(pool):
            nc.gpsimd.memset(ones[:, :], 1.0).then_inc(ones_done, 1)
            nc.gpsimd.memset(zero[:, :], 0.0).then_inc(zeroed, 1)
            with pool.Fori(0, T8) as n:
                pool.wait_ge(v_done, n + 1)
                nc.gpsimd.tensor_tensor(cube[:, :, :], y_in[:, :, :], y_in[:, :, :], ALU.mult).then_inc(cube_own, 1)
                pool.wait_ge(cube_own, n + 1)
                nc.gpsimd.tensor_tensor(cube[:, :, :], cube[:, :, :], y_in[:, :, :], ALU.mult).then_inc(cube_done, 1)
                step = Chain(pool, adds, n * 2)
                for branch, made in enumerate((c_hi_done, s_hi_done)):
                    pool.wait_ge(made, n + 1)
                    step(nc.gpsimd.tensor_tensor(sq[:, branch, 0:2], sq[:, branch, 0:2], sq[:, branch, 2:4], ALU.add))
                    nc.gpsimd.tensor_tensor(sq[:, branch, 0], sq[:, branch, 0], sq[:, branch, 1], ALU.add).then_inc(summed, 1)

        @block.scalar
        def _(act):
            act.wait_ge(pads, 32)
            act.wait_ge(params, 16 * PARAMS)

            def front1(n):
                act.wait_ge(gelu_arg, n + 1)
                nc.scalar.activation(sg[:, :, :], cube[:, :, :], ACT.Sigmoid, scale=GELU).then_inc(gelu_sig, 1)
                act.wait_ge(yg_done, n + 1)
                nc.scalar.copy(yg_hi[:, :, :], yg[:, :, :]).then_inc(yg_hi_done, 1)

            def front2(n, par):
                wait(act, c_lo_done, n)
                for b, bank in enumerate((pb, pc)):
                    act.wait_ge(ln_back, n * 2 + b + 1)
                    for c in (2 * b, 2 * b + 1):
                        nc.scalar.activation(yc[:, c], bank[:, (c % 2) * TN:(c % 2 + 1) * TN], ACT.Silu,
                                             scale=cols[:, LNG, c:c + 1], bias=cols[:, LNB, c:c + 1]).then_inc(yc_done, 1)

            def front3(n, par):
                act.wait_ge(yc_done, n * CT + CT)
                nc.scalar.activation(sq[:, 0], yc[:, :, :], ACT.Square)
                for c in range(CT):
                    last = nc.scalar.activation(cat_hi[:, par, c], yc[:, c], ACT.Copy, scale=cols[:, GBC, c:c + 1])
                last.then_inc(c_hi_done, 1)
                for b, bank in enumerate((pa, pb)):
                    act.wait_ge(glu_done, n * 2 + b + 1)
                    for m in (2 * b, 2 * b + 1):
                        last = nc.scalar.activation(sg[:, m], bank[:, (m % 2) * TN:(m % 2 + 1) * TN], ACT.Sigmoid,
                                                    bias=cols[:, GLB, m:m + 1])
                    last.then_inc(glu_sig, 1)
                act.wait_ge(ys_done, n + 1)
                nc.scalar.activation(sq[:, 1], ys[:, :, :], ACT.Square)
                for c in range(CT):
                    last = nc.scalar.activation(cat_hi[:, par, CT + c], ys[:, c], ACT.Copy, scale=cols[:, GBS, c:c + 1])
                last.then_inc(s_hi_done, 1)

            def tile_square(q, t):
                act.wait_ge(half_b, q * 2 + 2)
                nc.scalar.activation(junk[:, :], x2[:, t], ACT.Square, accum_out=st[:, 3, 3:4]).then_inc(x2_sq, 1)

            def logit(q, t):
                for b, bank in enumerate((pc, pa)):
                    act.wait_ge(h_turned, q * 2 + b + 1)
                    wait(act, logit_done, q)
                    nc.scalar.copy(hT[:, 4 * b:4 * b + 4, :].rearrange("p c k -> p (c k)"), bank[:, :]).then_inc(h_copied, 1)

            def body(n, par):
                if not last_step(n):
                    front1(n)
                if not first(n) and not (isinstance(n, int) and n == 1):
                    logit(n * 2 - 3, 1)
                if not last_step(n):
                    front2(n, par)
                if not first(n):
                    tile_square(n * 2 - 2, 0)
                if not last_step(n):
                    front3(n, par)
                if not first(n):
                    logit(n * 2 - 2, 0)
                    tile_square(n * 2 - 1, 1)
            over_steps(act, body)
            logit(2 * T8 - 1, 1)

        @block.vector
        def _(dve):
            V = nc.vector
            dve.wait_ge(params, 16 * PARAMS)

            F1 = 7 + RSQRT_STEPS
            FS = RSQRT_STEPS
            FO = 1 + RSQRT_STEPS

            def front1(n):
                step = Chain(dve, bn_own, n * F1)
                dve.wait_ge(y_ld, 16 * (n + 1))
                dve.wait_ge(s_ld, 16 * (n + 1))
                for c in range(CT):
                    last = V.scalar_tensor_tensor(out=y_in[:, c], in0=s_in[:, c], scalar=cols[:, DD, c:c + 1],
                                                  in1=y_in[:, c], op0=ALU.mult, op1=ALU.add)
                last.then_inc(v_done, 1)
                dve.wait_ge(ln_tr, n * 2 + 2)
                for t, bank in enumerate((pa, pb)):
                    V.bn_stats(bn[:, t], bank[:, :]).then_inc(own, 1)
                dve.wait_ge(own, n * 2 + 2)
                me, mo, ve, vo = (bn[:, :, i] for i in (1, 4, 2, 5))
                mean, dif, var = mv[:, :, 0], mv[:, :, 1], mv[:, :, 2]
                step(V.tensor_tensor(mean, me, mo, ALU.add))
                step(V.tensor_tensor(dif, me, mo, ALU.subtract))
                step(V.tensor_tensor(var, ve, vo, ALU.add))
                step(V.tensor_scalar(mean, mean, 0.5, None, ALU.mult))
                step(V.tensor_tensor(dif, dif, dif, ALU.mult))
                step(V.scalar_tensor_tensor(out=var, in0=dif, scalar=CW / 4.0, in1=var, op0=ALU.mult, op1=ALU.add))
                a = st[:, 0, 0:2]
                step(V.tensor_scalar(a, var, 1.0 / CW, EPS, ALU.mult, ALU.add))
                rsqrt(nc, step, st[:, 1, 0:2], a, st[:, 2, 0:2], st[:, 3, 0:2])
                for t, bank in enumerate((pa, pb)):
                    last = V.tensor_scalar(yn[:, t], bank[:, :], mv[:, t, 0:1], st[:, 1, t:t + 1], ALU.subtract, ALU.mult)
                last.then_inc(yn_done, 1)
                dve.wait_ge(cube_done, n + 1)
                V.scalar_tensor_tensor(out=cube[:, :, :], in0=cube[:, :, :], scalar=0.044715, in1=y_in[:, :, :],
                                       op0=ALU.mult, op1=ALU.add).then_inc(gelu_arg, 1)
                dve.wait_ge(gelu_sig, n + 1)
                V.tensor_tensor(yg[:, :, :], y_in[:, :, :], sg[:, :, :], ALU.mult).then_inc(yg_done, 1)
                dve.wait_ge(yg_hi_done, n + 1)
                V.tensor_tensor(yg_lo[:, :, :], yg[:, :, :], yg_hi[:, :, :].bitcast(FP32), ALU.subtract).then_inc(yg_lo_done, 1)

            def front2(n, par):
                dve.wait_ge(c_hi_done, n + 1)
                for c in range(CT):
                    last = V.scalar_tensor_tensor(out=cat_lo[:, par, c], in0=yc[:, c], scalar=cols[:, GBC, c:c + 1],
                                                  in1=cat_hi[:, par, c].bitcast(FP32), op0=ALU.mult, op1=ALU.subtract)
                last.then_inc(c_lo_done, 1)
                dve.wait_ge(glu_sig, n * 2 + 2)
                V.tensor_tensor(ys[:, :, :], yg[:, :, :], sg[:, :, :], ALU.mult).then_inc(ys_done, 1)
                dve.wait_ge(s_hi_done, n + 1)
                for c in range(CT):
                    last = V.scalar_tensor_tensor(out=cat_lo[:, par, CT + c], in0=ys[:, c], scalar=cols[:, GBS, c:c + 1],
                                                  in1=cat_hi[:, par, CT + c].bitcast(FP32), op0=ALU.mult, op1=ALU.subtract)
                last.then_inc(s_lo_done, 1)

            def sums(n):
                step = Chain(dve, sums_own, n * FS)
                dve.wait_ge(sums_done, n + 1)
                V.tensor_scalar(st[:, 0, :], pd[:, 0:4], 1.0 / CW, EPS, ALU.mult, ALU.add).then_inc(sums_read, 1)
                dve.wait_ge(sums_read, n + 1)
                rsqrt(nc, step, rs[:, :], st[:, 0, :], st[:, 1, :], st[:, 2, :])

            def out_tile(q, n, t):
                step = Chain(dve, x2_own, q * FO)
                dve.wait_ge(x_ld[t], 16 * (n + 1))
                wait(dve, x2_st[t], n * 16)
                wait(dve, h_st[t], n * 16)
                for half in range(2):
                    dve.wait_ge(out_done, q * 2 + half + 1)
                    sl = slice(half * 512, (half + 1) * 512)
                    V.scalar_tensor_tensor(out=x2[:, t, sl], in0=p_out[2 * half][:, :], scalar=rs[:, 2 * t:2 * t + 1],
                                           in1=x_sb[:, t, sl], op0=ALU.mult, op1=ALU.add).then_inc(half_a, 1)
                    dve.wait_ge(half_a, q * 2 + half + 1)
                    V.scalar_tensor_tensor(out=x2[:, t, sl], in0=p_out[2 * half + 1][:, :], scalar=rs[:, 2 * t + 1:2 * t + 2],
                                           in1=x2[:, t, sl], op0=ALU.mult, op1=ALU.add).then_inc(half_b, 1)
                dve.wait_ge(x2_sq, q + 1)
                step(V.tensor_scalar(st[:, 0, 0:1], st[:, 3, 3:4], 1.0 / D, EPS, ALU.mult, ALU.add))
                rsqrt(nc, step, st[:, 1, 0:1], st[:, 0, 0:1], st[:, 2, 0:1], st[:, 2, 1:2])
                V.scalar_tensor_tensor(out=h[:, t], in0=x2[:, t], scalar=st[:, 1, 0:1], in1=gain[:, :],
                                       op0=ALU.mult, op1=ALU.mult).then_inc(h_done, 1)

            def logit(q, t):
                dve.wait_ge(logit_done, q + 1)
                V.tensor_tensor(logits[:, bass.ds(q, 1), :].squeeze(1), pd[:, 64:64 + NL], br[:, :], ALU.add).then_inc(logit_read, 1)

            def body(n, par):
                if not last_step(n):
                    front1(n)
                if not first(n):
                    sums(n - 1)
                    out_tile(n * 2 - 2, n - 1, 0)
                    if not (isinstance(n, int) and n == 1):
                        logit(n * 2 - 3, 1)
                if not last_step(n):
                    front2(n, par)
                if not first(n):
                    out_tile(n * 2 - 1, n - 1, 1)
                    logit(n * 2 - 2, 0)
            over_steps(dve, body)
            logit(2 * T8 - 1, 1)

        @block.tensor
        def _(pe):
            def ln_in(n):
                pe.wait_ge(conv_ld, 16 * (n + 1))
                wait(pe, glu_sig, n * 2)
                if not (isinstance(n, int) and n < 2):
                    pe.wait_ge(h_copied, n * 4 - 6)
                for t, bank in enumerate((pa, pb)):
                    for c in range(CT):
                        last = nc.tensor.transpose(bank[:, c * P:(c + 1) * P], conv_in[:, c, t * P:(t + 1) * P], ident[:, :])
                    last.then_inc(ln_tr, 1)

            def ln_out(n):
                pe.wait_ge(yn_done, n + 1)
                wait(pe, yc_done, n * CT)
                for b, bank in enumerate((pb, pc)):
                    for c in (2 * b, 2 * b + 1):
                        for t in range(2):
                            at = (c % 2) * TN + t * P
                            last = nc.tensor.transpose(bank[:, at:at + P], yn[:, t, c * P:(c + 1) * P], ident[:, :])
                    last.then_inc(ln_back, 1)

            def glu(n):
                pe.wait_ge(yg_lo_done, n + 1)
                for b, bank in enumerate((pa, pb)):
                    if b == 1:
                        pe.wait_ge(yc_done, n * CT + 2)
                    for m in (2 * b, 2 * b + 1):
                        o = bank[:, (m % 2) * TN:(m % 2 + 1) * TN]
                        for c in range(CT):
                            ms = slice(m * P, (m + 1) * P)
                            nc.tensor.matmul(o, glu_hi[:, c, ms], yg_hi[:, c], start=c == 0, stop=False)
                            nc.tensor.matmul(o, glu_hi[:, c, ms], yg_lo[:, c], start=False, stop=False)
                            last = nc.tensor.matmul(o, glu_lo[:, c, ms], yg_hi[:, c], start=False, stop=c == CT - 1)
                    last.then_inc(glu_done, 1)

            def sums(n):
                pe.wait_ge(summed, n * 2 + 2)
                if not first(n):
                    pe.wait_ge(logit_read, n * 2 - 1)
                for t in range(2):
                    for branch in range(2):
                        last = nc.tensor.matmul(pd[:, 2 * t + branch:2 * t + branch + 1], sq[:, branch, 0, t * P:(t + 1) * P],
                                                ones[:, :], start=True, stop=True)
                last.then_inc(sums_done, 1)

            def out_tile(q, n, t, par):
                pe.wait_ge(c_lo_done, n + 1)
                pe.wait_ge(s_lo_done, n + 1)
                for half in range(2):
                    wait(pe, half_b, q * 2 - 1 + half if not (isinstance(q, int) and q == 0) else 0)
                    sl = slice(half * 512, (half + 1) * 512)
                    for branch in range(2):
                        o = p_out[2 * half + branch]
                        for c in range(CT):
                            k = branch * CT + c
                            ts = slice(t * P, (t + 1) * P)
                            nc.tensor.matmul(o[:, :], cat_hi[:, par, k, ts], wo_hi[:, k, sl], start=c == 0, stop=False)
                            nc.tensor.matmul(o[:, :], cat_lo[:, par, k, ts], wo_hi[:, k, sl], start=False, stop=False)
                            last = nc.tensor.matmul(o[:, :], cat_hi[:, par, k, ts], wo_lo[:, k, sl], start=False, stop=c == CT - 1)
                    last.then_inc(out_done, 1)

            def logit(q, t, sums_n):
                pe.wait_ge(h_done, q + 1)
                for b, bank in enumerate((pc, pa)):
                    for c in range(4 * b, 4 * b + 4):
                        last = nc.tensor.transpose(bank[:, (c % 4) * P:(c % 4 + 1) * P], h[:, t, c * P:(c + 1) * P], ident[:, :])
                    last.then_inc(h_turned, 1)
                pe.wait_ge(h_copied, q * 2 + 2)
                pe.wait_ge(sums_read, sums_n)
                wait(pe, logit_read, q)
                for c in range(KD):
                    last = nc.tensor.matmul(pd[:, 64:64 + NL], hT[:, c], wr[:, c], start=c == 0, stop=c == KD - 1)
                last.then_inc(logit_done, 1)

            pe.wait_ge(ones_done, 1)
            pe.wait_ge(params, 16 * PARAMS)

            def body(n, par):
                if not last_step(n):
                    ln_in(n)
                if not first(n):
                    sums(n - 1)
                    out_tile(n * 2 - 2, n - 1, 0, 1 - par)
                    if not (isinstance(n, int) and n == 1):
                        if not last_step(n):
                            pe.wait_ge(yn_done, n + 1)
                        logit(n * 2 - 3, 1, n)
                if not last_step(n):
                    ln_out(n)
                    glu(n)
                if not first(n):
                    out_tile(n * 2 - 1, n - 1, 1, 1 - par)
                    if not last_step(n):
                        pe.wait_ge(yc_done, n * CT + CT)
                        pe.wait_ge(glu_sig, n * 2 + 1)
                    logit(n * 2 - 2, 0, n)
            over_steps(pe, body)
            logit(2 * T8 - 1, 1, T8)


class ExpertWeights:
    HALVES = 2

    def __init__(self, nc, ctx, w_gate, w_up, w_down):
        sb, _, sem = alloc(nc, ctx, "expert")
        self.nc = nc
        self.raw = [sb(f"raw{u}", [P, 8, 512]) for u in range(3)]
        self.hi = [sb(f"hi{u}", [P, 8, 512], FP32R) for u in range(3)]
        self.lo = [sb(f"lo{u}", [P, 8, 512], FP32R) for u in range(3)]
        self.raw_in = [sem(f"raw_in{u}") for u in range(3)]
        self.hi_done = [sem(f"hi_done{u}") for u in range(3)]
        self.lo_done = [sem(f"lo_done{u}") for u in range(3)]
        self.views = [w_gate.rearrange("e (c p) f -> e p c f", p=P), w_up.rearrange("e (c p) f -> e p c f", p=P),
                      w_down.rearrange("e (c p) (h f) -> e p h c f", p=P, h=2)]

    def load(self, engine, e, u):
        for h in range(self.HALVES):
            piece = slice(4 * h, 4 * h + 4)
            source = self.views[u][e][:, piece] if u < 2 else self.views[u][e][:, h]
            engine.dma_start(self.raw[u][:, piece], source).then_inc(self.raw_in[u], 16)

    def split_hi(self, act, e, u):
        for h in range(self.HALVES):
            piece = slice(4 * h, 4 * h + 4)
            act.wait_ge(self.raw_in[u], e * 32 + 32)
            self.nc.scalar.copy(self.hi[u][:, piece], self.raw[u][:, piece]).then_inc(self.hi_done[u], 1)

    def split_lo(self, engine, tensor_tensor, e, u):
        for h in range(self.HALVES):
            piece = slice(4 * h, 4 * h + 4)
            engine.wait_ge(self.hi_done[u], e * self.HALVES + h + 1)
            tensor_tensor(self.lo[u][:, piece], self.raw[u][:, piece], self.hi[u][:, piece].bitcast(FP32),
                          ALU.subtract).then_inc(self.lo_done[u], 1)


def route(nc, scratch, ident, logits, counts, weights):
    MAXB = SEQ // P
    with ExitStack() as ctx:
        sb, ps, sem = alloc(nc, ctx, "route")
        before, ones = sb("before", [P, P]), sb("ones", [P, P])
        desc, thresh = sb("desc", [P, EPG]), sb("thresh", [P, MAXB])
        desc_i, thresh_i = sb("desc_i", [P, EPG], INT32), sb("thresh_i", [P, MAXB], INT32)
        blank = sb("blank", [P, TBLK, 2], INT32)
        pay, slot_i = sb("pay", [P, TT, 2, 2], INT32), sb("slot_i", [P, TT, 2], INT32)
        s1 = [sb(f"s1_{i}", [P, TT]) for i in range(12)]
        g4 = [sb(f"g4_{i}", [P, TT, NG]) for i in range(5)]
        e8 = [sb(f"e8_{i}", [P, TT, EPG]) for i in range(6)]
        pick = [sb(f"pick{k}", [P, TT, NE]) for k in range(2)]
        both, w1, w2, w3 = (sb(n, [P, TT, NE]) for n in ("both", "w1", "w2", "w3"))
        tot = sb("tot", [P, TT, NE])
        n32 = [sb(f"n32_{i}", [P, NE]) for i in range(4)]
        cmp = sb("cmp", [P, NE, MAXB])
        p_rank, p_tot = ps("p_rank"), ps("p_tot")
        cleared, built, blank_st, own = sem("cleared"), sem("built"), sem("blank_st"), sem("own")
        both_done, ranked, slots_done, scattered, iotas = (sem(n) for n in ("both_done", "ranked", "slots_done", "scattered", "iotas"))
        block = ctx.enter_context(nc.Block())

        @block.gpsimd
        def _(pool):
            G = nc.gpsimd
            G.memset(before[:, :], 1.0).then_inc(cleared, 1)
            G.memset(blank[:, :, :], 0).then_inc(cleared, 1)
            G.memset(ones[:, :], 1.0).then_inc(built, 1)
            pool.wait_ge(cleared, 2)
            G.affine_select(out=before[:, :], in_=before[:, :], compare_op=ALU.is_gt, fill=0.0, base=0,
                            pattern=[[1, P]], channel_multiplier=-1).then_inc(built, 1)
            G.iota(blank[:, :, 0:1], pattern=[[0, TBLK]], base=SEQ, channel_multiplier=1).then_inc(iotas, 1)
            G.iota(desc_i[:, :], pattern=[[-1, EPG]], base=EPG, channel_multiplier=0).then_inc(iotas, 1)
            G.iota(thresh_i[:, :], pattern=[[P, MAXB]], base=0, channel_multiplier=0).then_inc(iotas, 1)
            for k in range(2):
                G.iota(pay[:, :, k, 0:1], pattern=[[P, TT]], base=0, channel_multiplier=1).then_inc(iotas, 1)
            pool.wait_ge(iotas, 5)
            pool.dma_start(scratch["table"].rearrange("(b p) w -> p b w", p=P), blank[:, :, :]).then_inc(blank_st, 16)
            for u in range(3):
                weights.split_lo(pool, G.tensor_tensor, 0, u)
            pool.wait_ge(blank_st, 16)
            pool.wait_ge(slots_done, 1)
            for i in range(TT):
                for k in range(2):
                    G.indirect_dma_start(
                        out=scratch["table"][:, :],
                        out_offset=bass.IndirectOffsetOnAxis(ap=slot_i[:, i, k:k + 1], axis=0),
                        in_=pay[:, i, k, :], in_offset=None).then_inc(scattered, 16)
            pool.wait_ge(scattered, 16 * 2 * TT)

        @block.sync
        def _(sp):
            for u in range(3):
                weights.load(sp, 0, u)
            for u in range(3):
                sp.wait_ge(weights.lo_done[u], weights.HALVES)
                weights.load(sp, 1, u)

        @block.scalar
        def _(act):
            for u in range(3):
                weights.split_hi(act, 0, u)

        @block.tensor
        def _(pe):
            pe.wait_ge(built, 2)
            pe.wait_ge(both_done, 1)
            m = both[:, :, :].rearrange("p i e -> p (i e)")
            nc.tensor.matmul(p_rank[:, :], before[:, :], m, start=True, stop=True)
            nc.tensor.matmul(p_tot[:, :], ones[:, :], m, start=True, stop=True).then_inc(ranked, 1)

        @block.vector
        def _(dve):
            V = nc.vector
            step = Chain(dve, own)

            def t2(o, a, b, op):
                step(V.tensor_tensor(o, a, b, op))

            def largest(values, w, key, one, m, km):
                step(V.reduce_max(m, values, AX.X))
                t2(key, values, m.unsqueeze(2).broadcast_to([P, TT, w]), ALU.is_equal)
                t2(key, key, desc[:, 0:w].unsqueeze(1).broadcast_to([P, TT, w]), ALU.mult)
                step(V.reduce_max(km, key, AX.X))
                t2(one, key, km.unsqueeze(2).broadcast_to([P, TT, w]), ALU.is_equal)

            dve.wait_ge(iotas, 5)
            step(V.tensor_copy(desc[:, :], desc_i[:, :]))
            step(V.tensor_copy(thresh[:, :], thresh_i[:, :]))
            gl, el = logits[:, :, 0:NG], logits[:, :, NG:NG + NE]
            gmax, km, psum_, pgrp, m1, m2, ex, den, gate1, gate2 = (t[:, :] for t in s1[:10])
            key_g, one_g, dg, tg, ng = (t[:, :, :] for t in g4)
            key_e, one1, one2, e_in, e2, te = (t[:, :, :] for t in e8)
            largest(gl, NG, key_g, one_g, gmax, km)
            t2(dg, gl, gmax.unsqueeze(2).broadcast_to([P, TT, NG]), ALU.subtract)
            flat = lambda ap: ap.rearrange("p i g -> p (i g)")
            exp_precise(nc, step, flat(dg), flat(dg), flat(tg), flat(ng), flat(key_g))
            step(V.reduce_sum(psum_, dg, AX.X))
            step(V.reciprocal(pgrp, psum_))
            w4 = w1[:, :, :].rearrange("p i (g e) -> p i g e", g=NG)
            t2(w4, el.rearrange("p i (g e) -> p i g e", g=NG), one_g.unsqueeze(3).broadcast_to([P, TT, NG, EPG]), ALU.mult)
            step(V.reduce_sum(e_in, w1[:, :, :].rearrange("p i (g e) -> p i e g", g=NG), AX.X))
            largest(e_in, EPG, key_e, one1, m1, km)
            step(V.tensor_scalar(te, one1, -6e38 / 2, 3e38 / 2, ALU.mult, ALU.add))
            step(V.tensor_scalar(te, te, 2.0, None, ALU.mult))
            t2(e2, e_in, te, ALU.min)
            largest(e2, EPG, key_e, one2, m2, km)
            t2(ex, m2, m1, ALU.subtract)
            exp_precise(nc, step, ex, ex, s1[10][:, :], s1[11][:, :], km)
            step(V.tensor_scalar(den, ex, 1.0, None, ALU.add))
            step(V.reciprocal(den, den))
            t2(gate1, den, pgrp, ALU.mult)
            t2(gate2, gate1, ex, ALU.mult)
            for k, gate in enumerate((gate1, gate2)):
                step(V.tensor_copy(pay[:, :, k, 1:2].bitcast(FP32).squeeze(2), gate))
            for k, one in enumerate((one1, one2)):
                t2(pick[k][:, :, :].rearrange("p i (g e) -> p i g e", g=NG),
                   one_g.unsqueeze(3).broadcast_to([P, TT, NG, EPG]),
                   one.unsqueeze(2).broadcast_to([P, TT, NG, EPG]), ALU.mult)
            step(V.tensor_tensor(both[:, :, :], pick[0][:, :, :], pick[1][:, :, :], ALU.add))
            dve.sem_inc(both_done, 1)
            dve.wait_ge(ranked, 1)
            step(V.tensor_copy(tot[:, :, :].rearrange("p i e -> p (i e)"), p_tot[:, :]))
            a, b = tot[:, :, :], w1[:, :, :]
            spare = w2[:, :, :]
            d = 1
            while d < TT:
                step(V.tensor_copy(b[:, 0:d], a[:, 0:d]))
                t2(b[:, d:], a[:, d:], a[:, 0:TT - d], ALU.add)
                a, b, spare = b, (spare if d == 1 else a), spare
                d *= 2
            upto = a
            t2(w3[:, :, :], upto, tot[:, :, :], ALU.subtract)
            n, c1, c2, n2 = (t[:, :] for t in n32)
            t2(cmp[:, :, :], upto[:, TT - 1, :].unsqueeze(2).broadcast_to([P, NE, MAXB]),
               thresh[:, :].unsqueeze(1).broadcast_to([P, NE, MAXB]), ALU.is_gt)
            step(V.reduce_sum(n, cmp[:, :, :], AX.X))
            step(V.tensor_scalar(n, n, 1.0, None, ALU.max))
            step(V.tensor_copy(c1, n))
            d = 1
            while d < NE:
                step(V.tensor_copy(c2[:, 0:d], c1[:, 0:d]))
                t2(c2[:, d:], c1[:, d:], c1[:, 0:NE - d], ALU.add)
                c1, c2 = c2, c1
                d *= 2
            t2(c2, c1, n, ALU.subtract)
            step(V.tensor_copy(counts[:, 0, :], n))
            step(V.tensor_copy(counts[:, 1, :], c2))
            step(V.tensor_copy(n2, n))
            step(V.tensor_scalar(n2[:, NE - 1:NE], n[:, NE - 1:NE], float(2 * NBLK), None, ALU.add))
            step(V.tensor_copy(counts[:, 2, :], n2))
            t2(w3[:, :, :], w3[:, :, :], p_rank[:, :].rearrange("p (i e) -> p i e", i=TT), ALU.add)
            step(V.tensor_scalar(c2, c2, float(P), None, ALU.mult))
            t2(w3[:, :, :], w3[:, :, :], c2.unsqueeze(1).broadcast_to([P, TT, NE]), ALU.add)
            for k in range(2):
                t2(pick[k][:, :, :], pick[k][:, :, :], w3[:, :, :], ALU.mult)
                step(V.reduce_sum(m1, pick[k][:, :, :], AX.X))
                step(V.tensor_copy(slot_i[:, :, k:k + 1].squeeze(2), m1))
            dve.sem_inc(slots_done, 1)


def experts(nc, scratch, ident, counts, weights):
    HALVES = weights.HALVES
    hi, lo, w_lo = weights.hi, weights.lo, weights.lo_done
    with ExitStack() as ctx:
        sb, ps, sem = alloc(nc, ctx, "moe")
        ids_g, ids_s = sb("ids_g", [P, 2], INT32), sb("ids_s", [P, 2], INT32)
        xg = sb("xg", [P, D])
        xh, xl = sb("xh", [P, KD, P], FP32R), sb("xl", [P, KD, P], FP32R)
        sil, hid = sb("sil", [P, F]), sb("hid", [P, F])
        hh, hl = sb("hh", [P, F // P, P], FP32R), sb("hl", [P, F // P, P], FP32R)
        y = sb("y", [P, D])
        p_gate, p_up, p_hid = ps("p_gate"), ps("p_up"), ps("p_hid")
        p_x = [ps("p_x0"), ps("p_x1")]
        p_y = [ps("p_y0"), ps("p_y1")]

        ids_g_in, ids_s_in, x_in, scattered = sem("ids_g_in"), sem("ids_s_in"), sem("x_in"), sem("scattered")
        gathers, scatters = sem("gathers"), sem("scatters")
        x_turned, x_hi, x_lo = sem("x_turned"), sem("x_hi"), sem("x_lo")
        gate_done, up_done, sil_done, hid_done = (sem(n) for n in ("gate_done", "up_done", "sil_done", "hid_done"))
        hid_turned, hid_hi, hid_lo, down_done, y_done = (sem(n) for n in ("hid_turned", "hid_hi", "hid_lo", "down_done", "y_done"))
        block = ctx.enter_context(nc.Block())

        def over_blocks(engine, body, before=None, flags=False):
            with engine.Fori(0, NE) as e:
                n = engine.value_load(counts[0:1, 0, bass.ds(e, 1)], min_val=1, max_val=SEQ // P)
                start = engine.value_load(counts[0:1, 1, bass.ds(e, 1)], min_val=0, max_val=NBLK)
                last = engine.value_load(counts[0:1, 2, bass.ds(e, 1)], min_val=1, max_val=3 * NBLK) if flags else None
                with engine.Fori(0, n) as j:
                    body(start + j, e, j, last)

        @block.sync
        def _(sp):
            with sp.Fori(1, NE - 1) as e:
                for u in range(3):
                    sp.wait_ge(w_lo[u], (e + 1) * HALVES)
                    weights.load(sp, e + 1, u)

        @block.gpsimd
        def _(pool):
            table = scratch["table"].rearrange("(b p) w -> b p w", p=P)

            def load_ids(b):
                pool.dma_start(ids_g[:, :], table[b]).then_inc(ids_g_in, 16)

            def gather(b):
                pool.wait_ge(ids_g_in, b * 16 + 16)
                pool.sem_inc(gathers, 1)
                nc.gpsimd.indirect_dma_start(out=xg[:, :], out_offset=None, in_=scratch["h"][:, :],
                                             in_offset=bass.IndirectOffsetOnAxis(ap=ids_g[:, 0:1], axis=0)).then_inc(x_in, 16)

            load_ids(0)
            gather(0)
            pool.wait_ge(x_in, 16)
            load_ids(1)
            pool.wait_ge(x_turned, 2)
            gather(1)
            pool.dma_start(ids_s[:, :], table[0]).then_inc(scattered, 16)

            def body(b, e, j, last):
                pool.wait_ge(x_in, b * 16 + 32)
                pool.sem_inc(gathers, 1)
                load_ids(b + 2)
                pool.wait_ge(scattered, b * 16 + 16)
                pool.sem_inc(scatters, 1)
                pool.dma_start(ids_s[:, :], table[b]).then_inc(ids_s_in, 16)
                pool.wait_ge(x_turned, b * 2 + 4)
                gather(b + 2)
                pool.wait_ge(ids_s_in, b * 16 + 16)
                pool.wait_ge(y_done, b * 2 + 2)
                pool.sem_inc(scatters, 1)
                nc.gpsimd.indirect_dma_start(out=scratch["acc"][:, :],
                                             out_offset=bass.IndirectOffsetOnAxis(ap=ids_s[:, 0:1], axis=0),
                                             in_=y[:, :], in_offset=None, compute_op=ALU.add).then_inc(scattered, 16)
            over_blocks(pool, body)
            blocks = pool.value_load(counts[0:1, 1, NE - 1:NE], min_val=0, max_val=NBLK)
            blocks = blocks + pool.value_load(counts[0:1, 0, NE - 1:NE], min_val=1, max_val=SEQ // P)
            pool.wait_ge(scattered, blocks * 16 + 16)
            pool.wait_ge(x_in, blocks * 16 + 32)

        @block.scalar
        def _(act):
            def turn_x(b):
                for i in range(2):
                    act.wait_ge(x_turned, b * 2 + i + 1)
                    nc.scalar.copy(xh[:, 4 * i:4 * i + 4, :].rearrange("p c t -> p (c t)"), p_x[i][:, :]).then_inc(x_hi, 1)

            turn_x(0)

            def body(b, e, j, last):
                act.wait_ge(gate_done, b + 1)
                nc.scalar.activation(sil[:, :], p_gate[:, :], ACT.Silu).then_inc(sil_done, 1)
                with act.If(j == last - 1):
                    weights.split_hi(act, e + 1, 0)
                with act.Else():
                    pass
                act.wait_ge(hid_turned, b + 1)
                nc.scalar.copy(hh[:, :, :].rearrange("p c t -> p (c t)"), p_hid[:, :]).then_inc(hid_hi, 1)
                turn_x(b + 1)
                with act.If(j == last - 1):
                    weights.split_hi(act, e + 1, 1)
                with act.Else():
                    pass
                act.wait_ge(ids_s_in, b * 16 + 16)
                for i in range(2):
                    act.wait_ge(down_done, b * 2 + i + 1)
                    nc.scalar.activation(y[:, i * 512:(i + 1) * 512], p_y[i][:, :], ACT.Copy,
                                         scale=ids_s[:, 1:2].bitcast(FP32)).then_inc(y_done, 1)
                with act.If(j == last - 1):
                    weights.split_hi(act, e + 1, 2)
                with act.Else():
                    pass
            over_blocks(act, body, flags=True)

        @block.vector
        def _(dve):
            V = nc.vector

            def turn_x(b):
                for i in range(2):
                    dve.wait_ge(x_hi, b * 2 + i + 1)
                    V.tensor_tensor(xl[:, 4 * i:4 * i + 4, :].rearrange("p c t -> p (c t)"), p_x[i][:, :],
                                    xh[:, 4 * i:4 * i + 4, :].rearrange("p c t -> p (c t)").bitcast(FP32), ALU.subtract).then_inc(x_lo, 1)

            turn_x(0)

            def body(b, e, j, last):
                dve.wait_ge(sil_done, b + 1)
                dve.wait_ge(up_done, b + 1)
                V.tensor_tensor(hid[:, :], p_up[:, :], sil[:, :], ALU.mult).then_inc(hid_done, 1)
                dve.wait_ge(hid_hi, b + 1)
                V.tensor_tensor(hl[:, :, :].rearrange("p c t -> p (c t)"), p_hid[:, :],
                                hh[:, :, :].rearrange("p c t -> p (c t)").bitcast(FP32), ALU.subtract).then_inc(hid_lo, 1)
                turn_x(b + 1)
                with dve.If(j == last - 1):
                    for u in range(3):
                        weights.split_lo(dve, V.tensor_tensor, e + 1, u)
                with dve.Else():
                    pass
            over_blocks(dve, body, flags=True)

        @block.tensor
        def _(pe):
            def turn_x(b, halves):
                pe.wait_ge(x_in, b * 16 + 16)
                for i in halves:
                    for c in range(4):
                        last = nc.tensor.transpose(p_x[i][:, c * P:(c + 1) * P], xg[:, (4 * i + c) * P:(4 * i + c + 1) * P], ident[:, :])
                    last.then_inc(x_turned, 1)

            def product(out, e, u, a_hi, a_lo, chunk, kc, last):
                nc.tensor.matmul(out[:, :], a_hi, hi[u][:, chunk], start=kc == 0, stop=False)
                nc.tensor.matmul(out[:, :], a_lo, hi[u][:, chunk], start=False, stop=False)
                return nc.tensor.matmul(out[:, :], a_hi, lo[u][:, chunk], start=False, stop=last)

            turn_x(0, (0, 1))

            def body(b, e, j, last):
                pe.wait_ge(x_lo, b * 2 + 2)
                for u, bank, done in ((0, p_gate, gate_done), (1, p_up, up_done)):
                    if u == 0:
                        wait(pe, hid_done, b)
                    for c in range(KD):
                        if c % 4 == 0:
                            pe.wait_ge(w_lo[u], e * HALVES + c // 4 + 1)
                        last_mm = product(bank, e, u, xh[:, c], xl[:, c], c, c, c == KD - 1)
                    last_mm.then_inc(done, 1)
                turn_x(b + 1, (0,))
                pe.wait_ge(hid_done, b + 1)
                for c in range(F // P):
                    last_mm = nc.tensor.transpose(p_hid[:, c * P:(c + 1) * P], hid[:, c * P:(c + 1) * P], ident[:, :])
                last_mm.then_inc(hid_turned, 1)
                turn_x(b + 1, (1,))
                pe.wait_ge(hid_lo, b + 1)
                wait(pe, y_done, b * 2)
                for i in range(2):
                    pe.wait_ge(w_lo[2], e * HALVES + i + 1)
                    for c in range(F // P):
                        last_mm = product(p_y[i], e, 2, hh[:, c], hl[:, c], 4 * i + c, c, c == F // P - 1)
                    last_mm.then_inc(down_done, 1)
            over_blocks(pe, body)


def final_norm(nc, scratch, g_final, out):
    with ExitStack() as ctx:
        sb, _, sem = alloc(nc, ctx, "final")
        NB = 4
        x, o = sb("x", [P, NB, D]), sb("o", [P, NB, D])
        gain, junk, st, scale = sb("gain", [P, D]), sb("junk", [P, D]), sb("st", [P, 4, NB]), sb("scale", [P, NB])
        gain_in, squared, own, made, scales_read = (sem(n) for n in ("gain_in", "squared", "own", "made", "scales_read"))
        x_in, stored = [sem(f"x_in{i}") for i in range(NB)], [sem(f"stored{i}") for i in range(NB)]
        block = ctx.enter_context(nc.Block())
        rows = scratch["acc"][0:SEQ, :].rearrange("(n i p) d -> i n p d", i=NB, p=P)
        outs = out.rearrange("(h k s) d -> s h k d", s=T8, h=2)
        NI = TT // NB

        @block.sync
        def _(sp):
            for i in range(NB):
                sp.dma_start(x[:, i], rows[i][0]).then_inc(x_in[i], 16)
            sp.dma_start(gain[:, :], g_final.partition_broadcast(P)).then_inc(gain_in, 16)
            with sp.Fori(0, NI - 1) as n:
                for i in range(NB):
                    sp.wait_ge(made, n * NB + i + 1)
                    sp.dma_start(outs[n * 2 + i // 2][i % 2], o[:, i]).then_inc(stored[i], 16)
                    sp.dma_start(x[:, i], rows[i][n + 1]).then_inc(x_in[i], 16)
            for i in range(NB):
                sp.wait_ge(made, (NI - 1) * NB + i + 1)
                sp.dma_start(outs[(NI - 1) * 2 + i // 2][i % 2], o[:, i]).then_inc(stored[i], 16)
            for i in range(NB):
                sp.wait_ge(stored[i], 16 * NI)

        @block.scalar
        def _(act):
            with act.Fori(0, NI) as n:
                for i in range(NB):
                    act.wait_ge(x_in[i], n * 16 + 16)
                    if i == 0:
                        act.wait_ge(scales_read, n + 1)
                    nc.scalar.activation(junk[:, :], x[:, i], ACT.Square, accum_out=st[:, 0, i:i + 1]).then_inc(squared, 1)
                    act.wait_ge(squared, n * NB + (i + 1))

        @block.vector
        def _(dve):
            dve.wait_ge(gain_in, 16)
            dve.sem_inc(scales_read, 1)
            with dve.Fori(0, NI) as n:
                step = Chain(dve, own, n * (1 + RSQRT_STEPS))
                dve.wait_ge(squared, n * NB + NB)
                step(nc.vector.tensor_scalar(st[:, 1], st[:, 0], 1.0 / D, EPS, ALU.mult, ALU.add))
                dve.sem_inc(scales_read, 1)
                rsqrt(nc, step, scale[:, :], st[:, 1], st[:, 2], st[:, 3])
                for i in range(NB):
                    wait(dve, stored[i], n * 16)
                    nc.vector.scalar_tensor_tensor(out=o[:, i], in0=x[:, i], scalar=scale[:, i:i + 1], in1=gain[:, :],
                                                   op0=ALU.mult, op1=ALU.mult).then_inc(made, 1)


_INS = ["x", "g_mix", "w_in", "conv_w", "conv_b", "conv_ln_g", "conv_ln_b", "ssm_lam_re", "ssm_lam_im",
        "ssm_log_dt", "ssm_b_re", "ssm_b_im", "ssm_c_re", "ssm_c_im", "ssm_d", "ssm_glu_w", "ssm_glu_b",
        "g_branch", "w_out", "g_ffn", "w_router_group", "b_router_group", "w_router_expert",
        "b_router_expert", "w_gate", "w_up", "w_down", "g_final"]


def kernel(**inputs):
    import numpy as _np
    import concourse.bacc as _bacc
    from concourse import mybir as _mybir
    from concourse.bass_utils import run_bass_kernel_spmd as _run

    nc = _bacc.Bacc("TRN2", target_bir_lowering=False, num_devices=1)
    arrays, args = {}, []
    for name in _INS:
        a = _np.ascontiguousarray(inputs[name])
        arrays[f"in_{name}"] = a
        ap = nc.dram_tensor(f"in_{name}", a.shape, _mybir.dt.from_np(a.dtype), kind="ExternalInput").ap()
        args.append(ap if name == "g_final" else ap[0])
    out = nc.dram_tensor("out", (1, SEQ, D), FP32, kind="ExternalOutput").ap()
    hybrid_encoder(nc, *args, out[0])
    r = _run(nc, [arrays], core_ids=[0])
    return r.results[0]["out"]
```
